# Optimizing a Trainium2 kernel written in Bass

```python
import math
import numpy as np
import jax
import jax.numpy as jnp
from jax import lax
import jax, jax.numpy as jnp

D_MODEL = 1024
BATCH = 1
SEQ = 256
DEPTH = 2

HEAD_DIM = 64
N_MIXERS = 4
GROUP_WIDTH = D_MODEL // N_MIXERS
N_HEADS = GROUP_WIDTH // HEAD_DIM
ROPE_THETA = 10000.0
EPS = 1e-6
Q_BLOCK = 128
NEG_INF = -1e30

NSA_CMP_LEN = 32
NSA_CMP_STRIDE = 16
NSA_SLC_LEN = 64
NSA_TOP_N = 16
NSA_WINDOW = 512
NSA_FORCED_LOCAL = 2

DIFF_HALF = HEAD_DIM // 2

MLSTM_CHUNK = 64
MLSTM_CONV = 4

DILATED_PATTERNS = ((128, 1), (512, 4), (2048, 16))
DILATED_PAD = 2048

D_FF = ((8 * D_MODEL + 3 * 256 - 1) // (3 * 256)) * 256

IN_SPLITS = (
    GROUP_WIDTH,
    HEAD_DIM, HEAD_DIM,
    HEAD_DIM, HEAD_DIM,
    HEAD_DIM, HEAD_DIM,
    3 * N_HEADS,
    GROUP_WIDTH, GROUP_WIDTH, GROUP_WIDTH,
    GROUP_WIDTH, GROUP_WIDTH,
    N_HEADS, N_HEADS, GROUP_WIDTH,
    GROUP_WIDTH, GROUP_WIDTH, GROUP_WIDTH,
)
D_IN = sum(IN_SPLITS)


def rmsnorm(x, g):
    xf = x.astype(jnp.float32)
    y = xf * lax.rsqrt(jnp.mean(xf * xf, axis=-1, keepdims=True) + EPS)
    return (y * g.astype(jnp.float32)).astype(x.dtype)

def rope_tables(seq, dim):
    inv = 1.0 / (ROPE_THETA ** (jnp.arange(0, dim, 2, dtype=jnp.float32) / dim))
    ang = jnp.arange(seq, dtype=jnp.float32)[:, None] * inv[None, :]
    return jnp.cos(ang), jnp.sin(ang)

def apply_rope(x, cos, sin):
    shape = (cos.shape[0],) + (1,) * (x.ndim - 3) + (cos.shape[1],)
    c, s = cos.reshape(shape), sin.reshape(shape)
    xf = x.astype(jnp.float32)
    half = x.shape[-1] // 2
    x1, x2 = xf[..., :half], xf[..., half:]
    return jnp.concatenate([x1 * c - x2 * s, x1 * s + x2 * c], axis=-1).astype(x.dtype)

def masked_softmax(s, mask, return_lse=False):
    s = jnp.where(mask, s.astype(jnp.float32), NEG_INF)
    m = jnp.max(s, axis=-1, keepdims=True)
    e = jnp.where(mask, jnp.exp(s - m), 0.0)
    z = jnp.sum(e, axis=-1, keepdims=True)
    z_safe = jnp.where(z > 0, z, 1.0)
    p = e / z_safe
    if return_lse:
        return p, (m + jnp.log(z_safe))[..., 0]
    return p

def sweep_query_blocks(fn, seq):
    out = lax.map(fn, jnp.arange(seq // Q_BLOCK) * Q_BLOCK)
    out = jnp.moveaxis(out, 0, 1)
    return out.reshape((out.shape[0], seq) + out.shape[3:])

def nsa_mixer(q, k_cmp, v_cmp, k_slc, v_slc, k_win, v_win, gate_pre, cmp_pos, cmp_w, cos, sin):
    bsz, seq = q.shape[0], q.shape[1]
    scale = HEAD_DIM ** -0.5
    t_pos = jnp.arange(seq)

    n_cmp = (seq - NSA_CMP_LEN) // NSA_CMP_STRIDE + 1
    blk_idx = np.arange(n_cmp)[:, None] * NSA_CMP_STRIDE + np.arange(NSA_CMP_LEN)[None, :]

    def compress(t, pos_emb, w):
        blocks = t[:, blk_idx] + pos_emb
        return blocks.reshape(bsz, n_cmp, NSA_CMP_LEN * HEAD_DIM) @ w

    kc = compress(k_cmp, cmp_pos[0], cmp_w[0])
    vc = compress(v_cmp, cmp_pos[1], cmp_w[1])
    cmp_end = jnp.arange(n_cmp) * NSA_CMP_STRIDE + NSA_CMP_LEN - 1
    cmp_mask = cmp_end[None, :] <= t_pos[:, None]
    p_cmp = masked_softmax(jnp.einsum('bshd,bnd->bhsn', q, kc) * scale, cmp_mask)
    o_cmp = jnp.einsum('bhsn,bnd->bshd', p_cmp.astype(vc.dtype), vc)

    n_slc = seq // NSA_SLC_LEN
    top_n = min(NSA_TOP_N, n_slc)
    ratio_s, ratio_c = NSA_SLC_LEN // NSA_CMP_STRIDE, NSA_CMP_LEN // NSA_CMP_STRIDE
    jj = np.arange(n_slc)[:, None, None]
    src = ratio_s * jj - np.arange(ratio_s)[None, :, None] - np.arange(ratio_c)[None, None, :]
    ok = (src >= 0) & (src < n_cmp)
    cmp_to_slc = np.zeros((n_cmp, n_slc), np.float32)
    np.add.at(cmp_to_slc, (np.where(ok, src, 0), np.broadcast_to(jj, src.shape)), ok.astype(np.float32))
    importance = jnp.einsum('bhsn,nj->bsj', p_cmp, jnp.asarray(cmp_to_slc))
    blk = jnp.arange(n_slc)[None, :]
    cur = (t_pos // NSA_SLC_LEN)[:, None]
    forced = (blk == 0) | ((blk <= cur) & (blk > cur - NSA_FORCED_LOCAL))
    score = jnp.where(blk > cur, -1.0e6, jnp.where(forced, 1.0e6, importance))
    _, sel_idx = lax.top_k(score, top_n)
    sel_valid = sel_idx <= cur[None]

    q_rot = apply_rope(q, cos, sin)
    ks = apply_rope(k_slc, cos, sin).reshape(bsz, n_slc, NSA_SLC_LEN, HEAD_DIM)
    vs = v_slc.reshape(bsz, n_slc, NSA_SLC_LEN, HEAD_DIM)
    pad = ((0, 0), (NSA_WINDOW, 0), (0, 0))
    kw = jnp.pad(apply_rope(k_win, cos, sin), pad)
    vw = jnp.pad(v_win, pad)
    b_idx = jnp.arange(bsz)[:, None, None]
    n_sel_keys = top_n * NSA_SLC_LEN

    def block(s0):
        qb = lax.dynamic_slice_in_dim(q_rot, s0, Q_BLOCK, axis=1)
        tq = s0 + jnp.arange(Q_BLOCK)
        idx = lax.dynamic_slice_in_dim(sel_idx, s0, Q_BLOCK, axis=1)
        valid = lax.dynamic_slice_in_dim(sel_valid, s0, Q_BLOCK, axis=1)
        kg = ks[b_idx, idx].reshape(bsz, Q_BLOCK, n_sel_keys, HEAD_DIM)
        vg = vs[b_idx, idx].reshape(bsz, Q_BLOCK, n_sel_keys, HEAD_DIM)
        kpos = (idx[..., None] * NSA_SLC_LEN + jnp.arange(NSA_SLC_LEN)).reshape(bsz, Q_BLOCK, n_sel_keys)
        kvalid = jnp.repeat(valid, NSA_SLC_LEN, axis=-1) & (kpos <= tq[None, :, None])
        p = masked_softmax(jnp.einsum('bqhd,bqkd->bhqk', qb, kg) * scale, kvalid[:, None])
        o_slc = jnp.einsum('bhqk,bqkd->bqhd', p.astype(vg.dtype), vg)
        kwb = lax.dynamic_slice_in_dim(kw, s0, NSA_WINDOW + Q_BLOCK, axis=1)
        vwb = lax.dynamic_slice_in_dim(vw, s0, NSA_WINDOW + Q_BLOCK, axis=1)
        wpos = s0 - NSA_WINDOW + jnp.arange(NSA_WINDOW + Q_BLOCK)
        wmask = (wpos[None, :] <= tq[:, None]) & (wpos[None, :] > tq[:, None] - NSA_WINDOW) & (wpos[None, :] >= 0)
        p = masked_softmax(jnp.einsum('bqhd,bkd->bhqk', qb, kwb) * scale, wmask)
        o_win = jnp.einsum('bhqk,bkd->bqhd', p.astype(vwb.dtype), vwb)
        return jnp.stack([o_slc, o_win], axis=2)

    o_sw = sweep_query_blocks(block, seq)
    g = jax.nn.sigmoid(gate_pre.astype(jnp.float32)).reshape(bsz, seq, 3, N_HEADS, 1).astype(q.dtype)
    o = g[:, :, 0] * o_cmp + g[:, :, 1] * o_sw[:, :, 0] + g[:, :, 2] * o_sw[:, :, 1]
    return o.reshape(bsz, seq, GROUP_WIDTH)

def diff_mixer(q, k, v, lam_vecs, sub_g, lam_init, cos, sin):
    bsz, seq = q.shape[0], q.shape[1]
    q = apply_rope(q, cos, sin)
    k = apply_rope(k, cos, sin)
    lv = lam_vecs.astype(jnp.float32)
    lam = jnp.exp(jnp.sum(lv[0] * lv[1])) - jnp.exp(jnp.sum(lv[2] * lv[3])) + lam_init
    scale = DIFF_HALF ** -0.5
    kpos = jnp.arange(seq)

    def block(s0):
        qb = lax.dynamic_slice_in_dim(q, s0, Q_BLOCK, axis=1)
        tq = s0 + jnp.arange(Q_BLOCK)
        s = jnp.einsum('bqhcd,bkhcd->bhcqk', qb, k) * scale
        p = masked_softmax(s, kpos[None, :] <= tq[:, None])
        a = p[:, :, 0] - lam * p[:, :, 1]
        return jnp.einsum('bhqk,bkhd->bqhd', a.astype(v.dtype), v)

    o = sweep_query_blocks(block, seq)
    o = rmsnorm(o, sub_g) * (1.0 - lam_init)
    return o.reshape(bsz, seq, GROUP_WIDTH)

def mlstm_mixer(u, v, i_pre, f_pre, o_pre, conv_w, conv_b, wq, wk, gate_b, head_g):
    bsz, seq = u.shape[0], u.shape[1]
    f32 = jnp.float32
    uc = lax.conv_general_dilated(u, conv_w[:, None, :], window_strides=(1,),
                                  padding=[(MLSTM_CONV - 1, 0)],
                                  dimension_numbers=('NWC', 'WIO', 'NWC'),
                                  feature_group_count=GROUP_WIDTH) + conv_b
    uc = jax.nn.silu(uc).reshape(bsz, seq, N_HEADS, HEAD_DIM)
    q = jnp.einsum('bshd,hde->bhse', uc, wq).astype(f32)
    k = jnp.einsum('bshd,hde->bhse', uc, wk).astype(f32) * (HEAD_DIM ** -0.5)
    vv = v.reshape(bsz, seq, N_HEADS, HEAD_DIM).transpose(0, 2, 1, 3).astype(f32)
    gb = gate_b.astype(f32)
    ig = (i_pre.astype(f32) + gb[0]).transpose(0, 2, 1)
    lf = jax.nn.log_sigmoid(f_pre.astype(f32) + gb[1]).transpose(0, 2, 1)

    nc, L = seq // MLSTM_CHUNK, MLSTM_CHUNK
    q = q.reshape(bsz, N_HEADS, nc, L, HEAD_DIM)
    k = k.reshape(bsz, N_HEADS, nc, L, HEAD_DIM)
    vv = vv.reshape(bsz, N_HEADS, nc, L, HEAD_DIM)
    ig = ig.reshape(bsz, N_HEADS, nc, L)
    b = jnp.cumsum(lf.reshape(bsz, N_HEADS, nc, L), axis=-1)
    causal = jnp.tril(jnp.ones((L, L), dtype=bool))
    dmat = jnp.where(causal, b[..., :, None] - b[..., None, :] + ig[..., None, :], NEG_INF)

    a = b[..., -1]
    g_end = a[..., None] - b + ig
    m_loc = jnp.max(g_end, axis=-1)
    w_end = jnp.exp(g_end - m_loc[..., None])
    c_loc = jnp.einsum('bhcl,bhclv,bhclk->bhcvk', w_end, vv, k)
    n_loc = jnp.einsum('bhcl,bhclk->bhck', w_end, k)

    def step(carry, xs):
        c_st, n_st, m_st = carry
        a_c, m_l, c_l, n_l = xs
        m_new = jnp.maximum(a_c + m_st, m_l)
        decay = jnp.exp(a_c + m_st - m_new)
        fresh = jnp.exp(m_l - m_new)
        c_new = decay[..., None, None] * c_st + fresh[..., None, None] * c_l
        n_new = decay[..., None] * n_st + fresh[..., None] * n_l
        return (c_new, n_new, m_new), (c_st, n_st, m_st)

    init = (jnp.zeros((bsz, N_HEADS, HEAD_DIM, HEAD_DIM), f32),
            jnp.zeros((bsz, N_HEADS, HEAD_DIM), f32),
            jnp.zeros((bsz, N_HEADS), f32))
    xs = (jnp.moveaxis(a, 2, 0), jnp.moveaxis(m_loc, 2, 0),
          jnp.moveaxis(c_loc, 2, 0), jnp.moveaxis(n_loc, 2, 0))
    _, (c_in, n_in, m_in) = lax.scan(step, init, xs)
    c_in = jnp.moveaxis(c_in, 0, 2)
    n_in = jnp.moveaxis(n_in, 0, 2)
    m_in = jnp.moveaxis(m_in, 0, 2)

    inter = b + m_in[..., None]
    m_t = jnp.maximum(inter, jnp.max(dmat, axis=-1))
    e_inter = jnp.exp(inter - m_t)
    s_qk = jnp.einsum('bhctd,bhcsd->bhcts', q, k) * jnp.exp(dmat - m_t[..., None])
    num = (e_inter[..., None] * jnp.einsum('bhcvk,bhctk->bhctv', c_in, q)
           + jnp.einsum('bhcts,bhcsv->bhctv', s_qk, vv))
    den = e_inter * jnp.einsum('bhck,bhctk->bhct', n_in, q) + jnp.sum(s_qk, axis=-1)
    h = num / jnp.maximum(jnp.abs(den), jnp.exp(-m_t))[..., None]
    h = h.reshape(bsz, N_HEADS, seq, HEAD_DIM).transpose(0, 2, 1, 3)
    h = rmsnorm(h, head_g.reshape(N_HEADS, HEAD_DIM))
    h = h * jax.nn.sigmoid(o_pre.astype(f32)).reshape(bsz, seq, N_HEADS, HEAD_DIM)
    return h.reshape(bsz, seq, GROUP_WIDTH).astype(u.dtype)

def dilated_mixer(q, k, v, cos, sin):
    bsz, seq = q.shape[0], q.shape[1]
    q = apply_rope(q, cos, sin)
    k = apply_rope(k, cos, sin)
    pad = ((0, 0), (DILATED_PAD, 0), (0, 0), (0, 0))
    kp, vp = jnp.pad(k, pad), jnp.pad(v, pad)
    scale = HEAD_DIM ** -0.5

    def block(s0):
        qb = lax.dynamic_slice_in_dim(q, s0, Q_BLOCK, axis=1)
        tq = s0 + jnp.arange(Q_BLOCK)
        kseg = lax.dynamic_slice_in_dim(kp, s0, DILATED_PAD + Q_BLOCK, axis=1)
        vseg = lax.dynamic_slice_in_dim(vp, s0, DILATED_PAD + Q_BLOCK, axis=1)
        outs, lses = [], []
        for window, dil in DILATED_PATTERNS:
            n_keys = window // dil + 1
            rel = np.arange(Q_BLOCK)[:, None] + DILATED_PAD - np.arange(n_keys)[None, :] * dil
            kg, vg = kseg[:, rel], vseg[:, rel]
            kpos = tq[:, None] - jnp.arange(n_keys)[None, :] * dil
            s = jnp.einsum('bqhd,bqjhd->bhqj', qb, kg) * scale
            p, lse = masked_softmax(s, kpos >= 0, return_lse=True)
            outs.append(jnp.einsum('bhqj,bqjhd->bqhd', p.astype(vg.dtype), vg))
            lses.append(jnp.transpose(lse, (0, 2, 1)))
        alpha = jax.nn.softmax(jnp.stack(lses, axis=0), axis=0)
        return jnp.einsum('gbqh,gbqhd->bqhd', alpha.astype(q.dtype), jnp.stack(outs, axis=0))

    o = sweep_query_blocks(block, seq)
    return o.reshape(bsz, seq, GROUP_WIDTH)

def first_inputs(seed: int = 0) -> dict:
    key = jax.random.key(seed)
    k = jax.random.split(key, 20)
    f32 = jnp.float32

    def normal(kk, shape, scale):
        return jax.random.normal(kk, shape, f32) * scale

    def gain(kk, shape):
        return 1.0 + 0.02 * jax.random.normal(kk, shape, f32)

    forget_bias = jnp.linspace(3.0, 6.0, N_HEADS, dtype=f32)
    mlstm_gate_b = jnp.stack([normal(k[10], (DEPTH, N_HEADS), 0.1),
                              forget_bias + normal(k[11], (DEPTH, N_HEADS), 0.1)], axis=1)
    return {
        'x': normal(k[0], (BATCH, SEQ, D_MODEL), 1.0),
        'norm_mix': gain(k[1], (DEPTH, D_MODEL)),
        'w_in': normal(k[2], (DEPTH, D_MODEL, D_IN), D_MODEL ** -0.5),
        'nsa_cmp_pos': normal(k[3], (DEPTH, 2, NSA_CMP_LEN, HEAD_DIM), 0.1),
        'nsa_cmp_w': normal(k[4], (DEPTH, 2, NSA_CMP_LEN * HEAD_DIM, HEAD_DIM), (NSA_CMP_LEN * HEAD_DIM) ** -0.5),
        'diff_lambda': normal(k[5], (DEPTH, 4, DIFF_HALF), 0.1),
        'diff_norm': gain(k[6], (DEPTH, HEAD_DIM)),
        'mlstm_conv_w': normal(k[7], (DEPTH, MLSTM_CONV, GROUP_WIDTH), MLSTM_CONV ** -0.5),
        'mlstm_conv_b': normal(k[8], (DEPTH, GROUP_WIDTH), 0.02),
        'mlstm_wq': normal(k[9], (DEPTH, N_HEADS, HEAD_DIM, HEAD_DIM), HEAD_DIM ** -0.5),
        'mlstm_wk': normal(k[12], (DEPTH, N_HEADS, HEAD_DIM, HEAD_DIM), HEAD_DIM ** -0.5),
        'mlstm_gate_b': mlstm_gate_b,
        'mlstm_norm': gain(k[13], (DEPTH, GROUP_WIDTH)),
        'w_out': normal(k[14], (DEPTH, D_MODEL, D_MODEL), D_MODEL ** -0.5),
        'norm_ffn': gain(k[15], (DEPTH, D_MODEL)),
        'w_gate': normal(k[16], (DEPTH, D_MODEL, D_FF), D_MODEL ** -0.5),
        'w_up': normal(k[17], (DEPTH, D_MODEL, D_FF), D_MODEL ** -0.5),
        'w_down': normal(k[18], (DEPTH, D_FF, D_MODEL), D_FF ** -0.5),
        'norm_final': gain(k[19], (D_MODEL,)),
    }

def first_block(x, norm_mix, w_in, nsa_cmp_pos, nsa_cmp_w, diff_lambda, diff_norm,
              mlstm_conv_w, mlstm_conv_b, mlstm_wq, mlstm_wk, mlstm_gate_b, mlstm_norm,
              w_out, norm_ffn, w_gate, w_up, w_down, norm_final):
    bsz, seq, _ = x.shape
    cos64, sin64 = rope_tables(seq, HEAD_DIM)
    cos32, sin32 = rope_tables(seq, DIFF_HALF)
    offsets = [int(o) for o in np.cumsum(IN_SPLITS)[:-1]]

    def heads(t):
        return t.reshape(bsz, seq, N_HEADS, HEAD_DIM)

    for layer in range(DEPTH):
        h = rmsnorm(x, norm_mix[layer])
        z = h @ w_in[layer]
        (a_q, a_kc, a_vc, a_ks, a_vs, a_kw, a_vw, a_g,
         b_q, b_k, b_v, c_u, c_v, c_i, c_f, c_o, d_q, d_k, d_v) = jnp.split(z, offsets, axis=-1)
        o_a = nsa_mixer(heads(a_q), a_kc, a_vc, a_ks, a_vs, a_kw, a_vw, a_g,
                        nsa_cmp_pos[layer], nsa_cmp_w[layer], cos64, sin64)
        lam_init = 0.8 - 0.6 * math.exp(-0.3 * layer)
        o_b = diff_mixer(b_q.reshape(bsz, seq, N_HEADS, 2, DIFF_HALF),
                         b_k.reshape(bsz, seq, N_HEADS, 2, DIFF_HALF), heads(b_v),
                         diff_lambda[layer], diff_norm[layer], lam_init, cos32, sin32)
        o_c = mlstm_mixer(c_u, c_v, c_i, c_f, c_o, mlstm_conv_w[layer], mlstm_conv_b[layer],
                          mlstm_wq[layer], mlstm_wk[layer], mlstm_gate_b[layer], mlstm_norm[layer])
        o_d = dilated_mixer(heads(d_q), heads(d_k), heads(d_v), cos64, sin64)
        x = x + jnp.concatenate([o_a, o_b, o_c, o_d], axis=-1) @ w_out[layer]
        h = rmsnorm(x, norm_ffn[layer])
        x = x + (jax.nn.silu(h @ w_gate[layer]) * (h @ w_up[layer])) @ w_down[layer]
    return rmsnorm(x, norm_final)


CHUNK = 64
N_MIXERS_2 = 2
N_LAYERS_A = (DEPTH + N_MIXERS_2 - 1) // N_MIXERS_2
N_LAYERS_B = DEPTH // N_MIXERS_2
CONV_A_WIDTH = 31
CONV_B_WIDTH = 3
N_GROUPS = 4
EXPERTS_PER_GROUP = 8
N_EXPERTS = N_GROUPS * EXPERTS_PER_GROUP
TOP_K = 2
D_EXPERT = D_MODEL // 2
ROUTE_BLOCK = 128
ALPHA = (2.0 * DEPTH) ** 0.25
BETA = (8.0 * DEPTH) ** -0.25
LN_EPS = 1e-5


def layer_norm(x, g, b):
    xf = x.astype(jnp.float32)
    mu = jnp.mean(xf, axis=-1, keepdims=True)
    var = jnp.mean(jnp.square(xf - mu), axis=-1, keepdims=True)
    y = (xf - mu) * lax.rsqrt(var + LN_EPS)
    return (y * g.astype(jnp.float32) + b.astype(jnp.float32)).astype(x.dtype)

def causal_depthwise_conv(u, w):
    k = w.shape[0]
    return lax.conv_general_dilated(
        u, w[:, None, :].astype(u.dtype), window_strides=(1,), padding=[(k - 1, 0)],
        dimension_numbers=("NWC", "WIO", "NWC"), feature_group_count=u.shape[-1])

def conformer_conv(h, w_in, b_in, w_dw, b_dw, ln_g, ln_b, w_out, b_out):
    a, g = jnp.split(h @ w_in + b_in, 2, axis=-1)
    u = a * jax.nn.sigmoid(g)
    u = causal_depthwise_conv(u, w_dw) + b_dw
    u = jax.nn.silu(layer_norm(u, ln_g, ln_b))
    return u @ w_out + b_out

def short_gated_conv(h, w_in, w_dw, w_out):
    gb, gc, v = jnp.split(h @ w_in, 3, axis=-1)
    u = causal_depthwise_conv(gc * v, w_dw)
    return (gb * u) @ w_out

def hierarchical_moe(h, w_group, b_group, w_router, b_router, w_gate, w_up, w_down):
    bsz, seq, d = h.shape
    t = bsz * seq
    xf = h.reshape(t, d)
    g_logits = (xf @ w_group + b_group).astype(jnp.float32)
    g_probs = jax.nn.softmax(g_logits, axis=-1)
    g_idx = jnp.argmax(g_logits, axis=-1).astype(jnp.int32)
    g_w = jnp.take_along_axis(g_probs, g_idx[:, None], axis=-1)
    e_logits = (xf @ w_router + b_router).astype(jnp.float32).reshape(t, N_GROUPS, EXPERTS_PER_GROUP)
    e_logits = jnp.take_along_axis(e_logits, g_idx[:, None, None], axis=1)[:, 0]
    e_probs = jax.nn.softmax(e_logits, axis=-1)
    top_p, top_e = lax.top_k(e_probs, TOP_K)
    top_p = top_p / jnp.sum(top_p, axis=-1, keepdims=True)
    weights = (g_w * top_p).reshape(-1)
    flat_e = (g_idx[:, None] * EXPERTS_PER_GROUP + top_e.astype(jnp.int32)).reshape(-1)
    n_assign = t * TOP_K
    order = jnp.argsort(flat_e)
    sorted_e = flat_e[order]
    sorted_tok = (order // TOP_K).astype(jnp.int32)
    counts = jnp.zeros((N_EXPERTS,), jnp.int32).at[flat_e].add(1)
    starts = jnp.cumsum(counts) - counts
    padded = (counts + ROUTE_BLOCK - 1) // ROUTE_BLOCK * ROUTE_BLOCK
    pad_ends = jnp.cumsum(padded)
    pad_starts = pad_ends - padded
    dest = pad_starts[sorted_e] + (jnp.arange(n_assign, dtype=jnp.int32) - starts[sorted_e])
    n_slots = n_assign + N_EXPERTS * ROUTE_BLOCK
    n_blocks = n_slots // ROUTE_BLOCK
    slot_tok = jnp.full((n_slots,), t, jnp.int32).at[dest].set(sorted_tok)
    block_start = jnp.arange(n_blocks, dtype=jnp.int32) * ROUTE_BLOCK
    block_e = jnp.minimum(jnp.sum(pad_ends[None, :] <= block_start[:, None], axis=-1), N_EXPERTS - 1)
    x_pad = jnp.concatenate([xf, jnp.zeros((1, d), xf.dtype)], axis=0)
    xb = x_pad[slot_tok].reshape(n_blocks, ROUTE_BLOCK, d)

    def expert_block(args):
        xblk, e = args
        hid = jax.nn.silu(xblk @ w_gate[e]) * (xblk @ w_up[e])
        return hid @ w_down[e]

    yb = lax.map(expert_block, (xb, block_e)).reshape(n_slots, d)
    contrib = weights[order][:, None].astype(xf.dtype) * yb[dest]
    y = jnp.zeros((t, d), xf.dtype).at[sorted_tok].add(contrib)
    return y.reshape(bsz, seq, d)

def second_inputs(seed: int = 0) -> dict:
    key = jax.random.key(seed)
    ks = jax.random.split(key, 26)
    D, F = D_MODEL, D_EXPERT
    nrm = lambda k, shape, s: jax.random.normal(k, shape, jnp.float32) * s
    return {
        "x": nrm(ks[0], (BATCH, SEQ, D), 1.0),
        "c": nrm(ks[1], (BATCH, D), 1.0),
        "ada_w": nrm(ks[2], (DEPTH, D, 6 * D), 0.5 * D ** -0.5),
        "ada_b": nrm(ks[3], (DEPTH, 6 * D), 0.01),
        "a_w_in": nrm(ks[4], (N_LAYERS_A, D, 2 * D), D ** -0.5),
        "a_b_in": nrm(ks[5], (N_LAYERS_A, 2 * D), 0.01),
        "a_w_dw": nrm(ks[6], (N_LAYERS_A, CONV_A_WIDTH, D), CONV_A_WIDTH ** -0.5),
        "a_b_dw": nrm(ks[7], (N_LAYERS_A, D), 0.01),
        "a_ln_g": 1.0 + nrm(ks[8], (N_LAYERS_A, D), 0.01),
        "a_ln_b": nrm(ks[9], (N_LAYERS_A, D), 0.01),
        "a_w_out": nrm(ks[10], (N_LAYERS_A, D, D), BETA * D ** -0.5),
        "a_b_out": nrm(ks[11], (N_LAYERS_A, D), 0.01),
        "b_w_in": nrm(ks[12], (N_LAYERS_B, D, 3 * D), D ** -0.5),
        "b_w_dw": nrm(ks[13], (N_LAYERS_B, CONV_B_WIDTH, D), CONV_B_WIDTH ** -0.5),
        "b_w_out": nrm(ks[14], (N_LAYERS_B, D, D), BETA * D ** -0.5),
        "mix_ln_g": 1.0 + nrm(ks[15], (DEPTH, D), 0.01),
        "mix_ln_b": nrm(ks[16], (DEPTH, D), 0.01),
        "ffn_ln_g": 1.0 + nrm(ks[17], (DEPTH, D), 0.01),
        "ffn_ln_b": nrm(ks[18], (DEPTH, D), 0.01),
        "r_w_group": nrm(ks[19], (DEPTH, D, N_GROUPS), D ** -0.5),
        "r_b_group": nrm(ks[20], (DEPTH, N_GROUPS), 0.01),
        "r_w_expert": nrm(ks[21], (DEPTH, D, N_EXPERTS), D ** -0.5),
        "r_b_expert": nrm(ks[22], (DEPTH, N_EXPERTS), 0.01),
        "e_w_gate": nrm(ks[23], (DEPTH, N_EXPERTS, D, F), D ** -0.5),
        "e_w_up": nrm(ks[24], (DEPTH, N_EXPERTS, D, F), D ** -0.5),
        "e_w_down": nrm(ks[25], (DEPTH, N_EXPERTS, F, D), BETA * F ** -0.5),
    }

def second_block(x, c, ada_w, ada_b, a_w_in, a_b_in, a_w_dw, a_b_dw, a_ln_g, a_ln_b, a_w_out, a_b_out,
              b_w_in, b_w_dw, b_w_out, mix_ln_g, mix_ln_b, ffn_ln_g, ffn_ln_b,
              r_w_group, r_b_group, r_w_expert, r_b_expert, e_w_gate, e_w_up, e_w_down):
    c_act = jax.nn.silu(c)
    for i in range(DEPTH):
        mods = (c_act @ ada_w[i] + ada_b[i])[:, None, :]
        sh_m, sc_m, g_m, sh_f, sc_f, g_f = jnp.split(mods, 6, axis=-1)
        h = x * (1.0 + sc_m) + sh_m
        j = i // N_MIXERS_2
        if i % N_MIXERS_2 == 0:
            y = conformer_conv(h, a_w_in[j], a_b_in[j], a_w_dw[j], a_b_dw[j],
                               a_ln_g[j], a_ln_b[j], a_w_out[j], a_b_out[j])
        else:
            y = short_gated_conv(h, b_w_in[j], b_w_dw[j], b_w_out[j])
        x = layer_norm(ALPHA * x + (1.0 + g_m) * y, mix_ln_g[i], mix_ln_b[i])
        h = x * (1.0 + sc_f) + sh_f
        y = hierarchical_moe(h, r_w_group[i], r_b_group[i], r_w_expert[i], r_b_expert[i],
                             e_w_gate[i], e_w_up[i], e_w_down[i])
        x = layer_norm(ALPHA * x + (1.0 + g_f) * y, ffn_ln_g[i], ffn_ln_b[i])
    return x


def setup_inputs(seed=0):
    out = dict(first_inputs(seed))
    for name, value in second_inputs(seed + 1).items():
        if name != "x":
            out[name + "_2"] = value
    return out


def reference(
    x, norm_mix, w_in, nsa_cmp_pos, nsa_cmp_w, diff_lambda, diff_norm, mlstm_conv_w,
    mlstm_conv_b, mlstm_wq, mlstm_wk, mlstm_gate_b, mlstm_norm, w_out, norm_ffn, w_gate, w_up,
    w_down, norm_final, c_2, ada_w_2, ada_b_2, a_w_in_2, a_b_in_2, a_w_dw_2, a_b_dw_2, a_ln_g_2,
    a_ln_b_2, a_w_out_2, a_b_out_2, b_w_in_2, b_w_dw_2, b_w_out_2, mix_ln_g_2, mix_ln_b_2,
    ffn_ln_g_2, ffn_ln_b_2, r_w_group_2, r_b_group_2, r_w_expert_2, r_b_expert_2, e_w_gate_2,
    e_w_up_2, e_w_down_2,
):
    x = first_block(
        x, norm_mix, w_in, nsa_cmp_pos, nsa_cmp_w, diff_lambda, diff_norm, mlstm_conv_w,
        mlstm_conv_b, mlstm_wq, mlstm_wk, mlstm_gate_b, mlstm_norm, w_out, norm_ffn, w_gate,
        w_up, w_down, norm_final,
    )
    return second_block(
        x, c_2, ada_w_2, ada_b_2, a_w_in_2, a_b_in_2, a_w_dw_2, a_b_dw_2, a_ln_g_2, a_ln_b_2,
        a_w_out_2, a_b_out_2, b_w_in_2, b_w_dw_2, b_w_out_2, mix_ln_g_2, mix_ln_b_2, ffn_ln_g_2,
        ffn_ln_b_2, r_w_group_2, r_b_group_2, r_w_expert_2, r_b_expert_2, e_w_gate_2, e_w_up_2,
        e_w_down_2,
    )


_drawn_inputs = setup_inputs


def setup_inputs(seed=0):
    import zlib

    import numpy as np

    out = dict(_drawn_inputs(seed))
    spreads = {}
    factors = {'mlstm_norm': 3.427,
     'a_b_in_2': 8.0,
     'a_b_dw_2': 3.79,
     'a_ln_g_2': 4.544,
     'a_ln_b_2': 8.0,
     'a_b_out_2': 4.768,
     'mix_ln_g_2': 2.9,
     'ffn_ln_g_2': 3.188,
     'ffn_ln_b_2': 2.884,
     'r_b_group_2': 4.783,
     'r_b_expert_2': 5.277}
    for name, (base, spread) in spreads.items():
        noise = np.random.default_rng([zlib.crc32(name.encode()), seed]).standard_normal(out[name].shape)
        drawn = base * np.exp(spread * noise) if base else spread * noise
        out[name] = jnp.asarray(drawn.astype(out[name].dtype))
    for name, factor in factors.items():
        out[name] = (out[name] * factor).astype(out[name].dtype)
    return out
```

```python
import math
from concourse import mybir

F32 = mybir.dt.float32
ACT = mybir.ActivationFunctionType
ALU = mybir.AluOpType
AX = mybir.AxisListType.X

P = 128
SEQ, D, DEPTH = 256, 1024, 2
TILES, KC = SEQ // P, D // P
HD, NH, GW = 64, 4, 256
D_FF = 2816
EPS, LN_EPS = 1e-6, 1e-5
ALPHA = (2.0 * DEPTH) ** 0.25

Z_Q, Z_KC, Z_VC, Z_KS, Z_VS, Z_KW, Z_VW, Z_G = 0, 256, 320, 384, 448, 512, 576, 640
Z_BQ, Z_BV, Z_U, Z_CV, Z_I, Z_F, Z_O, Z_DQ, Z_DV = 652, 1164, 1420, 1676, 1932, 1936, 1940, 2196, 2708
D_IN = 2964
N_IN = 6
ZC = D_IN // N_IN
SLOT = 4096
N_SLOTS = 6

T_QRAW, T_KC, T_VC, T_QROT, T_KS, T_KW, T_DQ, T_DK, T_BQ, T_BK = 0, 4, 5, 6, 10, 11, 12, 16, 20, 28
N_T = 36
R_Q, R_K, R_D, R_B, R_ALL = 0, 256, 384, 896, 1408

N_CMP, CMP_LEN, CMP_STRIDE = 15, 32, 16
N_PREP = 16
FU = 256
N_FU = D_FF // FU

UNITS = ([(k, t, 0) for k in ("slc", "win", "dil") for t in range(TILES)]
         + [("diff", t, hp) for t in range(TILES) for hp in range(2)]
         + [(k, t, 0) for k in ("mlstm", "cmp") for t in range(TILES)])

FIRST_SEMS = ["std", "hn", "tr", "hT", "z_ps", "z_act", "z_dve", "rope", "prep_ps", "prep_ev", "gates_in", "gate_abs",
              "gate_ln", "gate_rows", "gate_cols", "conv", "uc", "blocks", "lam_in", "lam_exp", "small_ready",
              "scores", "masked", "exps", "probs", "pt_ps", "pt", "pv", "o_done", "ss", "o_std", "o_final",
              "std_b", "hn_b", "tr_b", "hT_b", "tr_o", "OT", "y_ps", "x_mid",
              "gu", "silu", "hid", "down", "ffn_full0", "ffn_full1", "ffn_free0", "ffn_free1", "arrive"]


class Mem:
    pass


def host_tables():
    import numpy as np
    t = {}
    t["ident"] = np.eye(P, dtype=np.float32)
    for name, dim in (("64", HD), ("32", HD // 2)):
        inv = (1.0 / (np.float32(10000.0) ** (np.arange(0, dim, 2, dtype=np.float32) / np.float32(dim)))).astype(np.float32)
        ang = np.arange(SEQ, dtype=np.float32)[:, None] * inv[None, :]
        c, s = np.cos(ang).astype(np.float32), np.sin(ang).astype(np.float32)
        t["cos" + name] = np.concatenate([c, c], 1)
        t["sin" + name] = np.concatenate([-s, s], 1)
    q, k = np.arange(SEQ)[:, None], np.arange(SEQ)[None, :]
    dist = q - k
    t["causal"] = np.where(dist >= 0, 0.0, -1e30).astype(np.float32)
    counts = ((dist >= 0) & (dist <= 128)).astype(np.float32)
    counts += ((dist >= 0) & (dist % 4 == 0)).astype(np.float32)
    counts += ((dist >= 0) & (dist % 16 == 0)).astype(np.float32)
    t["dil_counts"] = counts
    t["dil_mask"] = np.where(counts > 0, 0.0, -1e30).astype(np.float32)
    end = np.arange(N_CMP) * CMP_STRIDE + CMP_LEN - 1
    seen = end[None, :] <= np.arange(SEQ)[:, None]
    t["cmp_mask"] = np.where(seen, 0.0, -1e30).astype(np.float32)
    t["cmp_seen"] = seen.astype(np.float32)
    sel = np.zeros((NH, NH, P), np.float32)
    for h in range(NH):
        sel[h, h] = 1.0
    t["head_rows"] = sel
    init = [0.8 - 0.6 * math.exp(-0.3 * layer) for layer in range(DEPTH)]
    t["lam_init"] = np.array([[v, 1.0 - v] for v in init], np.float32)
    t["before"] = np.triu(np.ones((P, P), np.float32), 1)
    t["ones"] = np.ones((P, P), np.float32)
    t["iota64"] = np.tile(np.arange(64, dtype=np.float32), (P, 1))
    return t


def place(nc, m):
    sb = nc.alloc_sbuf_tensor
    m.ring = sb("ring", [P, N_SLOTS * SLOT], F32)
    m.x = sb("x", [P, TILES, D], F32)
    m.hT = sb("hT", [P, KC, SEQ], F32)
    m.O = sb("O", [P, TILES, D], F32)
    m.z = sb("z", [P, TILES, D_IN], F32)
    m.qkT = sb("qkT", [P, N_T, SEQ], F32)
    m.uT = sb("uT", [P, 2, SEQ + 3], F32)
    m.ucT = sb("ucT", [P, 2, SEQ], F32)
    m.posT = sb("posT", [HD, 2, CMP_LEN], F32)
    m.kcT = sb("kcT", [HD, 16], F32)
    m.vc = sb("vc", [16, HD], F32)
    m.gates = sb("gates", [P, TILES, 12], F32)
    m.small = sb("small", [P, 160], F32)
    m.eps = sb("eps", [P, 4], F32)
    m.ident = sb("ident", [P, P], F32)
    m.cos64 = sb("cos64", [P, TILES, HD], F32)
    m.sin64 = sb("sin64", [P, TILES, HD], F32)
    m.cos32 = sb("cos32", [P, TILES, HD // 2], F32)
    m.sin32 = sb("sin32", [P, TILES, HD // 2], F32)
    m.causal = sb("causal", [P, TILES, SEQ], F32)
    m.dil_mask = sb("dil_mask", [P, TILES, SEQ], F32)
    m.dil_counts = sb("dil_counts", [P, TILES, SEQ], F32)
    m.cmp_mask = sb("cmp_mask", [P, TILES, N_CMP], F32)
    m.cmp_seen = sb("cmp_seen", [P, TILES, N_CMP], F32)
    m.head_rows = sb("head_rows", [NH, NH, P], F32)
    m.g_mix = sb("g_mix", [P, KC], F32)
    m.g_ffn = sb("g_ffn", [P, KC], F32)
    m.pos = sb("pos", [CMP_LEN, 2, HD], F32)
    m.lamv = sb("lamv", [P, 4, 32], F32)
    m.g_sub = sb("g_sub", [P, 2 * GW], F32)
    m.conv_w = sb("conv_w", [P, 2, 4], F32)
    m.conv_b = sb("conv_b", [P, 2], F32)
    m.wqz = sb("wqz", [P, 2, 2, HD], F32)
    m.wkz = sb("wkz", [P, 2, 2, HD], F32)
    m.gate_b = sb("gate_b", [NH, 2], F32)
    m.lam_init = sb("lam_init", [P, 2], F32)
    m.ps = nc.alloc_psum_tensor("ps", [P, 8, 512], F32)

    def ring(a, b):
        return m.ring[:, a:b]
    m.slot = [ring(s * SLOT, (s + 1) * SLOT) for s in range(N_SLOTS)]
    m.ffn = [ring(2 * SLOT + b * 6144, 2 * SLOT + (b + 1) * 6144) for b in range(2)]
    m.rz = m.ffn[0][:, 0:2 * R_ALL].rearrange("p (i c) -> p i c", i=TILES)
    att = m.ffn[1]
    m.sm = att[:, 0:2048].rearrange("p (b h k) -> p b h k", b=2, h=4)
    m.pr = att[:, 2048:4096].rearrange("p (b h k) -> p b h k", b=2, h=4)
    m.rb = att[:, 4096:5120].rearrange("p (h k) -> p h k", h=4)
    m.pt = att[:, 5120:6144].rearrange("p (h t q) -> p h t q", h=4, t=2)
    flat = m.hT[:].rearrange("p j t -> p (j t)")
    m.tmp = flat[:, 0:R_ALL]
    m.blocks = flat[0:HD, 0:2 * CMP_LEN * N_CMP].rearrange("d (w l n) -> d w l n", w=2, l=CMP_LEN)
    m.grow = m.O[:].rearrange("p i c -> p (i c)").rearrange("p (g t) -> p g t", t=SEQ)

    s = m.small
    m.ssq, m.std, m.rstd = s[:, 0:2], s[:, 2:4], s[:, 4:6]
    m.mx = [s[:, 8 + 4 * b:12 + 4 * b] for b in range(2)]
    m.nmx = [s[:, 16 + 4 * b:20 + 4 * b] for b in range(2)]
    m.zs = [s[:, 24 + 4 * b:28 + 4 * b] for b in range(2)]
    m.rs = [s[:, 32 + 4 * b:36 + 4 * b] for b in range(2)]
    m.nM = s[:, 40:48].rearrange("p (i h) -> p i h", i=TILES)
    m.em = s[:, 48:56].rearrange("p (i h) -> p i h", i=TILES)
    m.lam = s[:, 56:62]
    m.sso = s[:, 64:80].rearrange("p (i h) -> p i h", i=TILES)
    m.sstd = s[:, 80:96].rearrange("p (i h) -> p i h", i=TILES)
    m.srec = s[:, 96:112].rearrange("p (i h) -> p i h", i=TILES)


def banks(m, b, n=1):
    return m.ps[:, b:b + n, :].rearrange("p b c -> p (b c)")


def bcast(ap, shape):
    return ap.to_broadcast(shape)



def norm_act(nc, act, m, std):
    for i in range(TILES):
        nc.scalar.activation(m.O[:, i, :], m.x[:, i, :], ACT.Square, accum_out=m.ssq[:, i:i + 1])
    act.drain()
    nc.scalar.activation(m.std, m.ssq, ACT.Sqrt, scale=1.0 / D, bias=m.eps[:, 0:1]).then_inc(std, 1)


def norm_dve(nc, dve, m, std, hn):
    dve.wait_ge(std, 1)
    nc.vector.reciprocal(m.rstd, m.std)
    dve.drain()
    for i in range(TILES):
        nc.vector.tensor_scalar(m.O[:, i, :], m.x[:, i, :], m.rstd[:, i:i + 1], None, ALU.mult).then_inc(hn, 1)


def transpose_pe(nc, pe, m, ready, count, done):
    pe.wait_ge(ready, count)
    for j in range(KC):
        for i in range(TILES):
            src = m.O[:, i, :].rearrange("t (p j) -> t j p", j=KC)[:, j, :]
            dst = m.ps[:, j // 2, (j % 2) * 256 + i * P:(j % 2) * 256 + (i + 1) * P]
            last = nc.tensor.transpose(dst, src, m.ident[:])
        last.then_inc(done, 1)


def evacuate_dve(nc, dve, m, gain, tr, done):
    for j in range(KC):
        dve.wait_ge(tr, 2 * (j // 2) + 2)
        src = m.ps[:, j // 2, (j % 2) * 256:(j % 2) * 256 + SEQ]
        if gain is None:
            nc.vector.tensor_copy(m.hT[:, j, :], src).then_inc(done, 1)
        else:
            nc.vector.tensor_scalar(m.hT[:, j, :], src, gain[:, j:j + 1], None, ALU.mult).then_inc(done, 1)


def prep_bank(b):
    return 2 * (b % 4)



def first_sync(nc, sp, m, a):
    s = m.s
    with sp.Fori(0, DEPTH) as L:
        w_in = a["w_in"][L].rearrange("(p j) n -> p j n", j=KC)
        for c in range(N_IN):
            per = 2 if c in (0, 1, 5) else 1
            sp.wait_ge(m.ring_free[c], L * per + 1)
            sp.dma_start(m.slot[c][:, 0:KC * ZC].rearrange("p (j n) -> p j n", j=KC),
                         w_in[:, :, c * ZC:(c + 1) * ZC]).then_inc(m.ring_full[c], 16)
        sp.wait_ge(m.ring_free[5], L * 2 + 2)
        sp.dma_start(m.slot[5][0:HD, :].rearrange("d (w l e) -> d w l e", w=2, l=CMP_LEN),
                     a["nsa_cmp_w"][L].rearrange("w (l d) e -> d w l e", d=HD)).then_inc(m.ring_full[5], 16)
        w_out = a["w_out"][L].rearrange("(p j) n -> p j n", j=KC)
        for n in range(2):
            sp.wait_ge(m.ring_free[n], L * 2 + 2)
            sp.dma_start(m.slot[n].rearrange("p (j n) -> p j n", j=KC),
                         w_out[:, :, n * 512:(n + 1) * 512]).then_inc(m.ring_full[n], 16)
        w_gate = a["w_gate"][L].rearrange("(p j) n -> p j n", j=KC)
        w_up = a["w_up"][L].rearrange("(p j) n -> p j n", j=KC)
        w_down = a["w_down"][L].rearrange("(u p j) n -> u p (j n)", p=P, j=2)
        for u in range(N_FU):
            buf = m.ffn[u % 2]
            if u == 0:
                sp.wait_ge(s["prep_ps"], 11)
            elif u == 1:
                sp.wait_ge(s["pv"], len(UNITS))
            else:
                sp.wait_ge(s[f"ffn_free{u % 2}"], u // 2)
            full = s[f"ffn_full{u % 2}"]
            sp.dma_start(buf[:, 0:2048].rearrange("p (j n) -> p j n", j=KC), w_gate[:, :, u * FU:(u + 1) * FU]).then_inc(full, 16)
            sp.dma_start(buf[:, 2048:4096].rearrange("p (j n) -> p j n", j=KC), w_up[:, :, u * FU:(u + 1) * FU]).then_inc(full, 16)
            sp.dma_start(buf[:, 4096:6144], w_down[u]).then_inc(full, 16)


N_PARAMS = 14


def first_pool(nc, pool, m, a):
    s = m.s
    with pool.Fori(0, DEPTH) as L:
        pool.dma_start(m.g_mix[:], a["norm_mix"][L].rearrange("(p j) -> p j", j=KC)).then_inc(m.params, 16)
        pool.dma_start(m.g_ffn[:], a["norm_ffn"][L].rearrange("(p j) -> p j", j=KC)).then_inc(m.params, 16)
        pool.dma_start(m.pos[:], a["nsa_cmp_pos"][L].rearrange("w l d -> l w d")).then_inc(m.params, 16)
        pool.dma_start(m.lamv[:], a["diff_lambda"][L].partition_broadcast(P)).then_inc(m.params, 16)
        for h in range(NH):
            pool.dma_start(m.g_sub[:, h * HD:(h + 1) * HD], a["diff_norm"][L].partition_broadcast(P)).then_inc(m.params, 16)
        pool.dma_start(m.g_sub[:, GW:2 * GW], a["mlstm_norm"][L].partition_broadcast(P)).then_inc(m.params, 16)
        with nc.allow_non_contiguous_dma(reason="small parameters"):
            for c in range(2):
                pool.dma_start(m.conv_w[:, c, :], a["mlstm_conv_w"][L][:, c * P:(c + 1) * P].rearrange("k p -> p k")).then_inc(m.params, 16)
            pool.dma_start(m.conv_b[:], a["mlstm_conv_b"][L].rearrange("(c p) -> p c", p=P)).then_inc(m.params, 16)
            pool.dma_start(m.gate_b[:], a["mlstm_gate_b"][L].rearrange("g h -> h g")).then_inc(m.params, 16)
        pool.dma_start(m.lam_init[:], a["lam_init"][L].partition_broadcast(P)).then_inc(m.params, 16)
        for w, src in ((m.wqz, a["mlstm_wq"]), (m.wkz, a["mlstm_wk"])):
            for hp in range(2):
                pool.dma_start(w[hp * HD:(hp + 1) * HD, :, hp, :],
                               src[L].rearrange("(c hp) d e -> hp d c e", hp=2)[hp]).then_inc(m.heads_w, 16)
        layer_end(nc, pool, m, L)


def layer_end(nc, eng, m, L):
    eng.drain().then_inc(m.s["arrive"], 1)
    eng.wait_ge(m.release, L + 1)
    eng.sem_inc(m.seen, 1)


def layer_end_leader(nc, dve, m):
    dve.wait_ge(m.s["arrive"], 3)
    dve.sem_clear(m.first_range)
    dve.sem_inc(m.release, 1)


def mlstm_rows(m, col, h):
    at = col + (h % 2) * SEQ
    return m.z[0:HD, h // 2, at:at + SEQ]


def unit_maps(m, kind, t, hp):
    out = []
    q = slice(t * P, (t + 1) * P)
    nk = P * (t + 1)
    for h in range(4):
        if kind in ("slc", "win"):
            out.append((m.qkT[0:HD, T_QROT + h, q], m.qkT[0:HD, T_KS if kind == "slc" else T_KW, 0:nk]))
        elif kind == "dil":
            out.append((m.qkT[0:HD, T_DQ + h, q], m.qkT[0:HD, T_DK + h, 0:nk]))
        elif kind == "diff":
            out.append((m.qkT[0:32, T_BQ + 4 * hp + h, q], m.qkT[0:32, T_BK + 4 * hp + h, 0:nk]))
        elif kind == "mlstm":
            out.append((mlstm_rows(m, Z_BQ, h)[:, q], mlstm_rows(m, Z_DQ, h)[:, 0:nk]))
        else:
            out.append((m.qkT[0:HD, T_QRAW + h, q], m.kcT[:, 0:N_CMP]))
    return out


def unit_values(kind, hp):
    if kind == "slc":
        return [(h, Z_VS) for h in range(4)]
    if kind == "win":
        return [(h, Z_VW) for h in range(4)]
    if kind == "dil":
        return [(h, Z_DV + HD * h) for h in range(4)]
    if kind == "mlstm":
        return [(h, Z_CV + HD * h) for h in range(4)]
    return [(2 * h, Z_BV + HD * (2 * hp + h)) for h in range(2)]


def keys_of(kind, t):
    return N_CMP if kind == "cmp" else P * (t + 1)


def scores_of(m, u):
    kind, t, _ = UNITS[u]
    return banks(m, 2 * (u % 2), 2).rearrange("p (h k) -> p h k", h=4)[:, :, 0:keys_of(kind, t)]


def first_tensor(nc, pe, m):
    s = m.s
    mm = nc.tensor.matmul
    for c in range(N_SLOTS):
        pe.sem_inc(m.ring_free[c], 1)
    with pe.Fori(0, DEPTH) as L:
        transpose_pe(nc, pe, m, s["hn"], TILES, s["tr"])
        pe.wait_ge(s["hT"], KC)
        for c in range(N_IN):
            per = 2 if c in (0, 1, 5) else 1
            pe.wait_ge(m.ring_full[c], (L * per + 1) * 16)
            w = m.slot[c][:, 0:KC * ZC].rearrange("p (j n) -> p j n", j=KC)
            for i in range(TILES):
                g = TILES * c + i
                if g >= 4:
                    pe.wait_ge(s["z_act"] if g % 2 == 0 else s["z_dve"], (g - 4) // 2 + 1)
                for j in range(KC):
                    last = mm(m.ps[:, 4 + g % 4, 0:ZC], m.hT[:, j, i * P:(i + 1) * P], w[:, j, :], start=(j == 0), stop=(j == KC - 1))
                last.then_inc(s["z_ps"], 1)
            if c in (0, 1, 5):
                pe.drain().then_inc(m.ring_free[c], 1)
        pe.wait_ge(s["z_act"], N_IN)
        pe.wait_ge(s["z_dve"], N_IN)

        def batch(b):
            if b >= 4:
                pe.wait_ge(s["prep_ev"], b - 3)
            if b == 5:
                pe.wait_ge(s["gates_in"], 1)

        def transposed(b, sources):
            batch(b)
            for k, (src, width) in enumerate(sources):
                for i in range(TILES):
                    at = k * SEQ + i * P
                    dst = banks(m, prep_bank(b), 2)[0:width, at:at + P]
                    last = nc.tensor.transpose(dst, src(i), m.ident[:])
            last.then_inc(s["prep_ps"], 1)

        def zcol(at, width):
            return (lambda i: m.z[:, i, at:at + width]), width

        def rcol(at, width):
            return (lambda i: m.rz[:, i, at:at + width]), width

        transposed(0, [zcol(Z_Q + HD * h, HD) for h in range(NH)])
        transposed(1, [zcol(Z_KC, HD), zcol(Z_VC, HD), zcol(Z_I, NH), zcol(Z_F, NH)])
        batch(2)
        pe.wait_ge(m.params, (L + 1) * 16 * N_PARAMS)
        for c in range(2):
            for i in range(TILES):
                nc.tensor.transpose(m.ps[:, 4, c * SEQ + i * P:c * SEQ + (i + 1) * P], m.z[:, i, Z_U + c * P:Z_U + (c + 1) * P], m.ident[:])
        for w in range(2):
            last = nc.tensor.transpose(m.ps[0:HD, 5, w * CMP_LEN:(w + 1) * CMP_LEN], m.pos[:, w, :], m.ident[0:CMP_LEN, 0:CMP_LEN])
        last.then_inc(s["prep_ps"], 1)
        pe.wait_ge(s["rope"], 1)
        transposed(3, [rcol(R_Q + HD * h, HD) for h in range(NH)])
        transposed(4, [rcol(R_K + HD * h, HD) for h in range(2)])
        for b in range(2):
            transposed(5 + b, [rcol(R_D + HD * (4 * b + h), HD) for h in range(4)])
        for b in range(4):
            transposed(7 + b, [rcol(R_B + 32 * (4 * b + h), 32) for h in range(4)])
        pe.wait_ge(m.heads_w, (L + 1) * 64)
        for b, w in ((11, m.wqz), (12, m.wkz)):
            batch(b)
            if b == 11:
                pe.wait_ge(s["uc"], 1)
            for h in range(NH):
                last = mm(banks(m, prep_bank(b), 2)[0:HD, h * SEQ:(h + 1) * SEQ], w[:, h // 2, h % 2, :], m.ucT[:, h // 2, :], start=True, stop=True)
            last.then_inc(s["prep_ps"], 1)
        batch(13)
        pe.wait_ge(m.ring_full[5], (L * 2 + 2) * 16)
        pe.sem_inc(m.seen, 1)
        pe.wait_ge(s["blocks"], 1)
        cw = m.slot[5][0:HD, :].rearrange("d (w l e) -> d w l e", w=2, l=CMP_LEN)
        for l in range(CMP_LEN):
            mm(m.ps[0:HD, 2, 0:N_CMP], cw[:, 0, l, :], m.blocks[:, 0, l, :], start=(l == 0), stop=(l == CMP_LEN - 1))
        for l in range(CMP_LEN):
            last = mm(m.ps[0:N_CMP, 3, 0:HD], m.blocks[:, 1, l, :], cw[:, 1, l, :], start=(l == 0), stop=(l == CMP_LEN - 1))
        last.then_inc(s["prep_ps"], 1)
        pe.drain().then_inc(m.ring_free[5], 1)
        batch(14)
        pe.wait_ge(s["gate_rows"], 1)
        for h in range(NH):
            last = mm(banks(m, 4, 2)[:, h * SEQ:(h + 1) * SEQ], m.head_rows[:, h, :], m.grow[0:NH, 6, :], start=True, stop=True)
        last.then_inc(s["prep_ps"], 1)
        batch(15)
        for w in range(2):
            for i in range(TILES):
                at = (2 * w + i) * NH
                last = nc.tensor.transpose(m.ps[:, 6, at:at + NH], m.grow[0:NH, 4 + w, i * P:(i + 1) * P], m.ident[0:NH, 0:NH])
        last.then_inc(s["prep_ps"], 1)
        pe.wait_ge(s["prep_ev"], N_PREP)
        pe.wait_ge(s["gate_cols"], 1)

        n = len(UNITS)
        for k in range(n + 2):
            if k < n:
                kind, t, hp = UNITS[k]
                if k >= 2:
                    pe.wait_ge(s["probs"], k - 1)
                view = scores_of(m, k)
                for h, (q, kk) in enumerate(unit_maps(m, kind, t, hp)):
                    last = mm(view[:, h, :], q, kk, start=True, stop=True)
                last.then_inc(s["scores"], 1)
            if 1 <= k <= n:
                u = k - 1
                kind, t, hp = UNITS[u]
                pe.wait_ge(s["probs"], u + 1)
                if u >= 1:
                    pe.wait_ge(s["pt"], u)
                pt = banks(m, 4, 2).rearrange("p (h t q) -> p h t q", h=4, t=2)
                maps = range(4) if kind == "cmp" else [v for v, _ in unit_values(kind, hp)]
                for h in maps:
                    for kt in range(1 if kind == "cmp" else t + 1):
                        if kind == "cmp":
                            last = nc.tensor.transpose(pt[0:N_CMP, h, 0, :], m.pr[:, u % 2, h, 0:N_CMP], m.ident[:])
                        else:
                            last = nc.tensor.transpose(pt[:, h, kt, :], m.pr[:, u % 2, h, kt * P:(kt + 1) * P], m.ident[:])
                last.then_inc(s["pt_ps"], 1)
            if k >= 2:
                u = k - 2
                kind, t, hp = UNITS[u]
                pe.wait_ge(s["pt"], u + 1)
                if u >= 2:
                    pe.wait_ge(s["o_done"], u - 1)
                if kind == "cmp":
                    for h in range(4):
                        last = mm(m.ps[:, 6 + u % 2, h * HD:(h + 1) * HD], m.pt[0:N_CMP, h, 0, :], m.vc[0:N_CMP, :], start=True, stop=True)
                else:
                    for o, (h, col) in enumerate(unit_values(kind, hp)):
                        for kt in range(t + 1):
                            last = mm(m.ps[:, 6 + u % 2, o * HD:(o + 1) * HD], m.pt[:, h, kt, :], m.z[:, kt, col:col + HD], start=(kt == 0), stop=(kt == t))
                last.then_inc(s["pv"], 1)

        transpose_pe(nc, pe, m, s["o_final"], 1, s["tr_o"])
        pe.wait_ge(s["OT"], KC)
        for c in range(2):
            pe.wait_ge(m.ring_full[c], (L * 2 + 2) * 16)
            w = m.slot[c].rearrange("p (j n) -> p j n", j=KC)
            for i in range(TILES):
                for j in range(KC):
                    last = mm(m.ps[:, 4 + 2 * c + i, :], m.hT[:, j, i * P:(i + 1) * P], w[:, j, :], start=(j == 0), stop=(j == KC - 1))
                last.then_inc(s["y_ps"], 1)
            pe.drain().then_inc(m.ring_free[c], 1)

        transpose_pe(nc, pe, m, s["hn_b"], TILES, s["tr_b"])
        pe.wait_ge(s["hT_b"], KC)
        for u in range(N_FU):
            pe.wait_ge(s[f"ffn_full{u % 2}"], 48 * (u // 2 + 1))
            wg = m.ffn[u % 2][:, 0:2048].rearrange("p (j f c) -> p j c f", j=KC, c=2)
            wu = m.ffn[u % 2][:, 2048:4096].rearrange("p (j f c) -> p j c f", j=KC, c=2)
            wd = m.ffn[u % 2][:, 4096:6144].rearrange("p (c n) -> p c n", c=2)
            for c in range(2):
                if u >= 1:
                    pe.wait_ge(s["hid"], 2 * (u - 1) + c + 1)
                for w, at in ((wg, 0), (wu, SEQ)):
                    for j in range(KC):
                        last = mm(m.ps[:, c, at:at + SEQ], w[:, j, c, :], m.hT[:, j, :], start=(j == 0), stop=(j == KC - 1))
                last.then_inc(s["gu"], 1)
            for c in range(2):
                pe.wait_ge(s["hid"], 2 * u + c + 1)
                for i in range(TILES):
                    for n2 in range(2):
                        last = mm(m.ps[:, 4 + 2 * i + n2, :], m.ucT[:, c, i * P:(i + 1) * P], wd[:, c, n2 * 512:(n2 + 1) * 512],
                                  start=(u == 0 and c == 0), stop=(u == N_FU - 1 and c == 1))
                last.then_inc(s["down"], 1)
            pe.drain().then_inc(s[f"ffn_free{u % 2}"], 1)
        for c in (2, 3, 4):
            pe.sem_inc(m.ring_free[c], 1)
        layer_end(nc, pe, m, L)


def first_scalar(nc, act, m):
    s = m.s
    a = nc.scalar.activation
    act.wait_ge(m.x_in, 16 * 2)
    act.wait_ge(m.eps_set, 1)
    act.wait_ge(m.consts_in, 16 * m.n_consts)
    with act.Fori(0, DEPTH) as L:
        norm_act(nc, act, m, s["std"])
        for g in range(0, TILES * N_IN, 2):
            act.wait_ge(s["z_ps"], g + 1)
            a(m.z[:, g % 2, (g // 2) * ZC:(g // 2 + 1) * ZC], m.ps[:, 4 + g % 4, 0:ZC], ACT.Copy).then_inc(s["z_act"], 1)

        def evac(b, out, src):
            act.wait_ge(s["prep_ps"], b + 1)
            return a(out, src, ACT.Copy)

        def qk(b, at, count, rows):
            src = banks(m, prep_bank(b), 2)[0:rows, 0:count * SEQ].rearrange("p (s t) -> p s t", t=SEQ)
            evac(b, m.qkT[0:rows, at:at + count, :], src).then_inc(s["prep_ev"], 1)

        qk(0, T_QRAW, 4, HD)
        qk(1, T_KC, 2, HD)
        evac(2, m.uT[:, :, 3:], m.ps[:, 4, :].rearrange("p (c t) -> p c t", c=2))
        evac(2, m.posT[:], m.ps[0:HD, 5, 0:2 * CMP_LEN].rearrange("p (w l) -> p w l", w=2)).then_inc(s["prep_ev"], 1)
        act.wait_ge(s["gate_abs"], 1)
        a(m.grow[0:NH, 2, :], m.grow[0:NH, 2, :], ACT.Exp, scale=-1.0)
        act.wait_ge(s["lam_in"], 1)
        a(m.lam[:, 2:4], m.lam[:, 0:2], ACT.Exp).then_inc(s["lam_exp"], 1)
        act.drain()
        a(m.grow[0:NH, 3, :], m.grow[0:NH, 2, :], ACT.Ln, bias=m.eps[0:NH, 1:2]).then_inc(s["gate_ln"], 1)
        qk(3, T_QROT, 4, HD)
        qk(4, T_KS, 2, HD)
        qk(5, T_DQ, 4, HD)
        qk(6, T_DK, 4, HD)
        for b in range(4):
            qk(7 + b, T_BQ + 4 * b, 4, 32)
        act.wait_ge(s["conv"], 1)
        a(m.ucT[:], m.ucT[:], ACT.Silu).then_inc(s["uc"], 1)
        act.wait_ge(s["z_dve"], N_IN)
        a(m.gates[:], m.z[:, :, Z_G:Z_G + 12], ACT.Sigmoid)
        a(m.z[:, :, Z_O:Z_O + GW], m.z[:, :, Z_O:Z_O + GW], ACT.Sigmoid).then_inc(s["small_ready"], 1)
        for b, col in ((11, Z_BQ), (12, Z_DQ)):
            evac(b, m.z[0:HD, :, col:col + 2 * SEQ], banks(m, prep_bank(b), 2)[0:HD, :].rearrange("p (i c) -> p i c", i=TILES)).then_inc(s["prep_ev"], 1)
        evac(13, m.kcT[:, 0:N_CMP], m.ps[0:HD, 2, 0:N_CMP])
        evac(13, m.vc[0:N_CMP, :], m.ps[0:N_CMP, 3, 0:HD]).then_inc(s["prep_ev"], 1)
        evac(14, m.rb.rearrange("p h k -> p (h k)"), banks(m, 4, 2)).then_inc(s["prep_ev"], 1)
        act.wait_ge(s["gate_cols"], 1)
        a(m.em, m.ps[:, 6, 8:16].rearrange("p (i h) -> p i h", i=TILES), ACT.Exp, scale=-1.0).then_inc(s["prep_ev"], 1)

        n = len(UNITS)
        for k in range(n + 1):
            if k < n:
                kind, t, hp = UNITS[k]
                nk = keys_of(kind, t)
                act.wait_ge(s["masked"], k + 1)
                if k >= 2:
                    act.wait_ge(s["pt_ps"], k - 1)
                scale = 1.0 if kind == "mlstm" else 32 ** -0.5 if kind == "diff" else HD ** -0.5
                for h in range(4):
                    bias = m.nM[:, t, h:h + 1] if kind == "mlstm" else m.nmx[k % 2][:, h:h + 1]
                    last = a(m.pr[:, k % 2, h, 0:nk], m.sm[:, k % 2, h, 0:nk], ACT.Exp, bias=bias, scale=scale,
                             accum_out=m.zs[k % 2][:, h:h + 1])
                act.drain().then_inc(s["exps"], 1)
            if k >= 1:
                u = k - 1
                kind, t, hp = UNITS[u]
                act.wait_ge(s["pt_ps"], u + 1)
                if u >= 1:
                    act.wait_ge(s["pv"], u)
                pt = banks(m, 4, 2).rearrange("p (h t q) -> p h t q", h=4, t=2)
                if kind == "cmp":
                    last = a(m.pt[0:N_CMP, :, 0, :], pt[0:N_CMP, :, 0, :], ACT.Copy)
                elif kind == "diff":
                    for h in (0, 2):
                        last = a(m.pt[:, h, 0:t + 1, :], pt[:, h, 0:t + 1, :], ACT.Copy)
                else:
                    last = a(m.pt[:, :, 0:t + 1, :], pt[:, :, 0:t + 1, :], ACT.Copy)
                last.then_inc(s["pt"], 1)
        act.wait_ge(s["ss"], 1)
        a(m.sstd, m.sso, ACT.Sqrt, scale=1.0 / HD, bias=m.eps[:, 0:1]).then_inc(s["o_std"], 1)
        act.wait_ge(s["x_mid"], 1)
        norm_act(nc, act, m, s["std_b"])
        for g in range(2 * N_FU):
            act.wait_ge(s["gu"], g + 1)
            if g >= 2:
                act.wait_ge(s["hid"], g - 1)
            a(m.uT[:, g % 2, 0:SEQ], m.ps[:, g % 2, 0:SEQ], ACT.Silu).then_inc(s["silu"], 1)
        layer_end(nc, act, m, L)


def first_vector(nc, dve, m):
    s = m.s
    v = nc.vector
    tt, ts, stt = v.tensor_tensor, v.tensor_scalar, v.scalar_tensor_tensor
    dve.wait_ge(m.x_in, 16 * 2)
    v.memset(m.eps[:, 0:1], EPS)
    v.memset(m.eps[:, 1:2], 1.0).then_inc(m.eps_set, 1)
    dve.wait_ge(m.consts_in, 16 * m.n_consts)
    with dve.Fori(0, DEPTH) as L:
        norm_dve(nc, dve, m, s["std"], s["hn"])
        dve.wait_ge(m.params, (L + 1) * 16 * N_PARAMS)
        evacuate_dve(nc, dve, m, m.g_mix, s["tr"], s["hT"])
        for g in range(1, TILES * N_IN, 2):
            dve.wait_ge(s["z_ps"], g + 1)
            v.tensor_copy(m.z[:, 1, (g // 2) * ZC:(g // 2 + 1) * ZC], m.ps[:, 4 + g % 4, 0:ZC]).then_inc(s["z_dve"], 1)
        dve.wait_ge(s["z_act"], N_IN)
        dve.drain()
        for i in range(TILES):
            regions = [(m.z[:, i, Z_Q:Z_Q + GW].rearrange("p (h d) -> p h d", d=HD), R_Q, 4, HD),
                       (m.z[:, i, Z_KS:Z_KS + 256].rearrange("p (h d) -> p h d", d=128)[:, :, 0:HD], R_K, 2, HD),
                       (m.z[:, i, Z_DQ:Z_DQ + 512].rearrange("p (h d) -> p h d", d=HD), R_D, 8, HD),
                       (m.z[:, i, Z_BQ:Z_BQ + 512].rearrange("p (h d) -> p h d", d=32), R_B, 16, 32)]
            if i > 0:
                dve.drain()
            for src, at, n, dim in regions:
                half = dim // 2
                cos, sin = (m.cos64, m.sin64) if dim == HD else (m.cos32, m.sin32)
                out = m.rz[:, i, at:at + n * dim].rearrange("p (h d) -> p h d", d=dim)
                tmp = m.tmp[:, at:at + n * dim].rearrange("p (h d) -> p h d", d=dim)
                tt(out, src, bcast(cos[:, i, :].unsqueeze(1), [P, n, dim]), ALU.mult)
                tt(tmp[:, :, 0:half], src[:, :, half:], bcast(sin[:, i, 0:half].unsqueeze(1), [P, n, half]), ALU.mult)
                tt(tmp[:, :, half:], src[:, :, 0:half], bcast(sin[:, i, half:].unsqueeze(1), [P, n, half]), ALU.mult)
            dve.drain()
            last = tt(m.rz[:, i, :], m.rz[:, i, :], m.tmp, ALU.add)
        last.then_inc(s["rope"], 1)
        g = m.grow
        dve.wait_ge(s["prep_ps"], 2)
        ts(g[0:NH, 0, :], m.ps[0:NH, 3, 0:SEQ], m.gate_b[:, 0:1], None, ALU.add)
        ts(g[0:NH, 1, :], m.ps[0:NH, 3, SEQ:2 * SEQ], m.gate_b[:, 1:2], None, ALU.add).then_inc(s["gates_in"], 1)
        dve.drain()
        stt(g[0:NH, 2, :], g[0:NH, 1, :], -1.0, g[0:NH, 1, :], ALU.mult, ALU.max).then_inc(s["gate_abs"], 1)
        lv = m.tmp[:, 0:64].rearrange("p (w c) -> p w c", w=2)
        pairs = m.lamv[:].rearrange("p (w c) d -> p w c d", w=2)
        dve.drain()
        tt(lv, pairs[:, :, 0, :], pairs[:, :, 1, :], ALU.mult)
        dve.drain()
        v.reduce_sum(m.lam[:, 0:2], lv, axis=AX).then_inc(s["lam_in"], 1)
        dve.wait_ge(s["prep_ev"], 3)
        for c in range(2):
            ts(m.ucT[:, c, :], m.uT[:, c, 0:SEQ], m.conv_w[:, c, 0:1], m.conv_b[:, c:c + 1], ALU.mult, ALU.add)
        for k in range(1, 4):
            dve.drain()
            for c in range(2):
                last = stt(m.ucT[:, c, :], m.uT[:, c, k:k + SEQ], m.conv_w[:, c, k:k + 1], m.ucT[:, c, :], ALU.mult, ALU.add)
        last.then_inc(s["conv"], 1)
        for w in range(2):
            for lh in range(2):
                src = m.qkT[0:HD, T_KC + w, 16 * lh:16 * lh + 240].rearrange("d (n l) -> d l n", l=16)
                last = tt(m.blocks[:, w, 16 * lh:16 * lh + 16, :], src,
                          bcast(m.posT[:, w, 16 * lh:16 * lh + 16].unsqueeze(2), [HD, 16, N_CMP]), ALU.add)
        last.then_inc(s["blocks"], 1)
        dve.wait_ge(s["lam_exp"], 1)
        tt(m.lam[:, 4:5], m.lam[:, 3:4], m.lam[:, 2:3], ALU.subtract)
        v.memset(g[0:NH, 7, :], 0.0)
        dve.wait_ge(s["gate_ln"], 1)
        stt(g[0:NH, 3, :], g[0:NH, 1, :], 0.0, g[0:NH, 3, :], ALU.min, ALU.subtract)
        dve.drain()
        tt(m.lam[:, 5:6], m.lam[:, 4:5], m.lam_init[:, 0:1], ALU.subtract)
        v.tensor_tensor_scan(out=g[0:NH, 2, :], data0=g[0:NH, 3, :], data1=g[0:NH, 7, :], initial=0.0, op0=ALU.add, op1=ALU.add)
        dve.drain()
        tt(g[0:NH, 6, :], g[0:NH, 0, :], g[0:NH, 2, :], ALU.subtract)
        dve.drain()
        v.tensor_tensor_scan(out=g[0:NH, 4, :], data0=g[0:NH, 6, :], data1=g[0:NH, 6, :], initial=0.0, op0=ALU.max, op1=ALU.max)
        dve.drain()
        tt(g[0:NH, 5, :], g[0:NH, 4, :], g[0:NH, 2, :], ALU.add).then_inc(s["gate_rows"], 1)
        dve.wait_ge(s["prep_ps"], N_PREP)
        ts(m.nM, m.ps[:, 6, 0:8].rearrange("p (i h) -> p i h", i=TILES), -1.0, None, ALU.mult).then_inc(s["gate_cols"], 1)
        dve.wait_ge(s["prep_ev"], N_PREP)
        dve.wait_ge(s["small_ready"], 1)

        n = len(UNITS)
        for k in range(n + 3):
            if k < n:
                kind, t, hp = UNITS[k]
                nk = keys_of(kind, t)
                b = k % 2
                dve.wait_ge(s["scores"], k + 1)
                if k >= 2:
                    dve.wait_ge(s["exps"], k - 1)
                mask = {"cmp": m.cmp_mask, "dil": m.dil_mask}.get(kind, m.causal)[:, t, 0:nk]
                sm = m.sm[:, b, :, 0:nk]
                src = m.rb[:, :, 0:nk] if kind == "mlstm" else scores_of(m, k)
                last = tt(sm, src, bcast(mask.unsqueeze(1), [P, 4, nk]), ALU.add)
                if kind != "mlstm":
                    dve.drain()
                    v.reduce_max(m.mx[b], sm, axis=AX)
                    dve.drain()
                    last = ts(m.nmx[b], m.mx[b], -(32 ** -0.5 if kind == "diff" else HD ** -0.5), None, ALU.mult)
                last.then_inc(s["masked"], 1)
            if 1 <= k <= n:
                u = k - 1
                kind, t, hp = UNITS[u]
                nk = keys_of(kind, t)
                b = u % 2
                pr, zs, rs = m.pr[:, b, :, 0:nk], m.zs[b], m.rs[b]
                dve.wait_ge(s["exps"], u + 1)
                if kind in ("slc", "win"):
                    v.reciprocal(rs, zs)
                    dve.drain()
                    br = 1 if kind == "slc" else 2
                    last = tt(rs, rs, m.gates[:, t, 4 * br:4 * br + 4], ALU.mult)
                elif kind in ("dil", "cmp"):
                    w = (m.dil_counts if kind == "dil" else m.cmp_seen)[:, t, 0:nk]
                    tt(pr, pr, bcast(w.unsqueeze(1), [P, 4, nk]), ALU.mult)
                    dve.drain()
                    v.reduce_sum(zs, pr, axis=AX)
                    dve.drain()
                    if kind == "cmp":
                        ts(zs, zs, 1e-30, None, ALU.max)
                        dve.drain()
                    last = v.reciprocal(rs, zs)
                    if kind == "cmp":
                        dve.drain()
                        last = tt(rs, rs, m.gates[:, t, 0:4], ALU.mult)
                elif kind == "diff":
                    v.reciprocal(rs, zs)
                    dve.drain()
                    odd = rs.rearrange("p (h c) -> p h c", c=2)[:, :, 1]
                    ts(odd, odd, m.lam[:, 5:6], None, ALU.mult)
                    for h in (0, 2):
                        ts(pr[:, h, :], pr[:, h, :], rs[:, h:h + 1], None, ALU.mult)
                    dve.drain()
                    for h in (0, 2):
                        last = stt(pr[:, h, :], pr[:, h + 1, :], rs[:, h + 1:h + 2], pr[:, h, :], ALU.mult, ALU.add)
                else:
                    for h in range(4):
                        stt(pr[:, h, :], scores_of(m, u)[:, h, :], HD ** -0.5, pr[:, h, :], ALU.mult, ALU.mult)
                    dve.drain()
                    v.reduce_sum(zs, pr, axis=AX)
                    dve.drain()
                    stt(zs, zs, -1.0, zs, ALU.mult, ALU.max)
                    dve.drain()
                    tt(zs, zs, m.em[:, t, :], ALU.max)
                    dve.drain()
                    last = v.reciprocal(rs, zs)
                last.then_inc(s["probs"], 1)
            if 2 <= k <= n + 1:
                u = k - 2
                kind, t, hp = UNITS[u]
                b = u % 2
                dve.wait_ge(s["pv"], u + 1)
                src = m.ps[:, 6 + b, 0:GW]
                src4 = src.rearrange("p (h d) -> p h d", d=HD)
                scale = bcast(m.rs[b].unsqueeze(2), [P, 4, HD])
                cols = {"slc": 0, "win": 0, "cmp": 0, "dil": 768, "mlstm": 512, "diff": 256 + 128 * hp}[kind]
                if kind == "diff":
                    last = v.tensor_copy(m.O[:, t, cols:cols + 128], src[:, 0:128])
                else:
                    o4 = m.O[:, t, cols:cols + GW].rearrange("p (h d) -> p h d", d=HD)
                    if kind in ("win", "cmp"):
                        tmp = m.ucT[:, 0, :].rearrange("p (h d) -> p h d", d=HD)
                        dve.drain()
                        tt(tmp, src4, scale, ALU.mult)
                        dve.drain()
                        last = tt(o4, o4, tmp, ALU.add)
                    else:
                        last = tt(o4, src4, scale, ALU.mult)
                last.then_inc(s["o_done"], 1)
        sub = m.O[:, :, GW:3 * GW]
        sq = m.hT[:].rearrange("p j t -> p (j t)")[:, 0:4 * GW].rearrange("p (i c) -> p i c", i=TILES)
        dve.drain()
        tt(sq, sub, sub, ALU.mult)
        dve.drain()
        v.reduce_sum(m.sso, sq.rearrange("p i (h d) -> p i h d", d=HD), axis=AX).then_inc(s["ss"], 1)
        dve.wait_ge(s["o_std"], 1)
        v.reciprocal(m.srec, m.sstd)
        dve.drain()
        ts(m.srec[:, :, 0:4], m.srec[:, :, 0:4], m.lam_init[:, 1:2], None, ALU.mult)
        dve.drain()
        for i in range(TILES):
            tt(sub[:, i, :].rearrange("p (h d) -> p h d", d=HD), sub[:, i, :].rearrange("p (h d) -> p h d", d=HD),
               bcast(m.srec[:, i, :].unsqueeze(2), [P, 8, HD]), ALU.mult)
        dve.drain()
        tt(sub, sub, bcast(m.g_sub[:].unsqueeze(1), [P, TILES, 2 * GW]), ALU.mult)
        dve.drain()
        tt(m.O[:, :, 2 * GW:3 * GW], m.O[:, :, 2 * GW:3 * GW], m.z[:, :, Z_O:Z_O + GW], ALU.mult).then_inc(s["o_final"], 1)
        evacuate_dve(nc, dve, m, None, s["tr_o"], s["OT"])
        for c in range(2):
            for i in range(TILES):
                dve.wait_ge(s["y_ps"], 2 * c + i + 1)
                part = m.x[:, i, c * 512:(c + 1) * 512]
                last = tt(part, m.ps[:, 4 + 2 * c + i, :], part, ALU.add)
        last.then_inc(s["x_mid"], 1)
        norm_dve(nc, dve, m, s["std_b"], s["hn_b"])
        evacuate_dve(nc, dve, m, m.g_ffn, s["tr_b"], s["hT_b"])
        for g2 in range(2 * N_FU):
            dve.wait_ge(s["silu"], g2 + 1)
            if g2 >= 2:
                dve.wait_ge(s["down"], g2 - 1)
            tt(m.ucT[:, g2 % 2, :], m.ps[:, g2 % 2, SEQ:2 * SEQ], m.uT[:, g2 % 2, 0:SEQ], ALU.mult).then_inc(s["hid"], 1)
        dve.wait_ge(s["down"], 2 * N_FU)
        for i in range(TILES):
            for c in range(2):
                part = m.x[:, i, c * 512:(c + 1) * 512]
                tt(part, m.ps[:, 4 + 2 * i + c, :], part, ALU.add)
        v.memset(m.uT[:, :, 0:3], 0.0)
        dve.drain()
        layer_end_leader(nc, dve, m)



T = 64
N_EXP, N_GRP, PER_GRP = 32, 4, 8
N_PAIRS = N_EXP // 2
K_A, K_B = 31, 3
PAD = K_A - 1
V_DW, V_BDW, V_LG, V_LB, V_BA, V_BG, V_DWB, N_V = 0, 31, 32, 33, 34, 35, 36, 39

SECOND_SEMS = ["std2", "hn2", "vec_ps", "vec", "c_act", "c_wide", "ada_ps", "mod", "x_new", "h_ready", "tr2", "hT2", "ag", "sig", "glu",
               "bank_free", "v_ready", "back_ps", "ln_var", "ln_std", "ln_x", "tr3", "silu_T", "y2", "var3", "std3",
               "router_ps", "gmaxed", "gexp", "emaxed", "eexp", "routed", "pos_ps", "rounds", "zeros",
               "gsel", "gw", "xg_ps", "xg", "comb", "acc", "esilu", "ehid", "hidT_ps", "hidT", "gwt_ps", "gwt", "ye", "arrive2"]


def ring_plan():
    plan = []

    def add(what, count, first):
        for k in range(count):
            plan.append((what, k, (first + k) % N_SLOTS))
    add("ada0", 6, 0)
    add("a_in", 4, 0)
    add("a_out", 2, 4)
    add("ada1", 6, 0)
    add("moe0", 6, 0)
    add("ada2", 6, 0)
    add("b_in", 6, 0)
    add("b_out", 2, 0)
    add("ada3", 6, 2)
    add("moe1", 6, 0)
    return plan


def ring_counts():
    loads = [4 if c in (0, 1, 5) else 2 for c in range(N_SLOTS)]
    frees = list(loads)
    out = {}
    for what, k, slot in ring_plan():
        frees_needed = frees[slot] + 1
        frees[slot] += 1
        if not what.startswith("moe"):
            loads[slot] += 1
        out[what, k] = (slot, frees_needed, 16 * loads[slot])
    return out


RING = ring_counts()


def place_second(nc, m):
    sb = nc.alloc_sbuf_tensor
    m.before = sb("before", [P, P], F32)
    m.ones = sb("ones", [P, P], F32)
    m.iota64 = sb("iota64", [P, T], F32)
    m.rounds_i = sb("rounds_i", [1, 1], mybir.dt.int32)
    m.stat = sb("stat", [P, 64], F32)
    m.cur = sb("cur", [P, 2, TILES, 2], F32)
    q = m.qkT[:].rearrange("p s t -> p (s t)")
    m.mod = q[:, 0:3072].rearrange("p (k d) -> p k d", k=3)
    m.upad = q[:, 3072:3072 + KC * (SEQ + PAD)].rearrange("p (j t) -> p j t", j=KC)
    m.cvT = q[:, 5360:7408].rearrange("p (j t) -> p j t", j=KC)
    m.sg2 = q[:, 7408:7920].rearrange("p (b t) -> p b t", b=2)
    m.xg = q[:, 3072:4096].rearrange("p (j s) -> p j s", j=KC)
    m.G = q[:, 4096:4352].rearrange("p (g s) -> p g s", s=T)
    m.Gw = q[:, 4352:4608].rearrange("p (g s) -> p g s", s=T)
    m.GwT = q[:, 4608:4864].rearrange("p (i t) -> p i t", i=TILES)
    m.ye = q[:, 4864:5888]
    m.hid2 = q[:, 5888:6400]
    m.sgx = q[:, 6400:6912]
    m.hidT = m.hT[:].rearrange("p j t -> p (j t)")[:, 0:512].rearrange("p (c s) -> p c s", c=4)
    m.yacc = q[:, 6912:8960].rearrange("p (i d) -> p i d", i=TILES)
    z = m.z[:].rearrange("p i c -> p (i c)")
    m.rows = [z[:, k * D:(k + 1) * D] for k in range(3)]
    m.prm = z[0:N_V, 3072:4096]
    m.vec = z[:, 4096:4096 + KC * N_V].rearrange("p (j v) -> p j v", j=KC)
    m.cw = z[:, 4408:4408 + KC * P].rearrange("p (j c) -> p j c", j=KC)
    m.cc = z[:, 5432:5432 + KC]
    m.r_w = z[:, 5440:5440 + KC * 36].rearrange("p (j e) -> p j e", j=KC)
    m.r_b = z[:, 5728:5764]
    r = m.rows[2]
    def tile(at, n):
        return r[:, at:at + TILES * n].rearrange("p (i e) -> p i e", i=TILES)
    m.lg, m.geq, m.gcs, m.gfirst, m.gex = tile(0, 36), tile(72, 4), tile(80, 4), tile(88, 4), tile(96, 4)
    m.lm, m.eq, m.cs, m.first1, m.first2 = tile(112, 32), tile(176, 32), tile(240, 32), tile(304, 32), tile(368, 32)
    m.zero32 = r[:, 432:464]
    m.A, m.W, m.posm = tile(496, 32), tile(560, 32), tile(624, 32)
    m.w1t = tile(688, 32)


def second_sems(nc, m):
    sem = nc.alloc_semaphore
    m.t = {name: sem(name) for name in SECOND_SEMS}
    m.second_range = range(m.t["std2"].num, m.t["arrive2"].num + 1)
    assert len(m.second_range) == len(SECOND_SEMS)
    m.x_out = sem("x_out")
    m.rounds_set = [sem(f"rounds_set{l}") for l in range(DEPTH)]
    m.rel2, m.rows_in = sem("rel2"), sem("rows_in")
    m.e_full = [[sem(f"e_full{l}_{c}") for c in range(6)] for l in range(DEPTH)]
    m.e_used = [[sem(f"e_used{l}_{c}") for c in range(3)] for l in range(DEPTH)]


def phase_end(eng, m, k):
    eng.drain().then_inc(m.t["arrive2"], 1)
    eng.wait_ge(m.rel2, k)


def phase_end_leader(dve, m):
    dve.wait_ge(m.t["arrive2"], 3)
    dve.sem_clear(m.second_range)
    dve.sem_inc(m.rel2, 1)


ROW_LOADS = [3, 9, 7, 3, 7]


def rows_count(phase):
    return 16 * sum(ROW_LOADS[:phase + 1])


def second_pool(nc, pool, m, a):
    def load(dst, src):
        pool.dma_start(dst, src).then_inc(m.rows_in, 16)

    def wide(dst, src):
        load(dst, src.partition_broadcast(P))
    wide(m.rows[0], a["norm_final"])
    load(m.cc, a["c_2"][0].rearrange("(p j) -> p j", j=KC))
    load(m.prm[V_DWB:N_V, :], a["b_w_dw_2"][0])
    phase_end(pool, m, 1)
    load(m.prm[V_DW:V_DW + K_A, :], a["a_w_dw_2"][0])
    load(m.prm[V_BDW:V_BDW + 1, :], a["a_b_dw_2"])
    load(m.prm[V_LG:V_LG + 1, :], a["a_ln_g_2"])
    load(m.prm[V_LB:V_LB + 1, :], a["a_ln_b_2"])
    load(m.prm[V_BA:V_BA + 2, :], a["a_b_in_2"][0].rearrange("(h d) -> h d", h=2))
    wide(m.mod.rearrange("p k d -> p (k d)"), a["ada_b_2"][0][0:3 * D])
    wide(m.rows[0], a["a_b_out_2"][0])
    wide(m.rows[1], a["mix_ln_g_2"][0])
    wide(m.rows[2], a["mix_ln_b_2"][0])
    phase_end(pool, m, 2)
    for l in range(DEPTH):
        load(m.r_w[:, :, 0:N_GRP], a["r_w_group_2"][l].rearrange("(p j) e -> p j e", j=KC))
        load(m.r_w[:, :, N_GRP:], a["r_w_expert_2"][l].rearrange("(p j) e -> p j e", j=KC))
        wide(m.r_b[:, 0:N_GRP], a["r_b_group_2"][l])
        wide(m.r_b[:, N_GRP:], a["r_b_expert_2"][l])
        wide(m.mod.rearrange("p k d -> p (k d)"), a["ada_b_2"][l][3 * D:6 * D])
        nc.gpsimd.memset(m.yacc, 0.0)
        nc.gpsimd.memset(m.ye, 0.0)
        nc.gpsimd.memset(m.GwT, 0.0)
        pool.drain().then_inc(m.t["zeros"], 1)
        wide(m.rows[0], a["ffn_ln_g_2"][l])
        wide(m.rows[1], a["ffn_ln_b_2"][l])
        phase_end(pool, m, 3 + 2 * l)
        if l == 0:
            wide(m.mod.rearrange("p k d -> p (k d)"), a["ada_b_2"][1][0:3 * D])
            wide(m.rows[1], a["mix_ln_g_2"][1])
            wide(m.rows[2], a["mix_ln_b_2"][1])
            phase_end(pool, m, 4)


def expert_load(sp, m, a, l, e, c):
    src = [a["e_w_gate_2"], a["e_w_up_2"], a["e_w_down_2"]][c % 3][l]
    return src[e].rearrange("(p j) n -> p (j n)", p=P)


def second_sync(nc, sp, m, a, out):
    def load(what, k, src, three=True):
        slot, frees, _ = RING[what, k]
        sp.wait_ge(m.ring_free[slot], frees)
        dst = m.slot[slot].rearrange("p (j n) -> p j n", j=KC) if three else m.slot[slot]
        sp.dma_start(dst, src).then_inc(m.ring_full[slot], 16)

    def ada(g):
        w = a["ada_w_2"][g // 2].rearrange("(p j) n -> p j n", j=KC)
        for k in range(6):
            at = (g % 2) * 3 * D + k * 512
            load(f"ada{g}", k, w[:, :, at:at + 512])

    def halves(what, w, order, rows):
        w = w.rearrange(rows, j=KC)
        for k, at in enumerate(order):
            load(what, k, w[:, :, at:at + 512])

    def experts(l):
        for c in range(6):
            slot, frees, _ = RING[f"moe{l}", c]
            sp.wait_ge(m.ring_free[slot], frees)
        full = m.e_full[l]

        def pairs(r):
            with sp.Fori(0, N_PAIRS) as p:
                it = r * N_PAIRS + p
                for c in range(3):
                    sp.wait_ge(m.e_used[l][c], it + 1)
                    for x in range(2):
                        sp.dma_start(m.slot[2 * c + x], expert_load(sp, m, a, l, p * 2 + x, c)).then_inc(full[2 * c + x], 16)
        pairs(0)
        sp.wait_ge(m.rounds_set[l], 1)
        rounds = sp.value_load(m.rounds_i[0:1, 0:1], min_val=1, max_val=4)
        with sp.If(rounds > 1):
            with sp.Fori(1, rounds) as r:
                pairs(r)

    ada(0)
    halves("a_in", a["a_w_in_2"][0], (0, D, 512, D + 512), "(p j) n -> p j n")
    halves("a_out", a["a_w_out_2"][0], (0, 512), "(j p) n -> p j n")
    ada(1)
    experts(0)
    ada(2)
    halves("b_in", a["b_w_in_2"][0], (0, D, 2 * D, 512, D + 512, 2 * D + 512), "(p j) n -> p j n")
    halves("b_out", a["b_w_out_2"][0], (0, 512), "(j p) n -> p j n")
    ada(3)
    experts(1)
    for i in range(TILES):
        sp.wait_ge(m.x_out, 1)
        sp.dma_start(out[0, i * P:(i + 1) * P, :], m.x[:, i, :]).then_inc(m.stored, 16)
    sp.wait_ge(m.stored, 16 * TILES)


def second_tensor(nc, pe, m):
    t = m.t
    mm = nc.tensor.matmul

    def full(what, k):
        slot, _, count = RING[what, k]
        pe.wait_ge(m.ring_full[slot], count)
        return slot, m.slot[slot].rearrange("p (j n) -> p j n", j=KC)

    def free(slot):
        pe.drain().then_inc(m.ring_free[slot], 1)

    def ada(g):
        for k in range(6):
            slot, w = full(f"ada{g}", k)
            for j in range(KC):
                last = mm(m.ps[:, k, :], m.cw[:, j, :], w[:, j, :], start=(j == 0), stop=(j == KC - 1))
            last.then_inc(t["ada_ps"], 1)
            free(slot)

    phase_end(pe, m, 1)

    for l in range(DEPTH):
        if l == 0:
            pe.wait_ge(m.rows_in, rows_count(1))
            for j in range(KC):
                last = nc.tensor.transpose(m.ps[:, 7, j * N_V:(j + 1) * N_V], m.prm[:, j * P:(j + 1) * P], m.ident[0:N_V, 0:N_V])
            last.then_inc(t["vec_ps"], 1)
        ada(2 * l)
        pe.wait_ge(t["mod"], 6)
        transpose_pe(nc, pe, m, t["hn2"], TILES, t["tr2"])
        pe.wait_ge(t["hT2"], KC)
        if l == 0:
            pe.wait_ge(t["vec"], 1)
            w = [full("a_in", k)[1] for k in range(2)]
            for c in range(KC):
                if c == 4:
                    free(0)
                    free(1)
                    w = [full("a_in", k)[1] for k in (2, 3)]
                if c >= 2:
                    pe.wait_ge(t["glu"], c - 1)
                at = (c % 4) * P
                for half in range(2):
                    for j in range(KC):
                        last = mm(m.ps[:, c % 2, half * SEQ:(half + 1) * SEQ], w[half][:, j, at:at + P], m.hT[:, j, :], start=(j == 0), stop=(j == KC - 1))
                last.then_inc(t["ag"], 1)
            free(2)
            free(3)
            pe.wait_ge(t["v_ready"], KC)
            for i in range(TILES):
                for c in range(KC):
                    dst = m.ps[:, 4 + 2 * i + c // 4, (c % 4) * P:(c % 4 + 1) * P]
                    last = nc.tensor.transpose(dst, m.cvT[:, c, i * P:(i + 1) * P], m.ident[:])
                last.then_inc(t["back_ps"], 1)
            pe.wait_ge(t["ln_x"], 1)
            for c in range(KC):
                for i in range(TILES):
                    last = nc.tensor.transpose(m.ps[:, c // 2, (c % 2) * SEQ + i * P:(c % 2) * SEQ + (i + 1) * P], m.O[:, i, c * P:(c + 1) * P], m.ident[:])
                last.then_inc(t["tr3"], 1)
            pe.wait_ge(t["silu_T"], KC)
            vT, what = m.hT, "a_out"
        else:
            for c in range(KC):
                if c % 4 == 0:
                    w = [full("b_in", 3 * (c // 4) + k)[1] for k in range(3)]
                if c >= 2:
                    pe.wait_ge(t["v_ready"], c - 1)
                at = (c % 4) * P
                for half, bank in ((1, c % 2), (2, c % 2), (0, 2 + c % 2)):
                    dst = m.ps[:, bank, 0:SEQ] if half != 2 else m.ps[:, bank, SEQ:2 * SEQ]
                    for j in range(KC):
                        last = mm(dst, w[half][:, j, at:at + P], m.hT[:, j, :], start=(j == 0), stop=(j == KC - 1))
                last.then_inc(t["ag"], 1)
                if c % 4 == 3:
                    for k in range(3):
                        free(3 * (c // 4) + k)
            pe.wait_ge(t["v_ready"], KC)
            vT, what = m.cvT, "b_out"
        for n in range(2):
            slot, w = full(what, n)
            for i in range(TILES):
                for j in range(KC):
                    last = mm(m.ps[:, 4 + 2 * i + n, :], vT[:, j, i * P:(i + 1) * P], w[:, j, :], start=(j == 0), stop=(j == KC - 1))
            free(slot)
        pe.drain().then_inc(t["y2"], 1)
        phase_end(pe, m, 2 + 2 * l)

        ada(2 * l + 1)
        for c in range(3):
            pe.sem_inc(m.e_used[l][c], 1)
        pe.wait_ge(t["mod"], 6)
        transpose_pe(nc, pe, m, t["hn2"], TILES, t["tr2"])
        pe.wait_ge(m.rows_in, rows_count(2 + 2 * l))
        pe.wait_ge(t["hT2"], KC)
        for i in range(TILES):
            for j in range(KC):
                last = mm(m.ps[:, 6, i * 36:(i + 1) * 36], m.hT[:, j, i * P:(i + 1) * P], m.r_w[:, j, :], start=(j == 0), stop=(j == KC - 1))
        last.then_inc(t["router_ps"], 1)
        pe.wait_ge(t["routed"], 1)
        mm(m.ps[:, 7, 0:32], m.before[:], m.A[:, 0, :], start=True, stop=True)
        mm(m.ps[:, 7, 32:64], m.ones[:], m.A[:, 0, :], start=True, stop=False)
        mm(m.ps[:, 7, 32:64], m.before[:], m.A[:, 1, :], start=False, stop=True)
        mm(m.ps[:, 7, 64:96], m.ones[:], m.A[:, 0, :], start=True, stop=False)
        mm(m.ps[:, 7, 64:96], m.ones[:], m.A[:, 1, :], start=False, stop=True).then_inc(t["pos_ps"], 1)
        pe.wait_ge(t["rounds"], 1)
        pe.wait_ge(t["zeros"], 1)
        rounds = pe.value_load(m.rounds_i[0:1, 0:1], min_val=1, max_val=4)
        ef = m.e_full[l]

        def combine(i):
            for n in range(2):
                last = mm(m.ps[:, 6 + n, :], m.GwT[:, i, :], m.ye[:, n * 512:(n + 1) * 512], start=True, stop=True)
            last.then_inc(t["comb"], 1)

        with pe.Fori(0, rounds) as r:
            with pe.Fori(0, N_PAIRS) as p:
                it = r * N_PAIRS + p

                def product(c, out, count, operand):
                    for x in range(2):
                        pe.wait_ge(ef[2 * c + x], it * 16 + 16)
                        if x == 0:
                            pe.sem_inc(m.seen, 1)
                    halves = 2 if c == 2 else 1
                    w = [m.slot[2 * c + x].rearrange("p (j n) -> p j n", j=count) for x in range(2)]
                    for n in range(halves):
                        for j in range(count):
                            for x in range(2):
                                last = mm(m.ps[x * T:(x + 1) * T, out + n, :], operand[:, j, x * T:(x + 1) * T], w[x][:, j, n * 512:(n + 1) * 512],
                                          start=(j == 0), stop=(j == count - 1))
                    last.then_inc(m.e_used[l][c], 1)

                pe.wait_ge(t["gsel"], it + 1)
                for j in range(KC):
                    for i in range(TILES):
                        hN = m.O[:, i, :].rearrange("t (p j) -> t j p", j=KC)[:, j, :]
                        g = m.G[:, 2 * i:2 * i + 2, :].rearrange("p x s -> p (x s)")
                        last = mm(m.ps[:, j // 4, (j % 4) * P:(j % 4 + 1) * P], hN, g, start=(i == 0), stop=(i == 1))
                last.then_inc(t["xg_ps"], 1)
                pe.wait_ge(t["ye"], it + 1)
                pe.sem_inc(m.seen, 1)
                pe.wait_ge(t["acc"], it * 2 + 1)
                combine(0)
                pe.wait_ge(t["xg"], it + 1)
                pe.sem_inc(m.seen, 1)
                product(0, 2, KC, m.xg)
                product(1, 3, KC, m.xg)
                pe.wait_ge(t["acc"], it * 2 + 2)
                combine(1)
                pe.wait_ge(t["ehid"], it + 1)
                for c in range(4):
                    src = m.hid2.rearrange("s (p c) -> s c p", c=4)[:, c, :]
                    last = nc.tensor.transpose(m.ps[:, 1, c * P:(c + 1) * P], src, m.ident[:])
                last.then_inc(t["hidT_ps"], 1)
                pe.wait_ge(t["gw"], it + 1)
                for i in range(TILES):
                    last = nc.tensor.transpose(m.ps[:, 0, i * P:(i + 1) * P], m.Gw[:, 2 * i:2 * i + 2, :].rearrange("p x s -> p (x s)"), m.ident[:])
                last.then_inc(t["gwt_ps"], 1)
                pe.wait_ge(t["hidT"], it + 1)
                pe.sem_inc(m.seen, 1)
                product(2, 4, 4, m.hidT)
        done = rounds * N_PAIRS
        for i in range(TILES):
            if i == 0:
                pe.wait_ge(t["ye"], done + 1)
                pe.sem_inc(m.seen, 1)
            pe.wait_ge(t["acc"], done * 2 + (i + 1))
            combine(i)
        for c in range(N_SLOTS):
            free(c)
        phase_end(pe, m, 3 + 2 * l)


def second_scalar(nc, act, m):
    t = m.t
    a = nc.scalar.activation
    norm_act(nc, act, m, t["std2"])
    act.wait_ge(m.rows_in, rows_count(0))
    a(m.cc, m.cc, ACT.Silu).then_inc(t["c_act"], 1)
    phase_end(act, m, 1)
    for l in range(DEPTH):
        if l == 0:
            for c in range(KC):
                act.wait_ge(t["ag"], c + 1)
                if c == 0:
                    act.wait_ge(t["vec"], 1)
                if c >= 2:
                    act.wait_ge(t["glu"], c - 1)
                a(m.sg2[:, c % 2, :], m.ps[:, c % 2, SEQ:2 * SEQ], ACT.Sigmoid, bias=m.vec[:, c, V_BG:V_BG + 1]).then_inc(t["sig"], 1)
            act.wait_ge(t["ln_var"], 1)
            a(m.stat[:, 32:34], m.stat[:, 28:32].rearrange("p (i k) -> p i k", k=2)[:, :, 1], ACT.Sqrt, bias=m.eps[:, 2:3]).then_inc(t["ln_std"], 1)
            for c in range(KC):
                act.wait_ge(t["tr3"], 2 * (c // 2) + 2)
                a(m.hT[:, c, :], m.ps[:, c // 2, (c % 2) * SEQ:(c % 2 + 1) * SEQ], ACT.Silu,
                  bias=m.vec[:, c, V_LB:V_LB + 1], scale=m.vec[:, c, V_LG:V_LG + 1]).then_inc(t["silu_T"], 1)
        else:
            for c in range(KC):
                act.wait_ge(t["ag"], c + 1)
                if c >= 2:
                    act.wait_ge(t["glu"], c - 1)
                a(m.sg2[:, c % 2, :], m.ps[:, c % 2, 0:SEQ], ACT.Copy).then_inc(t["sig"], 1)
        act.wait_ge(t["var3"], 1)
        a(m.stat[:, 32:34], m.stat[:, 28:32].rearrange("p (i k) -> p i k", k=2)[:, :, 1], ACT.Sqrt, bias=m.eps[:, 2:3]).then_inc(t["std3"], 1)
        phase_end(act, m, 2 + 2 * l)
        act.wait_ge(t["gmaxed"], 1)
        a(m.gex, m.gex, ACT.Exp).then_inc(t["gexp"], 1)
        act.wait_ge(t["emaxed"], 1)
        a(m.stat[:, 44:46], m.stat[:, 42:44], ACT.Exp).then_inc(t["eexp"], 1)
        act.wait_ge(t["rounds"], 1)
        act.wait_ge(t["zeros"], 1)
        act.sem_inc(t["ye"], 1)
        act.sem_inc(t["gwt"], 1)
        rounds = act.value_load(m.rounds_i[0:1, 0:1], min_val=1, max_val=4)
        with act.Fori(0, rounds) as r:
            with act.Fori(0, N_PAIRS) as p:
                it = r * N_PAIRS + p
                act.wait_ge(t["xg_ps"], it + 1)
                a(m.xg.rearrange("p j s -> p (j s)"), banks(m, 0, 2), ACT.Copy).then_inc(t["xg"], 1)
                act.wait_ge(m.e_used[l][0], it + 2)
                a(m.sgx, m.ps[:, 2, :], ACT.Silu).then_inc(t["esilu"], 1)
                act.wait_ge(t["hidT_ps"], it + 1)
                a(m.hidT.rearrange("p c s -> p (c s)"), m.ps[:, 1, :], ACT.Copy).then_inc(t["hidT"], 1)
                act.wait_ge(t["gwt_ps"], it + 1)
                a(m.GwT.rearrange("p i t -> p (i t)"), m.ps[:, 0, 0:256], ACT.Copy).then_inc(t["gwt"], 1)
                act.wait_ge(m.e_used[l][2], it + 2)
                a(m.ye, banks(m, 4, 2), ACT.Copy).then_inc(t["ye"], 1)
        act.wait_ge(t["var3"], 1)
        a(m.stat[:, 32:34], m.stat[:, 28:32].rearrange("p (i k) -> p i k", k=2)[:, :, 1], ACT.Sqrt, bias=m.eps[:, 2:3]).then_inc(t["std3"], 1)
        phase_end(act, m, 3 + 2 * l)


def second_vector(nc, dve, m):
    t = m.t
    v = nc.vector
    tt, ts, stt = v.tensor_tensor, v.tensor_scalar, v.scalar_tensor_tensor
    dve.wait_ge(t["std2"], 1)
    v.reciprocal(m.rstd, m.std)
    dve.drain()
    for i in range(TILES):
        ts(m.x[:, i, :], m.x[:, i, :], m.rstd[:, i:i + 1], None, ALU.mult)
    v.memset(m.eps[:, 2:3], LN_EPS)
    dve.wait_ge(m.rows_in, rows_count(0))
    dve.drain()
    tt(m.x[:], m.x[:], bcast(m.rows[0].unsqueeze(1), [P, TILES, D]), ALU.mult)
    dve.wait_ge(t["c_act"], 1)
    v.tensor_copy(m.cw, bcast(m.cc.unsqueeze(2), [P, KC, P]))
    dve.drain()
    phase_end_leader(dve, m)

    def mods(phase):
        dve.wait_ge(m.rows_in, rows_count(phase))
        for k in range(6):
            part = m.mod[:, k // 2, (k % 2) * 512:(k % 2 + 1) * 512]
            dve.wait_ge(t["ada_ps"], k + 1)
            if k < 2:
                tt(part, m.ps[:, k, :], part, ALU.add).then_inc(t["mod"], 1)
            else:
                stt(part, m.ps[:, k, :], 1.0, part, ALU.add, ALU.add).then_inc(t["mod"], 1)

    def modulate():
        dve.drain()
        tt(m.O[:], m.x[:], bcast(m.mod[:, 1, :].unsqueeze(1), [P, TILES, D]), ALU.mult)
        dve.drain()
        for i in range(TILES):
            tt(m.O[:, i, :], m.O[:, i, :], m.mod[:, 0, :], ALU.add).then_inc(t["hn2"], 1)

    def stats(src, sem):
        for i in range(TILES):
            for n in range(2):
                v.bn_stats(m.stat[:, (2 * i + n) * 6:(2 * i + n + 1) * 6], src(i, n))
        dve.drain()
        for i in range(TILES):
            last = v.bn_aggr(m.stat[:, 28 + 2 * i:30 + 2 * i], m.stat[:, 12 * i:12 * i + 12])
        last.then_inc(sem, 1)

    def layer_norm(gain, bias):
        dve.drain()
        stats(lambda i, n: m.x[:, i, n * 512:(n + 1) * 512], t["var3"])
        dve.wait_ge(t["std3"], 1)
        v.reciprocal(m.stat[:, 34:36], m.stat[:, 32:34])
        dve.drain()
        for i in range(TILES):
            ts(m.x[:, i, :], m.x[:, i, :], m.stat[:, 28 + 2 * i:29 + 2 * i], m.stat[:, 34 + i:35 + i], ALU.subtract, ALU.mult)
        dve.drain()
        tt(m.x[:], m.x[:], bcast(gain.unsqueeze(1), [P, TILES, D]), ALU.mult)
        dve.drain()
        tt(m.x[:], m.x[:], bcast(bias.unsqueeze(1), [P, TILES, D]), ALU.add)
        dve.drain()

    def residual(y):
        dve.drain()
        tt(m.O[:], y, bcast(m.mod[:, 2, :].unsqueeze(1), [P, TILES, D]), ALU.mult)
        dve.drain()
        stt(m.x[:].rearrange("p i d -> p (i d)"), m.x[:].rearrange("p i d -> p (i d)"), ALPHA, m.O[:].rearrange("p i d -> p (i d)"), ALU.mult, ALU.add)

    for l in range(DEPTH):
        if l == 0:
            dve.wait_ge(t["vec_ps"], 1)
            v.tensor_copy(m.vec.rearrange("p j v -> p (j v)"), m.ps[:, 7, 0:KC * N_V]).then_inc(t["vec"], 1)
        mods(1 + 2 * l)
        modulate()
        evacuate_dve(nc, dve, m, None, t["tr2"], t["hT2"])
        v.memset(m.upad[:, :, 0:PAD], 0.0)
        for c in range(KC):
            dve.wait_ge(t["sig"], c + 1)
            acc = m.ps[:, 2 + c % 2, 0:SEQ] if l == 0 else m.ps[:, 4 + c % 2, 0:SEQ]
            u = m.upad[:, c, PAD:]
            if l == 0:
                stt(u, m.ps[:, c % 2, 0:SEQ], m.vec[:, c, V_BA:V_BA + 1], m.sg2[:, c % 2, :], ALU.add, ALU.mult).then_inc(t["glu"], 1)
                taps, first, row = K_A, 0, V_DW
            else:
                tt(u, m.ps[:, c % 2, SEQ:2 * SEQ], m.sg2[:, c % 2, :], ALU.mult).then_inc(t["glu"], 1)
                taps, first, row = K_B, PAD - (K_B - 1), V_DWB
            for k in range(taps):
                dve.drain()
                w = m.vec[:, c, row + k:row + k + 1]
                src = m.upad[:, c, first + k:first + k + SEQ]
                if k == 0 and l == 0:
                    ts(acc, src, w, m.vec[:, c, V_BDW:V_BDW + 1], ALU.mult, ALU.add)
                elif k == 0:
                    ts(acc, src, w, None, ALU.mult)
                elif k < taps - 1:
                    stt(acc, src, w, acc, ALU.mult, ALU.add)
                elif l == 0:
                    stt(m.cvT[:, c, :], src, w, acc, ALU.mult, ALU.add).then_inc(t["v_ready"], 1)
                else:
                    stt(m.cvT[:, c, :], src, w, acc, ALU.mult, ALU.add)
                    dve.drain()
                    tt(m.cvT[:, c, :], m.ps[:, 2 + c % 2, 0:SEQ], m.cvT[:, c, :], ALU.mult).then_inc(t["v_ready"], 1)
        if l == 0:
            dve.wait_ge(t["back_ps"], TILES)
            stats(lambda i, n: m.ps[:, 4 + 2 * i + n, :], t["ln_var"])
            dve.wait_ge(t["ln_std"], 1)
            v.reciprocal(m.stat[:, 34:36], m.stat[:, 32:34])
            dve.drain()
            for i in range(TILES):
                last = ts(m.O[:, i, :], banks(m, 4 + 2 * i, 2), m.stat[:, 28 + 2 * i:29 + 2 * i], m.stat[:, 34 + i:35 + i], ALU.subtract, ALU.mult)
            last.then_inc(t["ln_x"], 1)
        dve.wait_ge(t["y2"], 1)
        for i in range(TILES):
            if l == 0:
                tt(m.O[:, i, :], banks(m, 4 + 2 * i, 2), m.rows[0], ALU.add)
            else:
                v.tensor_copy(m.O[:, i, :], banks(m, 4 + 2 * i, 2))
        residual(m.O[:])
        layer_norm(m.rows[1], m.rows[2])
        phase_end_leader(dve, m)

        mods(2 + 2 * l)
        modulate()
        evacuate_dve(nc, dve, m, None, t["tr2"], t["hT2"])
        dve.wait_ge(t["router_ps"], 1)
        tt(m.lg, m.ps[:, 6, 0:72].rearrange("p (i e) -> p i e", i=TILES), bcast(m.r_b.unsqueeze(1), [P, TILES, 36]), ALU.add)
        v.memset(m.zero32, 0.0)
        st = m.stat
        dve.drain()
        gl = m.lg[:, :, 0:N_GRP]

        def first_of(eq, cs, out, n):
            for i in range(TILES):
                v.tensor_tensor_scan(out=cs[:, i, :], data0=eq[:, i, :], data1=m.zero32[:, 0:n], initial=0.0, op0=ALU.add, op1=ALU.add)
            dve.drain()
            stt(out, cs, 1.0, eq, ALU.is_equal, ALU.mult)
            dve.drain()
        v.reduce_max(st[:, 36:38], gl, axis=AX)
        dve.drain()
        gm = bcast(st[:, 36:38].unsqueeze(2), [P, TILES, N_GRP])
        tt(m.gex, gl, gm, ALU.subtract).then_inc(t["gmaxed"], 1)
        tt(m.geq, gl, gm, ALU.is_equal)
        dve.drain()
        first_of(m.geq, m.gcs, m.gfirst, N_GRP)
        ts(m.gcs, m.gfirst, 1.0, 1e30, ALU.subtract, ALU.mult)
        for i in range(TILES):
            tt(m.lm[:, i, :].rearrange("p (g e) -> p g e", g=N_GRP), m.lg[:, i, N_GRP:].rearrange("p (g e) -> p g e", g=N_GRP),
               bcast(m.gfirst[:, i, :].unsqueeze(2), [P, N_GRP, PER_GRP]), ALU.mult)
        dve.drain()
        for i in range(TILES):
            lm = m.lm[:, i, :].rearrange("p (g e) -> p g e", g=N_GRP)
            tt(lm, lm, bcast(m.gcs[:, i, :].unsqueeze(2), [P, N_GRP, PER_GRP]), ALU.add)
        dve.drain()
        v.reduce_max(st[:, 38:40], m.lm, axis=AX)
        dve.drain()
        tt(m.eq, m.lm, bcast(st[:, 38:40].unsqueeze(2), [P, TILES, N_EXP]), ALU.is_equal)
        dve.drain()
        first_of(m.eq, m.cs, m.first1, N_EXP)
        stt(m.lm, m.first1, -2e30, m.lm, ALU.mult, ALU.add)
        dve.drain()
        v.reduce_max(st[:, 40:42], m.lm, axis=AX)
        dve.drain()
        tt(st[:, 42:44], st[:, 40:42], st[:, 38:40], ALU.subtract).then_inc(t["emaxed"], 1)
        tt(m.eq, m.lm, bcast(st[:, 40:42].unsqueeze(2), [P, TILES, N_EXP]), ALU.is_equal)
        dve.drain()
        first_of(m.eq, m.cs, m.first2, N_EXP)
        tt(m.A, m.first1, m.first2, ALU.add).then_inc(t["routed"], 1)
        dve.wait_ge(t["gexp"], 1)
        v.reduce_sum(st[:, 46:48], m.gex, axis=AX)
        dve.wait_ge(t["eexp"], 1)
        ts(st[:, 48:50], st[:, 44:46], 1.0, None, ALU.add)
        dve.drain()
        tt(st[:, 50:52], st[:, 48:50], st[:, 46:48], ALU.mult)
        dve.drain()
        v.reciprocal(st[:, 52:54], st[:, 50:52])
        dve.drain()
        tt(st[:, 54:56], st[:, 52:54], st[:, 44:46], ALU.mult)
        tt(m.w1t, m.first1, bcast(st[:, 52:54].unsqueeze(2), [P, TILES, N_EXP]), ALU.mult)
        dve.drain()
        tt(m.W, m.first2, bcast(st[:, 54:56].unsqueeze(2), [P, TILES, N_EXP]), ALU.mult)
        dve.drain()
        tt(m.W, m.W, m.w1t, ALU.add)
        dve.wait_ge(t["pos_ps"], 1)
        stt(m.posm, m.ps[:, 7, 0:64].rearrange("p (i e) -> p i e", i=TILES), 1.0, m.A, ALU.add, ALU.mult)
        v.reduce_max(st[:, 56:57], m.ps[:, 7, 64:96], axis=AX)
        dve.drain()
        ts(m.posm, m.posm, -1.0, None, ALU.add)
        for k in range(1, 4):
            ts(st[:, 56 + k:57 + k], st[:, 56:57], T * k + 0.5, None, ALU.is_gt)
        dve.drain()
        tt(st[:, 60:61], st[:, 57:58], st[:, 58:59], ALU.add)
        dve.drain()
        stt(st[:, 60:61], st[:, 60:61], 1.0, st[:, 59:60], ALU.add, ALU.add)
        dve.drain()
        v.tensor_copy(m.rounds_i[:], st[0:1, 60:61]).then_inc(t["rounds"], 1)
        dve.drain().then_inc(m.rounds_set[l], 1)
        dve.wait_ge(t["zeros"], 1)
        dve.sem_inc(t["acc"], 1)
        rounds = dve.value_load(m.rounds_i[0:1, 0:1], min_val=1, max_val=4)
        pairs = lambda ap: ap.rearrange("p i (q x) -> p i q x", x=2)
        with dve.Fori(0, rounds) as r:
            with dve.Fori(0, N_PAIRS) as p:
                it = r * N_PAIRS + p
                v.tensor_copy(m.cur[:, 0], pairs(m.posm)[:, :, p, :])
                v.tensor_copy(m.cur[:, 1], pairs(m.W)[:, :, p, :])
                dve.drain()
                dve.wait_ge(t["gwt"], it + 1)
                cur = m.cur[:].rearrange("p k i x -> p k (i x)")
                wide = [P, 4, T]
                tt(m.G, bcast(m.iota64[:].unsqueeze(1), wide), bcast(cur[:, 0, :].unsqueeze(2), wide), ALU.is_equal)
                dve.drain().then_inc(t["gsel"], 1)
                tt(m.Gw, m.G, bcast(cur[:, 1, :].unsqueeze(2), wide), ALU.mult).then_inc(t["gw"], 1)
                dve.wait_ge(t["comb"], it * 2 + 1)
                tt(m.yacc[:, 0, :], banks(m, 6, 2), m.yacc[:, 0, :], ALU.add).then_inc(t["acc"], 1)
                dve.wait_ge(t["esilu"], it + 1)
                dve.sem_inc(m.seen, 1)
                dve.wait_ge(m.e_used[l][1], it + 2)
                tt(m.hid2, m.ps[:, 3, :], m.sgx, ALU.mult).then_inc(t["ehid"], 1)
                dve.wait_ge(t["comb"], it * 2 + 2)
                tt(m.yacc[:, 1, :], banks(m, 6, 2), m.yacc[:, 1, :], ALU.add).then_inc(t["acc"], 1)
            ts(m.posm, m.posm, -float(T), None, ALU.add)
            dve.drain()
        done = rounds * N_PAIRS
        for x in range(2):
            dve.wait_ge(t["comb"], done * 2 + (x + 1))
            tt(m.yacc[:, x, :], banks(m, 6, 2), m.yacc[:, x, :], ALU.add).then_inc(t["acc"], 1)
        dve.drain()
        residual(m.yacc)
        dve.wait_ge(m.rows_in, rows_count(2 + 2 * l))
        layer_norm(m.rows[0], m.rows[1])
        if l == DEPTH - 1:
            dve.drain().then_inc(m.x_out, 1)
        phase_end_leader(dve, m)


CONSTS = ["ident", "cos64", "sin64", "cos32", "sin32", "causal", "dil_mask", "dil_counts", "cmp_mask", "cmp_seen", "head_rows",
          "before", "ones", "iota64"]


def program(nc, a, out):
    m = Mem()
    place(nc, m)
    place_second(nc, m)
    sem = nc.alloc_semaphore
    m.s = {name: sem(name) for name in FIRST_SEMS}
    m.first_range = range(m.s["std"].num, m.s["arrive"].num + 1)
    assert len(m.first_range) == len(FIRST_SEMS)
    m.ring_full = [sem(f"ring_full{i}") for i in range(N_SLOTS)]
    m.ring_free = [sem(f"ring_free{i}") for i in range(N_SLOTS)]
    m.params, m.release = sem("params"), sem("release")
    m.x_in, m.eps_set, m.heads_w, m.consts_in, m.zeroed = sem("x_in"), sem("eps_set"), sem("heads_w"), sem("consts_in"), sem("zeroed")
    m.stored = sem("stored")
    m.seen = sem("seen")
    second_sems(nc, m)
    m.n_consts = len(CONSTS)
    with nc.Block() as block:
        @block.sync
        def _(sp):
            for i in range(TILES):
                sp.dma_start(m.x[:, i, :], a["x"][0, i * P:(i + 1) * P, :]).then_inc(m.x_in, 16)
            first_sync(nc, sp, m, a)
            second_sync(nc, sp, m, a, out)

        @block.gpsimd
        def _(pool):
            nc.gpsimd.memset(m.wqz[:], 0.0)
            nc.gpsimd.memset(m.wkz[:], 0.0)
            nc.gpsimd.memset(m.uT[:, :, 0:3], 0.0)
            pool.drain()
            first_pool(nc, pool, m, a)
            second_pool(nc, pool, m, a)

        @block.scalar
        def _(act):
            for name in CONSTS:
                dst = {"ident": m.ident, "cos64": m.cos64, "sin64": m.sin64, "cos32": m.cos32, "sin32": m.sin32, "causal": m.causal,
                       "dil_mask": m.dil_mask, "dil_counts": m.dil_counts, "cmp_mask": m.cmp_mask, "cmp_seen": m.cmp_seen,
                       "head_rows": m.head_rows, "before": m.before, "ones": m.ones, "iota64": m.iota64}[name]
                src = a[name]
                if name not in ("ident", "head_rows", "before", "ones", "iota64"):
                    src = src.rearrange("(i p) c -> p i c", p=P)
                act.dma_start(dst[:], src).then_inc(m.consts_in, 16)
            first_scalar(nc, act, m)
            second_scalar(nc, act, m)

        @block.tensor
        def _(pe):
            pe.wait_ge(m.consts_in, 16 * m.n_consts)
            first_tensor(nc, pe, m)
            second_tensor(nc, pe, m)

        @block.vector
        def _(dve):
            first_vector(nc, dve, m)
            second_vector(nc, dve, m)


INPUTS = ["x", "norm_mix", "w_in", "nsa_cmp_pos", "nsa_cmp_w", "diff_lambda", "diff_norm", "mlstm_conv_w", "mlstm_conv_b",
          "mlstm_wq", "mlstm_wk", "mlstm_gate_b", "mlstm_norm", "w_out", "norm_ffn", "w_gate", "w_up", "w_down", "norm_final",
          "c_2", "ada_w_2", "ada_b_2", "a_w_in_2", "a_b_in_2", "a_w_dw_2", "a_b_dw_2", "a_ln_g_2", "a_ln_b_2", "a_w_out_2",
          "a_b_out_2", "b_w_in_2", "b_w_dw_2", "b_w_out_2", "mix_ln_g_2", "mix_ln_b_2", "ffn_ln_g_2", "ffn_ln_b_2",
          "r_w_group_2", "r_b_group_2", "r_w_expert_2", "r_b_expert_2", "e_w_gate_2", "e_w_up_2", "e_w_down_2"]


def kernel(**inputs):
    import numpy as np
    import concourse.bacc as bacc
    from concourse.bass_utils import run_bass_kernel_spmd

    nc = bacc.Bacc("TRN2", target_bir_lowering=False, num_devices=1)
    arrays = {}
    args = {}
    sources = {name: np.ascontiguousarray(inputs[name]) for name in INPUTS}
    sources.update(host_tables())
    for name, value in sources.items():
        arrays["in_" + name] = value
        args[name] = nc.dram_tensor("in_" + name, value.shape, mybir.dt.from_np(value.dtype), kind="ExternalInput").ap()
    out = nc.dram_tensor("out_0", (1, SEQ, D), F32, kind="ExternalOutput").ap()
    program(nc, args, out)
    r = run_bass_kernel_spmd(nc, [arrays], core_ids=[0])
    return r.results[0]["out_0"]
```

```python
import math
from concourse import mybir

F32 = mybir.dt.float32
ACT = mybir.ActivationFunctionType
ALU = mybir.AluOpType
AX = mybir.AxisListType.X

P = 128
SEQ, D, DEPTH = 256, 1024, 2
TILES, KC = SEQ // P, D // P
HD, NH, GW = 64, 4, 256
D_FF = 2816
EPS, LN_EPS = 1e-6, 1e-5
ALPHA = (2.0 * DEPTH) ** 0.25

Z_Q, Z_KC, Z_VC, Z_KS, Z_VS, Z_KW, Z_VW, Z_G = 0, 256, 320, 384, 448, 512, 576, 640
Z_BQ, Z_BV, Z_U, Z_CV, Z_I, Z_F, Z_O, Z_DQ, Z_DV = 652, 1164, 1420, 1676, 1932, 1936, 1940, 2196, 2708
D_IN = 2964
N_IN = 6
ZC = D_IN // N_IN
SLOT = 4096
N_SLOTS = 6

T_QRAW, T_KC, T_VC, T_QROT, T_KS, T_KW, T_DQ, T_DK, T_BQ, T_BK = 0, 4, 5, 6, 10, 11, 12, 16, 20, 28
N_T = 36
R_Q, R_K, R_D, R_B, R_ALL = 0, 256, 384, 896, 1408

N_CMP, CMP_LEN, CMP_STRIDE = 15, 32, 16
N_PREP = 16
FU = 256
N_FU = D_FF // FU

UNITS = [("slc", 0, 0), ("dil", 0, 0), ("slc", 1, 0), ("mlstm", 0, 0), ("diff", 0, 0), ("win", 0, 0), ("diff", 1, 0),
         ("dil", 1, 0), ("win", 1, 0), ("mlstm", 1, 0), ("diff", 0, 1), ("cmp", 0, 0), ("diff", 1, 1), ("cmp", 1, 0)]

N_ADA = 12
ADA_SLOTS = (0, 1, 5)
ADA_LOADS = [(0,), (1, 2), (3,), (4,), (5, 6), (7,), (8, 9), (10,), (11,), (), ()]
ADA_AFTER = [(0,), (1,), (2, 3), (4,), (5, 6), (7,), (8, 9), (10,), (11,), (), ()]
Z_ORDER = ADA_SLOTS + (2, 3, 4)

FIRST_SEMS = ["std", "hn", "tr", "hT", "z_ps", "z_act", "z_dve", "rope", "rope_b", "prep_ps", "prep_ev", "gates_in", "gate_abs",
              "gate_ln", "gate_rows", "gate_cols", "conv", "uc", "blocks", "lam_in", "lam_exp", "small_ready",
              "scores", "masked", "exps", "probs", "pt_ps", "pt", "pv", "o_done", "ss", "o_std", "o_final",
              "std_b", "hn_b", "tr_b", "hT_b", "tr_o", "OT", "y_ps", "x_mid",
              "gu", "silu", "hid", "down", "ffn_full0", "ffn_full1", "ffn_free0", "ffn_free1", "ada_full0", "ada_full1", "ada_full2", "ada_ps", "ada_row", "ada_out0", "ada_out1", "arrive"]


class Mem:
    pass


def host_tables():
    import numpy as np
    t = {}
    t["ident"] = np.eye(P, dtype=np.float32)
    for name, dim in (("64", HD), ("32", HD // 2)):
        inv = (1.0 / (np.float32(10000.0) ** (np.arange(0, dim, 2, dtype=np.float32) / np.float32(dim)))).astype(np.float32)
        ang = np.arange(SEQ, dtype=np.float32)[:, None] * inv[None, :]
        c, s = np.cos(ang).astype(np.float32), np.sin(ang).astype(np.float32)
        t["cos" + name] = np.concatenate([c, c], 1)
        t["sin" + name] = np.concatenate([-s, s], 1)
    q, k = np.arange(SEQ)[:, None], np.arange(SEQ)[None, :]
    dist = q - k
    t["causal"] = np.where(dist >= 0, 0.0, -1e30).astype(np.float32)
    counts = ((dist >= 0) & (dist <= 128)).astype(np.float32)
    counts += ((dist >= 0) & (dist % 4 == 0)).astype(np.float32)
    counts += ((dist >= 0) & (dist % 16 == 0)).astype(np.float32)
    t["dil_counts"] = counts
    t["dil_mask"] = np.where(counts > 0, 0.0, -1e30).astype(np.float32)
    end = np.arange(N_CMP) * CMP_STRIDE + CMP_LEN - 1
    seen = end[None, :] <= np.arange(SEQ)[:, None]
    t["cmp_mask"] = np.where(seen, 0.0, -1e30).astype(np.float32)
    t["cmp_seen"] = seen.astype(np.float32)
    sel = np.zeros((NH, NH, P), np.float32)
    for h in range(NH):
        sel[h, h] = 1.0
    t["head_rows"] = sel
    init = [0.8 - 0.6 * math.exp(-0.3 * layer) for layer in range(DEPTH)]
    t["lam_init"] = np.array([[v, 1.0 - v] for v in init], np.float32)
    t["before"] = np.triu(np.ones((P, P), np.float32), 1)
    t["ones"] = np.ones((P, P), np.float32)
    t["iota64"] = np.tile(np.arange(64, dtype=np.float32), (P, 1))
    return t


def place(nc, m):
    sb = nc.alloc_sbuf_tensor
    m.ring = sb("ring", [P, N_SLOTS * SLOT], F32)
    m.x = sb("x", [P, TILES, D], F32)
    m.hT = sb("hT", [P, KC, SEQ], F32)
    m.O = sb("O", [P, TILES, D], F32)
    m.z = sb("z", [P, TILES, D_IN], F32)
    m.qkT = sb("qkT", [P, N_T, SEQ], F32)
    m.late = sb("late", [P, 4 * D], F32)
    free = [0]

    def early(shape):
        n = math.prod(shape)
        at = free[0]
        free[0] += n
        assert free[0] <= 4 * D
        flat = m.late[:, at:at + n]
        if len(shape) == 1:
            return flat
        names = " ".join("abc"[:len(shape)])
        return flat.rearrange(f"p ({names}) -> p {names}", **dict(zip("abc", shape)))
    m.uT = early([2, SEQ + 3])
    m.ucT = early([2, SEQ])
    m.posT = sb("posT", [HD, 2, CMP_LEN], F32)
    m.kcT = sb("kcT", [HD, 16], F32)
    m.vc = sb("vc", [16, HD], F32)
    m.gates = sb("gates", [P, TILES, 12], F32)
    m.small = sb("small", [P, 160], F32)
    m.eps = sb("eps", [P, 4], F32)
    m.ident = sb("ident", [P, P], F32)
    m.cos64 = early([TILES, HD])
    m.sin64 = early([TILES, HD])
    m.cos32 = early([TILES, HD // 2])
    m.sin32 = early([TILES, HD // 2])
    m.causal = early([TILES, SEQ])
    m.dil_mask = early([TILES, SEQ])
    m.dil_counts = early([TILES, SEQ])
    m.cmp_mask = sb("cmp_mask", [P, TILES, N_CMP], F32)
    m.cmp_seen = sb("cmp_seen", [P, TILES, N_CMP], F32)
    m.head_rows = sb("head_rows", [NH, NH, P], F32)
    m.g_mix = sb("g_mix", [P, KC], F32)
    m.g_ffn = sb("g_ffn", [P, KC], F32)
    m.gains = sb("gains", [P, 2, DEPTH, KC], F32)
    m.cc = sb("cc", [P, KC], F32)
    m.c32 = sb("c32", [P, KC, 32], F32)
    m.pos = sb("pos", [CMP_LEN, 2, HD], F32)
    m.lamv = sb("lamv", [P, 4, 32], F32)
    m.g_sub = early([2 * GW])
    m.conv_w = sb("conv_w", [P, 2, 4], F32)
    m.conv_b = sb("conv_b", [P, 2], F32)
    m.wqz = early([2, 2, HD])
    m.wkz = early([2, 2, HD])
    m.gate_b = sb("gate_b", [NH, 2], F32)
    m.lam_init = sb("lam_init", [P, 2], F32)
    m.ps = nc.alloc_psum_tensor("ps", [P, 8, 512], F32)

    def ring(a, b):
        return m.ring[:, a:b]
    m.slot = [ring(s * SLOT, (s + 1) * SLOT) for s in range(N_SLOTS)]
    m.ffn = [ring(2 * SLOT + b * 6144, 2 * SLOT + (b + 1) * 6144) for b in range(2)]
    m.rz = m.ffn[0][:, 0:2 * R_ALL].rearrange("p (i c) -> p i c", i=TILES)
    att = m.ffn[1]
    m.sm = att[:, 0:2048].rearrange("p (b h k) -> p b h k", b=2, h=4)
    m.pr = att[:, 2048:4096].rearrange("p (b h k) -> p b h k", b=2, h=4)
    m.rb = att[:, 4096:5120].rearrange("p (h k) -> p h k", h=4)
    m.pt = att[:, 5120:6144].rearrange("p (h t q) -> p h t q", h=4, t=2)
    q = m.qkT[:].rearrange("p s t -> p (s t)")
    m.ada_b = q[0:N_ADA, 8192:8704]
    m.mrow = q[:, 8704:8704 + 2 * P].rearrange("p (b n) -> p b n", b=2)
    flat = m.hT[:].rearrange("p j t -> p (j t)")
    m.tmp = flat[:, 0:R_ALL]
    m.blocks = flat[0:HD, 0:2 * CMP_LEN * N_CMP].rearrange("d (w l n) -> d w l n", w=2, l=CMP_LEN)
    m.grow = m.O[:].rearrange("p i c -> p (i c)").rearrange("p (g t) -> p g t", t=SEQ)

    s = m.small
    m.ssq, m.std, m.rstd = s[:, 0:2], s[:, 2:4], s[:, 4:6]
    m.mx = [s[:, 8 + 4 * b:12 + 4 * b] for b in range(2)]
    m.nmx = [s[:, 16 + 4 * b:20 + 4 * b] for b in range(2)]
    m.zs = [s[:, 24 + 4 * b:28 + 4 * b] for b in range(2)]
    m.rs = [s[:, 32 + 4 * b:36 + 4 * b] for b in range(2)]
    m.nM = s[:, 40:48].rearrange("p (i h) -> p i h", i=TILES)
    m.em = s[:, 48:56].rearrange("p (i h) -> p i h", i=TILES)
    m.lam = s[:, 56:62]
    m.sso = s[:, 64:80].rearrange("p (i h) -> p i h", i=TILES)
    m.sstd = s[:, 80:96].rearrange("p (i h) -> p i h", i=TILES)
    m.srec = s[:, 96:112].rearrange("p (i h) -> p i h", i=TILES)


def banks(m, b, n=1):
    return m.ps[:, b:b + n, :].rearrange("p b c -> p (b c)")


def bcast(ap, shape):
    return ap.to_broadcast(shape)



def norm_act(nc, act, m, std):
    for i in range(TILES):
        nc.scalar.activation(m.O[:, i, :], m.x[:, i, :], ACT.Square, accum_out=m.ssq[:, i:i + 1])
    act.drain()
    nc.scalar.activation(m.std, m.ssq, ACT.Sqrt, scale=1.0 / D, bias=m.eps[:, 0:1]).then_inc(std, 1)


def norm_dve(nc, dve, m, std, hn):
    dve.wait_ge(std, 1)
    nc.vector.reciprocal(m.rstd, m.std)
    dve.drain()
    for i in range(TILES):
        nc.vector.tensor_scalar(m.O[:, i, :], m.x[:, i, :], m.rstd[:, i:i + 1], None, ALU.mult).then_inc(hn, 1)


def transpose_pe(nc, pe, m, ready, count, done):
    pe.wait_ge(ready, count)
    for j in range(KC):
        for i in range(TILES):
            src = m.O[:, i, :].rearrange("t (p j) -> t j p", j=KC)[:, j, :]
            dst = m.ps[:, j // 2, (j % 2) * 256 + i * P:(j % 2) * 256 + (i + 1) * P]
            last = nc.tensor.transpose(dst, src, m.ident[:])
        last.then_inc(done, 1)


def evacuate_dve(nc, dve, m, gain, tr, done):
    for j in range(KC):
        dve.wait_ge(tr, 2 * (j // 2) + 2)
        src = m.ps[:, j // 2, (j % 2) * 256:(j % 2) * 256 + SEQ]
        if gain is None:
            nc.vector.tensor_copy(m.hT[:, j, :], src).then_inc(done, 1)
        else:
            nc.vector.tensor_scalar(m.hT[:, j, :], src, gain[:, j:j + 1], None, ALU.mult).then_inc(done, 1)


def prep_bank(b):
    return 2 * (b % 4)



def first_sync(nc, sp, m, a):
    s = m.s
    with sp.Fori(0, DEPTH) as L:
        w_in = a["w_in"][L].rearrange("(p j) n -> p j n", j=KC)
        for c in Z_ORDER:
            per = 3 if c in ADA_SLOTS else 1
            sp.wait_ge(m.ring_free[c], L * per + 1)
            sp.dma_start(m.slot[c][:, 0:KC * ZC].rearrange("p (j n) -> p j n", j=KC),
                         w_in[:, :, c * ZC:(c + 1) * ZC]).then_inc(m.ring_full[c], 16)
        sp.wait_ge(m.ring_free[5], L * 3 + 2)
        sp.dma_start(m.slot[5][0:HD, :].rearrange("d (w l e) -> d w l e", w=2, l=CMP_LEN),
                     a["nsa_cmp_w"][L].rearrange("w (l d) e -> d w l e", d=HD)).then_inc(m.ring_full[5], 16)
        w_out = a["w_out"][L].rearrange("(p j) n -> p j n", j=KC)
        for n in range(2):
            sp.wait_ge(m.ring_free[n], L * 3 + 2)
            sp.dma_start(m.slot[n].rearrange("p (j n) -> p j n", j=KC),
                         w_out[:, :, n * 512:(n + 1) * 512]).then_inc(m.ring_full[n], 16)
        ada_w = a["ada_w_2"][L].rearrange("(p j) n -> p j n", j=KC)

        def ada(k):
            slot = ADA_SLOTS[k % 3]
            if k < 3:
                sp.wait_ge(m.ring_free[slot], L * 3 + 3)
            else:
                sp.wait_ge(s["ada_ps"], k - 2)
            sp.dma_start(m.slot[slot].rearrange("p (j n) -> p j n", j=KC), ada_w[:, :, k * 512:(k + 1) * 512]).then_inc(s[f"ada_full{k % 3}"], 16)

        w_gate = a["w_gate"][L].rearrange("(p j) n -> p j n", j=KC)
        w_up = a["w_up"][L].rearrange("(p j) n -> p j n", j=KC)
        w_down = a["w_down"][L].rearrange("(u p j) n -> u p (j n)", p=P, j=2)
        for u in range(N_FU):
            buf = m.ffn[u % 2]
            if u == 0:
                sp.wait_ge(s["prep_ps"], 11)
            elif u == 1:
                sp.wait_ge(s["pv"], len(UNITS))
            else:
                sp.wait_ge(s[f"ffn_free{u % 2}"], u // 2)
            full = s[f"ffn_full{u % 2}"]
            sp.dma_start(buf[:, 0:2048].rearrange("p (j n) -> p j n", j=KC), w_gate[:, :, u * FU:(u + 1) * FU]).then_inc(full, 16)
            sp.dma_start(buf[:, 2048:4096].rearrange("p (j n) -> p j n", j=KC), w_up[:, :, u * FU:(u + 1) * FU]).then_inc(full, 16)
            sp.dma_start(buf[:, 4096:6144], w_down[u]).then_inc(full, 16)
            for k in ADA_LOADS[u]:
                ada(k)


N_PARAMS = 12


def rotate(v, eng, m, regions):
    for i in range(TILES):
        if i > 0:
            eng.drain()
        at_all = regions(i)
        for src, at, n, dim in at_all:
            half = dim // 2
            cos, sin = (m.cos64, m.sin64) if dim == HD else (m.cos32, m.sin32)
            out = m.rz[:, i, at:at + n * dim].rearrange("p (h d) -> p h d", d=dim)
            tmp = m.tmp[:, at:at + n * dim].rearrange("p (h d) -> p h d", d=dim)
            v.tensor_tensor(out, src, bcast(cos[:, i, :].unsqueeze(1), [P, n, dim]), ALU.mult)
            v.tensor_tensor(tmp[:, :, 0:half], src[:, :, half:], bcast(sin[:, i, 0:half].unsqueeze(1), [P, n, half]), ALU.mult)
            v.tensor_tensor(tmp[:, :, half:], src[:, :, 0:half], bcast(sin[:, i, half:].unsqueeze(1), [P, n, half]), ALU.mult)
        eng.drain()
        lo, hi = at_all[0][1], at + n * dim
        last = v.tensor_tensor(m.rz[:, i, lo:hi], m.rz[:, i, lo:hi], m.tmp[:, lo:hi], ALU.add)
    return last


def first_pool(nc, pool, m, a):
    s = m.s

    def params(l):
        pool.dma_start(m.pos[:], a["nsa_cmp_pos"][l].rearrange("w l d -> l w d")).then_inc(m.params, 16)
        pool.dma_start(m.lamv[:], a["diff_lambda"][l].partition_broadcast(P)).then_inc(m.params, 16)
        for h in range(NH):
            pool.dma_start(m.g_sub[:, h * HD:(h + 1) * HD], a["diff_norm"][l].partition_broadcast(P)).then_inc(m.params, 16)
        pool.dma_start(m.g_sub[:, GW:2 * GW], a["mlstm_norm"][l].partition_broadcast(P)).then_inc(m.params, 16)
        with nc.allow_non_contiguous_dma(reason="small parameters"):
            for c in range(2):
                pool.dma_start(m.conv_w[:, c, :], a["mlstm_conv_w"][l][:, c * P:(c + 1) * P].rearrange("k p -> p k")).then_inc(m.params, 16)
            pool.dma_start(m.conv_b[:], a["mlstm_conv_b"][l].rearrange("(c p) -> p c", p=P)).then_inc(m.params, 16)
            pool.dma_start(m.gate_b[:], a["mlstm_gate_b"][l].rearrange("g h -> h g")).then_inc(m.params, 16)
        pool.dma_start(m.lam_init[:], a["lam_init"][l].partition_broadcast(P)).then_inc(m.params, 16)
        for w, src in ((m.wqz, a["mlstm_wq"]), (m.wkz, a["mlstm_wk"])):
            for hp in range(2):
                pool.dma_start(w[hp * HD:(hp + 1) * HD, :, hp, :],
                               src[l].rearrange("(c hp) d e -> hp d c e", hp=2)[hp]).then_inc(m.heads_w, 16)

    def ada_bias(l):
        pool.wait_ge(s["o_final"], 1)
        pool.dma_start(m.ada_b, a["ada_b_2"][l].rearrange("(k n) -> k n", n=512)).then_inc(m.ada_bias, 16)

    def rotate_diff():
        pool.wait_ge(s["z_act"], N_IN)
        pool.wait_ge(s["z_dve"], N_IN)
        rotate(nc.gpsimd, pool, m, lambda i: [(m.z[:, i, Z_BQ:Z_BQ + 512].rearrange("p (h d) -> p h d", d=32), R_B, 16, 32)]).then_inc(s["rope_b"], 1)

    params(0)
    pool.wait_ge(m.consts_in, 16 * m.n_consts)
    with pool.Fori(0, DEPTH - 1) as L:
        rotate_diff()
        ada_bias(L)
        params(L + 1)
        layer_end(nc, pool, m, L)
    rotate_diff()
    ada_bias(DEPTH - 1)
    pool.wait_ge(m.ada_bias, 16 * DEPTH)
    second_rows(nc, pool, m, a)
    layer_end(nc, pool, m, DEPTH - 1)


def layer_end(nc, eng, m, L):
    eng.drain().then_inc(m.s["arrive"], 1)
    eng.wait_ge(m.release, L + 1)
    eng.sem_inc(m.seen, 1)


def layer_end_leader(nc, dve, m):
    dve.wait_ge(m.s["arrive"], 3)
    dve.sem_clear(m.first_range)
    dve.sem_inc(m.release, 1)


def mlstm_rows(m, col, h):
    at = col + (h % 2) * SEQ
    return m.z[0:HD, h // 2, at:at + SEQ]


def unit_maps(m, kind, t, hp):
    out = []
    q = slice(t * P, (t + 1) * P)
    nk = P * (t + 1)
    for h in range(4):
        if kind in ("slc", "win"):
            out.append((m.qkT[0:HD, T_QROT + h, q], m.qkT[0:HD, T_KS if kind == "slc" else T_KW, 0:nk]))
        elif kind == "dil":
            out.append((m.qkT[0:HD, T_DQ + h, q], m.qkT[0:HD, T_DK + h, 0:nk]))
        elif kind == "diff":
            out.append((m.qkT[0:32, T_BQ + 4 * hp + h, q], m.qkT[0:32, T_BK + 4 * hp + h, 0:nk]))
        elif kind == "mlstm":
            out.append((mlstm_rows(m, Z_BQ, h)[:, q], mlstm_rows(m, Z_DQ, h)[:, 0:nk]))
        else:
            out.append((m.qkT[0:HD, T_QRAW + h, q], m.kcT[:, 0:N_CMP]))
    return out


def unit_values(kind, hp):
    if kind == "slc":
        return [(h, Z_VS) for h in range(4)]
    if kind == "win":
        return [(h, Z_VW) for h in range(4)]
    if kind == "dil":
        return [(h, Z_DV + HD * h) for h in range(4)]
    if kind == "mlstm":
        return [(h, Z_CV + HD * h) for h in range(4)]
    return [(2 * h, Z_BV + HD * (2 * hp + h)) for h in range(2)]


def keys_of(kind, t):
    return N_CMP if kind == "cmp" else P * (t + 1)


def scores_of(m, u):
    kind, t, _ = UNITS[u]
    return banks(m, 2 * (u % 2), 2).rearrange("p (h k) -> p h k", h=4)[:, :, 0:keys_of(kind, t)]


def first_tensor(nc, pe, m):
    s = m.s
    mm = nc.tensor.matmul
    for c in range(N_SLOTS):
        pe.sem_inc(m.ring_free[c], 1)
    pe.wait_ge(m.c_set, 1)
    with pe.Fori(0, DEPTH) as L:
        transpose_pe(nc, pe, m, s["hn"], TILES, s["tr"])
        pe.wait_ge(s["hT"], KC)
        for n, c in enumerate(Z_ORDER):
            per = 2 if c in ADA_SLOTS else 1
            pe.wait_ge(m.ring_full[c], (L * per + 1) * 16)
            w = m.slot[c][:, 0:KC * ZC].rearrange("p (j n) -> p j n", j=KC)
            for i in range(TILES):
                g = TILES * n + i
                if g >= 4:
                    pe.wait_ge(s["z_act"] if g % 2 == 0 else s["z_dve"], (g - 4) // 2 + 1)
                for j in range(KC):
                    last = mm(m.ps[:, 4 + g % 4, 0:ZC], m.hT[:, j, i * P:(i + 1) * P], w[:, j, :], start=(j == 0), stop=(j == KC - 1))
                last.then_inc(s["z_ps"], 1)
            if c in ADA_SLOTS:
                pe.drain().then_inc(m.ring_free[c], 1)
        pe.wait_ge(s["z_act"], N_IN)
        pe.wait_ge(s["z_dve"], N_IN)
        pe.wait_ge(m.consts_in, 16 * m.n_consts)

        def batch(b):
            if b >= 4:
                pe.wait_ge(s["prep_ev"], b - 3)
            if b == 5:
                pe.wait_ge(s["gates_in"], 1)

        def transposed(b, sources):
            batch(b)
            for k, (src, width) in enumerate(sources):
                for i in range(TILES):
                    at = k * SEQ + i * P
                    dst = banks(m, prep_bank(b), 2)[0:width, at:at + P]
                    last = nc.tensor.transpose(dst, src(i), m.ident[:])
            last.then_inc(s["prep_ps"], 1)

        def zcol(at, width):
            return (lambda i: m.z[:, i, at:at + width]), width

        def rcol(at, width):
            return (lambda i: m.rz[:, i, at:at + width]), width

        transposed(0, [zcol(Z_Q + HD * h, HD) for h in range(NH)])
        transposed(1, [zcol(Z_KC, HD), zcol(Z_VC, HD), zcol(Z_I, NH), zcol(Z_F, NH)])
        batch(2)
        pe.wait_ge(m.params, (L + 1) * 16 * N_PARAMS)
        for c in range(2):
            for i in range(TILES):
                nc.tensor.transpose(m.ps[:, 4, c * SEQ + i * P:c * SEQ + (i + 1) * P], m.z[:, i, Z_U + c * P:Z_U + (c + 1) * P], m.ident[:])
        for w in range(2):
            last = nc.tensor.transpose(m.ps[0:HD, 5, w * CMP_LEN:(w + 1) * CMP_LEN], m.pos[:, w, :], m.ident[0:CMP_LEN, 0:CMP_LEN])
        last.then_inc(s["prep_ps"], 1)
        pe.wait_ge(s["rope"], 1)
        transposed(3, [rcol(R_Q + HD * h, HD) for h in range(NH)])
        transposed(4, [rcol(R_K + HD * h, HD) for h in range(2)])
        for b in range(2):
            transposed(5 + b, [rcol(R_D + HD * (4 * b + h), HD) for h in range(4)])
        pe.wait_ge(s["rope_b"], 1)
        for b in range(4):
            transposed(7 + b, [rcol(R_B + 32 * (4 * b + h), 32) for h in range(4)])
        pe.wait_ge(m.heads_w, (L + 1) * 64)
        for b, w in ((11, m.wqz), (12, m.wkz)):
            batch(b)
            if b == 11:
                pe.wait_ge(s["uc"], 1)
            for h in range(NH):
                last = mm(banks(m, prep_bank(b), 2)[0:HD, h * SEQ:(h + 1) * SEQ], w[:, h // 2, h % 2, :], m.ucT[:, h // 2, :], start=True, stop=True)
            last.then_inc(s["prep_ps"], 1)
        batch(13)
        pe.wait_ge(m.ring_full[5], (L * 2 + 2) * 16)
        pe.sem_inc(m.seen, 1)
        pe.wait_ge(s["blocks"], 1)
        cw = m.slot[5][0:HD, :].rearrange("d (w l e) -> d w l e", w=2, l=CMP_LEN)
        for l in range(CMP_LEN):
            mm(m.ps[0:HD, 2, 0:N_CMP], cw[:, 0, l, :], m.blocks[:, 0, l, :], start=(l == 0), stop=(l == CMP_LEN - 1))
        for l in range(CMP_LEN):
            last = mm(m.ps[0:N_CMP, 3, 0:HD], m.blocks[:, 1, l, :], cw[:, 1, l, :], start=(l == 0), stop=(l == CMP_LEN - 1))
        last.then_inc(s["prep_ps"], 1)
        pe.drain().then_inc(m.ring_free[5], 1)
        batch(14)
        pe.wait_ge(s["gate_rows"], 1)
        for h in range(NH):
            last = mm(banks(m, 4, 2)[:, h * SEQ:(h + 1) * SEQ], m.head_rows[:, h, :], m.grow[0:NH, 6, :], start=True, stop=True)
        last.then_inc(s["prep_ps"], 1)
        batch(15)
        for w in range(2):
            for i in range(TILES):
                at = (2 * w + i) * NH
                last = nc.tensor.transpose(m.ps[:, 6, at:at + NH], m.grow[0:NH, 4 + w, i * P:(i + 1) * P], m.ident[0:NH, 0:NH])
        last.then_inc(s["prep_ps"], 1)
        pe.wait_ge(s["prep_ev"], N_PREP)
        pe.wait_ge(s["gate_cols"], 1)

        n = len(UNITS)
        for k in range(-1, n + 2):
            if k + 1 < n:
                kind, t, hp = UNITS[k + 1]
                if k >= 1:
                    pe.wait_ge(s["probs"] if UNITS[k - 1][0] == "mlstm" else s["masked"], k)
                view = scores_of(m, k + 1)
                for h, (q, kk) in enumerate(unit_maps(m, kind, t, hp)):
                    last = mm(view[:, h, :], q, kk, start=True, stop=True)
                last.then_inc(s["scores"], 1)
            if k >= 2:
                u = k - 2
                kind, t, hp = UNITS[u]
                pe.wait_ge(s["pt"], u + 1)
                if u >= 2:
                    pe.wait_ge(s["o_done"], u - 1)
                if kind == "cmp":
                    for h in range(4):
                        last = mm(m.ps[:, 6 + u % 2, h * HD:(h + 1) * HD], m.pt[0:N_CMP, h, 0, :], m.vc[0:N_CMP, :], start=True, stop=True)
                else:
                    for o, (h, col) in enumerate(unit_values(kind, hp)):
                        for kt in range(t + 1):
                            last = mm(m.ps[:, 6 + u % 2, o * HD:(o + 1) * HD], m.pt[:, h, kt, :], m.z[:, kt, col:col + HD], start=(kt == 0), stop=(kt == t))
                last.then_inc(s["pv"], 1)
            if 1 <= k <= n:
                u = k - 1
                kind, t, hp = UNITS[u]
                pe.wait_ge(s["probs"], u + 1)
                if u >= 1:
                    pe.wait_ge(s["pt"], u)
                pt = banks(m, 4, 2).rearrange("p (h t q) -> p h t q", h=4, t=2)
                maps = range(4) if kind == "cmp" else [v for v, _ in unit_values(kind, hp)]
                for h in maps:
                    for kt in range(1 if kind == "cmp" else t + 1):
                        if kind == "cmp":
                            last = nc.tensor.transpose(pt[0:N_CMP, h, 0, :], m.pr[:, u % 2, h, 0:N_CMP], m.ident[:])
                        else:
                            last = nc.tensor.transpose(pt[:, h, kt, :], m.pr[:, u % 2, h, kt * P:(kt + 1) * P], m.ident[:])
                last.then_inc(s["pt_ps"], 1)

        transpose_pe(nc, pe, m, s["o_final"], 1, s["tr_o"])
        pe.wait_ge(s["OT"], KC)
        for c in range(2):
            pe.wait_ge(m.ring_full[c], (L * 2 + 2) * 16)
            w = m.slot[c].rearrange("p (j n) -> p j n", j=KC)
            for i in range(TILES):
                for j in range(KC):
                    last = mm(m.ps[:, 4 + 2 * c + i, :], m.hT[:, j, i * P:(i + 1) * P], w[:, j, :], start=(j == 0), stop=(j == KC - 1))
                last.then_inc(s["y_ps"], 1)
            pe.drain().then_inc(m.ring_free[c], 1)

        transpose_pe(nc, pe, m, s["hn_b"], TILES, s["tr_b"])
        pe.wait_ge(s["hT_b"], KC)
        for u in range(N_FU):
            pe.wait_ge(s[f"ffn_full{u % 2}"], 48 * (u // 2 + 1))
            wg = m.ffn[u % 2][:, 0:2048].rearrange("p (j f c) -> p j c f", j=KC, c=2)
            wu = m.ffn[u % 2][:, 2048:4096].rearrange("p (j f c) -> p j c f", j=KC, c=2)
            wd = m.ffn[u % 2][:, 4096:6144].rearrange("p (c n) -> p c n", c=2)
            for c in range(2):
                if u >= 1:
                    pe.wait_ge(s["hid"], 2 * (u - 1) + c + 1)
                for w, at in ((wg, 0), (wu, SEQ)):
                    for j in range(KC):
                        last = mm(m.ps[:, c, at:at + SEQ], w[:, j, c, :], m.hT[:, j, :], start=(j == 0), stop=(j == KC - 1))
                last.then_inc(s["gu"], 1)
            for c in range(2):
                pe.wait_ge(s["hid"], 2 * u + c + 1)
                for i in range(TILES):
                    for n2 in range(2):
                        last = mm(m.ps[:, 4 + 2 * i + n2, :], m.ucT[:, c, i * P:(i + 1) * P], wd[:, c, n2 * 512:(n2 + 1) * 512],
                                  start=(u == 0 and c == 0), stop=(u == N_FU - 1 and c == 1))
                last.then_inc(s["down"], 1)
            pe.drain().then_inc(s[f"ffn_free{u % 2}"], 1)
            for k in ADA_AFTER[u]:
                pe.wait_ge(s[f"ada_full{k % 3}"], 16 * (k // 3 + 1))
                if k >= 2:
                    pe.wait_ge(s["ada_row"], k - 1)
                w = m.slot[ADA_SLOTS[k % 3]].rearrange("p (j n) -> p j n", j=KC)
                if k == 0:
                    pe.wait_ge(m.ada_bias, (L + 1) * 16)
                    pe.sem_inc(m.seen, 1)
                for j in range(KC):
                    for g in range(4):
                        mm(m.ps[32 * g:32 * (g + 1), 2 + k % 2, 0:P], m.c32[:, j, :], w[:, j, g * P:(g + 1) * P], start=(j == 0), stop=False)
                for g in range(4):
                    last = mm(m.ps[32 * g:32 * (g + 1), 2 + k % 2, 0:P], bcast(m.ident[0:N_ADA, k:k + 1], [N_ADA, 32]), m.ada_b[:, g * P:(g + 1) * P],
                              start=False, stop=True)
                last.then_inc(s["ada_ps"], 1)
                if k >= N_ADA - 3:
                    pe.drain().then_inc(m.ring_free[ADA_SLOTS[k % 3]], 1)
        for c in (2, 3, 4):
            pe.drain().then_inc(m.ring_free[c], 1)
        layer_end(nc, pe, m, L)


def first_scalar(nc, act, m):
    s = m.s
    a = nc.scalar.activation
    act.wait_ge(m.x_in, 16 * 6)
    a(m.cc[:], m.cc[:], ACT.Silu).then_inc(m.c_act, 1)
    act.wait_ge(m.eps_set, 1)
    with act.Fori(0, DEPTH) as L:
        norm_act(nc, act, m, s["std"])
        for g in range(0, TILES * N_IN, 2):
            act.wait_ge(s["z_ps"], g + 1)
            a(m.z[:, g % 2, Z_ORDER[g // 2] * ZC:(Z_ORDER[g // 2] + 1) * ZC], m.ps[:, 4 + g % 4, 0:ZC], ACT.Copy).then_inc(s["z_act"], 1)

        def evac(b, out, src):
            act.wait_ge(s["prep_ps"], b + 1)
            return a(out, src, ACT.Copy)

        def qk(b, at, count, rows):
            src = banks(m, prep_bank(b), 2)[0:rows, 0:count * SEQ].rearrange("p (s t) -> p s t", t=SEQ)
            evac(b, m.qkT[0:rows, at:at + count, :], src).then_inc(s["prep_ev"], 1)

        qk(0, T_QRAW, 4, HD)
        qk(1, T_KC, 2, HD)
        evac(2, m.uT[:, :, 3:], m.ps[:, 4, :].rearrange("p (c t) -> p c t", c=2))
        evac(2, m.posT[:], m.ps[0:HD, 5, 0:2 * CMP_LEN].rearrange("p (w l) -> p w l", w=2)).then_inc(s["prep_ev"], 1)
        act.wait_ge(s["gate_abs"], 1)
        a(m.grow[0:NH, 2, :], m.grow[0:NH, 2, :], ACT.Exp, scale=-1.0)
        act.wait_ge(s["lam_in"], 1)
        a(m.lam[:, 2:4], m.lam[:, 0:2], ACT.Exp).then_inc(s["lam_exp"], 1)
        act.drain()
        a(m.grow[0:NH, 3, :], m.grow[0:NH, 2, :], ACT.Ln, bias=m.eps[0:NH, 1:2]).then_inc(s["gate_ln"], 1)
        qk(3, T_QROT, 4, HD)
        qk(4, T_KS, 2, HD)
        qk(5, T_DQ, 4, HD)
        qk(6, T_DK, 4, HD)
        for b in range(4):
            qk(7 + b, T_BQ + 4 * b, 4, 32)
        act.wait_ge(s["conv"], 1)
        a(m.ucT, m.ucT, ACT.Silu).then_inc(s["uc"], 1)
        act.wait_ge(s["z_dve"], N_IN)
        a(m.gates[:], m.z[:, :, Z_G:Z_G + 12], ACT.Sigmoid)
        a(m.z[:, :, Z_O:Z_O + GW], m.z[:, :, Z_O:Z_O + GW], ACT.Sigmoid).then_inc(s["small_ready"], 1)
        for b, col in ((11, Z_BQ), (12, Z_DQ)):
            evac(b, m.z[0:HD, :, col:col + 2 * SEQ], banks(m, prep_bank(b), 2)[0:HD, :].rearrange("p (i c) -> p i c", i=TILES)).then_inc(s["prep_ev"], 1)
        evac(13, m.kcT[:, 0:N_CMP], m.ps[0:HD, 2, 0:N_CMP])
        evac(13, m.vc[0:N_CMP, :], m.ps[0:N_CMP, 3, 0:HD]).then_inc(s["prep_ev"], 1)
        evac(14, m.rb.rearrange("p h k -> p (h k)"), banks(m, 4, 2)).then_inc(s["prep_ev"], 1)
        act.wait_ge(s["gate_cols"], 1)
        a(m.em, m.ps[:, 6, 8:16].rearrange("p (i h) -> p i h", i=TILES), ACT.Exp, scale=-1.0).then_inc(s["prep_ev"], 1)

        n = len(UNITS)
        for k in range(n + 1):
            if k < n:
                kind, t, hp = UNITS[k]
                nk = keys_of(kind, t)
                act.wait_ge(s["masked"], k + 1)
                if k >= 2:
                    act.wait_ge(s["pt_ps"], k - 1)
                scale = 1.0 if kind == "mlstm" else 32 ** -0.5 if kind == "diff" else HD ** -0.5
                for h in range(4):
                    bias = m.nM[:, t, h:h + 1] if kind == "mlstm" else m.nmx[k % 2][:, h:h + 1]
                    last = a(m.pr[:, k % 2, h, 0:nk], m.sm[:, k % 2, h, 0:nk], ACT.Exp, bias=bias, scale=scale,
                             accum_out=m.zs[k % 2][:, h:h + 1])
                act.drain().then_inc(s["exps"], 1)
            if k >= 1:
                u = k - 1
                kind, t, hp = UNITS[u]
                act.wait_ge(s["pt_ps"], u + 1)
                if u >= 1:
                    act.wait_ge(s["pv"], u)
                pt = banks(m, 4, 2).rearrange("p (h t q) -> p h t q", h=4, t=2)
                if kind == "cmp":
                    last = a(m.pt[0:N_CMP, :, 0, :], pt[0:N_CMP, :, 0, :], ACT.Copy)
                elif kind == "diff":
                    for h in (0, 2):
                        last = a(m.pt[:, h, 0:t + 1, :], pt[:, h, 0:t + 1, :], ACT.Copy)
                else:
                    last = a(m.pt[:, :, 0:t + 1, :], pt[:, :, 0:t + 1, :], ACT.Copy)
                last.then_inc(s["pt"], 1)
        act.wait_ge(s["ss"], 1)
        a(m.sstd, m.sso, ACT.Sqrt, scale=1.0 / HD, bias=m.eps[:, 0:1]).then_inc(s["o_std"], 1)
        act.wait_ge(s["x_mid"], 1)
        norm_act(nc, act, m, s["std_b"])
        def ada_row(k):
            act.wait_ge(s["ada_ps"], k + 1)
            if k >= 2:
                act.wait_ge(s[f"ada_out{k % 2}"], 16 * (k // 2))
            a(m.mrow[:, k % 2, :], m.ps[:, 2 + k % 2, 0:P], ACT.Copy)
            act.drain().then_inc(s["ada_row"], 1)
            act.dma_start(m.mods[L][k * 512:(k + 1) * 512].rearrange("(g c) -> g c", g=4), m.mrow[0:P:32, k % 2, :]).then_inc(s[f"ada_out{k % 2}"], 16)

        for g in range(2 * N_FU):
            act.wait_ge(s["gu"], g + 1)
            if g >= 2:
                act.wait_ge(s["hid"], g - 1)
            a(m.uT[:, g % 2, 0:SEQ], m.ps[:, g % 2, 0:SEQ], ACT.Silu).then_inc(s["silu"], 1)
            if g % 2 == 1 and g >= 3:
                for k in ADA_AFTER[g // 2 - 1]:
                    ada_row(k)
        for x in range(2):
            act.wait_ge(s[f"ada_out{x}"], 16 * N_ADA // 2)
        layer_end(nc, act, m, L)


def first_vector(nc, dve, m):
    s = m.s
    v = nc.vector
    tt, ts, stt = v.tensor_tensor, v.tensor_scalar, v.scalar_tensor_tensor
    dve.wait_ge(m.x_in, 16 * 6)
    v.memset(m.eps[:, 0:1], EPS)
    v.memset(m.eps[:, 1:2], 1.0).then_inc(m.eps_set, 1)
    dve.wait_ge(m.c_act, 1)
    v.tensor_copy(m.c32[:], bcast(m.cc[:].unsqueeze(2), [P, KC, 32])).then_inc(m.c_set, 1)
    with dve.Fori(0, DEPTH) as L:
        norm_dve(nc, dve, m, s["std"], s["hn"])
        v.tensor_copy(m.g_mix[:], m.gains[:, 0, L, :])
        v.tensor_copy(m.g_ffn[:], m.gains[:, 1, L, :])
        dve.drain()
        evacuate_dve(nc, dve, m, m.g_mix, s["tr"], s["hT"])
        for g in range(1, TILES * N_IN, 2):
            dve.wait_ge(s["z_ps"], g + 1)
            v.tensor_copy(m.z[:, 1, Z_ORDER[g // 2] * ZC:(Z_ORDER[g // 2] + 1) * ZC], m.ps[:, 4 + g % 4, 0:ZC]).then_inc(s["z_dve"], 1)
        dve.wait_ge(s["z_act"], N_IN)
        dve.drain()
        dve.wait_ge(m.consts_in, 16 * m.n_consts)
        dve.wait_ge(m.params, (L + 1) * 16 * N_PARAMS)
        rotate(v, dve, m, lambda i: [(m.z[:, i, Z_Q:Z_Q + GW].rearrange("p (h d) -> p h d", d=HD), R_Q, 4, HD),
                                     (m.z[:, i, Z_KS:Z_KS + 256].rearrange("p (h d) -> p h d", d=128)[:, :, 0:HD], R_K, 2, HD),
                                     (m.z[:, i, Z_DQ:Z_DQ + 512].rearrange("p (h d) -> p h d", d=HD), R_D, 8, HD)]).then_inc(s["rope"], 1)
        g = m.grow
        dve.wait_ge(s["prep_ps"], 2)
        ts(g[0:NH, 0, :], m.ps[0:NH, 3, 0:SEQ], m.gate_b[:, 0:1], None, ALU.add)
        ts(g[0:NH, 1, :], m.ps[0:NH, 3, SEQ:2 * SEQ], m.gate_b[:, 1:2], None, ALU.add).then_inc(s["gates_in"], 1)
        dve.drain()
        stt(g[0:NH, 2, :], g[0:NH, 1, :], -1.0, g[0:NH, 1, :], ALU.mult, ALU.max).then_inc(s["gate_abs"], 1)
        lv = m.tmp[:, 0:64].rearrange("p (w c) -> p w c", w=2)
        pairs = m.lamv[:].rearrange("p (w c) d -> p w c d", w=2)
        dve.drain()
        tt(lv, pairs[:, :, 0, :], pairs[:, :, 1, :], ALU.mult)
        dve.drain()
        v.reduce_sum(m.lam[:, 0:2], lv, axis=AX).then_inc(s["lam_in"], 1)
        dve.wait_ge(s["prep_ev"], 3)
        for c in range(2):
            ts(m.ucT[:, c, :], m.uT[:, c, 0:SEQ], m.conv_w[:, c, 0:1], m.conv_b[:, c:c + 1], ALU.mult, ALU.add)
        for k in range(1, 4):
            dve.drain()
            for c in range(2):
                last = stt(m.ucT[:, c, :], m.uT[:, c, k:k + SEQ], m.conv_w[:, c, k:k + 1], m.ucT[:, c, :], ALU.mult, ALU.add)
        last.then_inc(s["conv"], 1)
        dve.wait_ge(s["rope_b"], 1)
        for w in range(2):
            for lh in range(2):
                src = m.qkT[0:HD, T_KC + w, 16 * lh:16 * lh + 240].rearrange("d (n l) -> d l n", l=16)
                last = tt(m.blocks[:, w, 16 * lh:16 * lh + 16, :], src,
                          bcast(m.posT[:, w, 16 * lh:16 * lh + 16].unsqueeze(2), [HD, 16, N_CMP]), ALU.add)
        last.then_inc(s["blocks"], 1)
        dve.wait_ge(s["lam_exp"], 1)
        tt(m.lam[:, 4:5], m.lam[:, 3:4], m.lam[:, 2:3], ALU.subtract)
        v.memset(g[0:NH, 7, :], 0.0)
        dve.wait_ge(s["gate_ln"], 1)
        stt(g[0:NH, 3, :], g[0:NH, 1, :], 0.0, g[0:NH, 3, :], ALU.min, ALU.subtract)
        dve.drain()
        tt(m.lam[:, 5:6], m.lam[:, 4:5], m.lam_init[:, 0:1], ALU.subtract)
        v.tensor_tensor_scan(out=g[0:NH, 2, :], data0=g[0:NH, 3, :], data1=g[0:NH, 7, :], initial=0.0, op0=ALU.add, op1=ALU.add)
        dve.drain()
        tt(g[0:NH, 6, :], g[0:NH, 0, :], g[0:NH, 2, :], ALU.subtract)
        dve.drain()
        v.tensor_tensor_scan(out=g[0:NH, 4, :], data0=g[0:NH, 6, :], data1=g[0:NH, 6, :], initial=0.0, op0=ALU.max, op1=ALU.max)
        dve.drain()
        tt(g[0:NH, 5, :], g[0:NH, 4, :], g[0:NH, 2, :], ALU.add).then_inc(s["gate_rows"], 1)
        dve.wait_ge(s["prep_ps"], N_PREP)
        ts(m.nM, m.ps[:, 6, 0:8].rearrange("p (i h) -> p i h", i=TILES), -1.0, None, ALU.mult).then_inc(s["gate_cols"], 1)
        dve.wait_ge(s["prep_ev"], N_PREP)
        dve.wait_ge(s["small_ready"], 1)

        n = len(UNITS)
        for k in range(n + 3):
            if k < n:
                kind, t, hp = UNITS[k]
                nk = keys_of(kind, t)
                b = k % 2
                dve.wait_ge(s["scores"], k + 1)
                if k >= 2:
                    dve.wait_ge(s["exps"], k - 1)
                mask = {"cmp": m.cmp_mask, "dil": m.dil_mask}.get(kind, m.causal)[:, t, 0:nk]
                sm = m.sm[:, b, :, 0:nk]
                src = m.rb[:, :, 0:nk] if kind == "mlstm" else scores_of(m, k)
                if kind == "mlstm":
                    dve.drain()
                last = tt(sm, src, bcast(mask.unsqueeze(1), [P, 4, nk]), ALU.add)
                if kind != "mlstm":
                    dve.drain()
                    v.reduce_max(m.mx[b], sm, axis=AX)
                    dve.drain()
                    last = ts(m.nmx[b], m.mx[b], -(32 ** -0.5 if kind == "diff" else HD ** -0.5), None, ALU.mult)
                last.then_inc(s["masked"], 1)
            if 1 <= k <= n:
                u = k - 1
                kind, t, hp = UNITS[u]
                nk = keys_of(kind, t)
                b = u % 2
                pr, zs, rs = m.pr[:, b, :, 0:nk], m.zs[b], m.rs[b]
                dve.wait_ge(s["exps"], u + 1)
                if kind in ("slc", "win"):
                    v.reciprocal(rs, zs)
                    dve.drain()
                    br = 1 if kind == "slc" else 2
                    last = tt(rs, rs, m.gates[:, t, 4 * br:4 * br + 4], ALU.mult)
                elif kind in ("dil", "cmp"):
                    w = (m.dil_counts if kind == "dil" else m.cmp_seen)[:, t, 0:nk]
                    tt(pr, pr, bcast(w.unsqueeze(1), [P, 4, nk]), ALU.mult)
                    dve.drain()
                    v.reduce_sum(zs, pr, axis=AX)
                    dve.drain()
                    if kind == "cmp":
                        ts(zs, zs, 1e-30, None, ALU.max)
                        dve.drain()
                    last = v.reciprocal(rs, zs)
                    if kind == "cmp":
                        dve.drain()
                        last = tt(rs, rs, m.gates[:, t, 0:4], ALU.mult)
                elif kind == "diff":
                    v.reciprocal(rs, zs)
                    dve.drain()
                    odd = rs.rearrange("p (h c) -> p h c", c=2)[:, :, 1]
                    ts(odd, odd, m.lam[:, 5:6], None, ALU.mult)
                    for h in (0, 2):
                        ts(pr[:, h, :], pr[:, h, :], rs[:, h:h + 1], None, ALU.mult)
                    dve.drain()
                    for h in (0, 2):
                        last = stt(pr[:, h, :], pr[:, h + 1, :], rs[:, h + 1:h + 2], pr[:, h, :], ALU.mult, ALU.add)
                else:
                    for h in range(4):
                        stt(pr[:, h, :], scores_of(m, u)[:, h, :], HD ** -0.5, pr[:, h, :], ALU.mult, ALU.mult)
                    dve.drain()
                    v.reduce_sum(zs, pr, axis=AX)
                    dve.drain()
                    stt(zs, zs, -1.0, zs, ALU.mult, ALU.max)
                    dve.drain()
                    tt(zs, zs, m.em[:, t, :], ALU.max)
                    dve.drain()
                    last = v.reciprocal(rs, zs)
                last.then_inc(s["probs"], 1)
            if 2 <= k <= n + 1:
                u = k - 2
                kind, t, hp = UNITS[u]
                b = u % 2
                dve.wait_ge(s["pv"], u + 1)
                src = m.ps[:, 6 + b, 0:GW]
                src4 = src.rearrange("p (h d) -> p h d", d=HD)
                scale = bcast(m.rs[b].unsqueeze(2), [P, 4, HD])
                cols = {"slc": 0, "win": 0, "cmp": 0, "dil": 768, "mlstm": 512, "diff": 256 + 128 * hp}[kind]
                if kind == "diff":
                    last = v.tensor_copy(m.O[:, t, cols:cols + 128], src[:, 0:128])
                else:
                    o4 = m.O[:, t, cols:cols + GW].rearrange("p (h d) -> p h d", d=HD)
                    if kind in ("win", "cmp"):
                        tmp = m.ucT[:, 0, :].rearrange("p (h d) -> p h d", d=HD)
                        dve.drain()
                        tt(tmp, src4, scale, ALU.mult)
                        dve.drain()
                        last = tt(o4, o4, tmp, ALU.add)
                    else:
                        last = tt(o4, src4, scale, ALU.mult)
                last.then_inc(s["o_done"], 1)
        sub = m.O[:, :, GW:3 * GW]
        sq = m.hT[:].rearrange("p j t -> p (j t)")[:, 0:4 * GW].rearrange("p (i c) -> p i c", i=TILES)
        dve.drain()
        tt(sq, sub, sub, ALU.mult)
        dve.drain()
        v.reduce_sum(m.sso, sq.rearrange("p i (h d) -> p i h d", d=HD), axis=AX).then_inc(s["ss"], 1)
        dve.wait_ge(s["o_std"], 1)
        v.reciprocal(m.srec, m.sstd)
        dve.drain()
        ts(m.srec[:, :, 0:4], m.srec[:, :, 0:4], m.lam_init[:, 1:2], None, ALU.mult)
        dve.drain()
        for i in range(TILES):
            tt(sub[:, i, :].rearrange("p (h d) -> p h d", d=HD), sub[:, i, :].rearrange("p (h d) -> p h d", d=HD),
               bcast(m.srec[:, i, :].unsqueeze(2), [P, 8, HD]), ALU.mult)
        dve.drain()
        tt(sub, sub, bcast(m.g_sub.unsqueeze(1), [P, TILES, 2 * GW]), ALU.mult)
        dve.drain()
        tt(m.O[:, :, 2 * GW:3 * GW], m.O[:, :, 2 * GW:3 * GW], m.z[:, :, Z_O:Z_O + GW], ALU.mult).then_inc(s["o_final"], 1)
        evacuate_dve(nc, dve, m, None, s["tr_o"], s["OT"])
        for c in range(2):
            for i in range(TILES):
                dve.wait_ge(s["y_ps"], 2 * c + i + 1)
                part = m.x[:, i, c * 512:(c + 1) * 512]
                last = tt(part, m.ps[:, 4 + 2 * c + i, :], part, ALU.add)
        last.then_inc(s["x_mid"], 1)
        norm_dve(nc, dve, m, s["std_b"], s["hn_b"])
        evacuate_dve(nc, dve, m, m.g_ffn, s["tr_b"], s["hT_b"])
        for g2 in range(2 * N_FU):
            dve.wait_ge(s["silu"], g2 + 1)
            if g2 >= 2:
                dve.wait_ge(s["down"], g2 - 1)
            tt(m.ucT[:, g2 % 2, :], m.ps[:, g2 % 2, SEQ:2 * SEQ], m.uT[:, g2 % 2, 0:SEQ], ALU.mult).then_inc(s["hid"], 1)
        dve.wait_ge(s["down"], 2 * N_FU)
        for i in range(TILES):
            for c in range(2):
                part = m.x[:, i, c * 512:(c + 1) * 512]
                tt(part, m.ps[:, 4 + 2 * i + c, :], part, ALU.add)
        v.memset(m.uT[:, :, 0:3], 0.0)
        dve.drain()
        layer_end_leader(nc, dve, m)



T = 64
N_EXP, N_GRP, PER_GRP = 32, 4, 8
N_PAIRS = N_EXP // 2
K_A, K_B = 31, 3
PAD = K_A - 1
V_DW, V_BDW, V_LG, V_LB, V_BA, V_BG, V_DWB, N_V = 0, 31, 32, 33, 34, 35, 36, 39

SECOND_SEMS = ["std2", "hn2", "vec_ps", "vec", "x_new", "h_ready", "tr2", "hT2", "ag", "sig", "glu",
               "diag", "diag_used", "dw_ps", "v_ready", "back_ps", "ln_var", "ln_std", "ln_x", "tr3", "silu_T", "y2", "var3", "std3",
               "router_ps", "gmaxed", "gexp", "emaxed", "eexp", "routed", "pos_ps", "rounds", "zeros",
               "gsel", "gw", "xg_ps", "xg", "comb", "acc", "esilu", "ehid", "hidT_ps", "hidT", "gwt_ps", "gwt", "ye", "arrive2"]


def ring_plan():
    plan = []

    def add(what, *slots):
        for k, slot in enumerate(slots):
            plan.append((what, k, slot))
    add("a_in", 0, 1, 5, 4)
    add("a_out", 2, 3)
    add("moe0", *range(N_SLOTS))
    add("b_in", *range(N_SLOTS))
    add("b_out", 0, 1)
    add("moe1", *range(N_SLOTS))
    return plan


def ring_counts():
    loads = [4 if c in (0, 1, 5) else 2 for c in range(N_SLOTS)]
    frees = [6 if c in (0, 1, 5) else 2 for c in range(N_SLOTS)]
    out = {}
    for what, k, slot in ring_plan():
        frees_needed = frees[slot] + 1
        frees[slot] += 1
        if not what.startswith("moe"):
            loads[slot] += 1
        out[what, k] = (slot, frees_needed, 16 * loads[slot])
    return out


RING = ring_counts()


CONV_GROUPS = {1: (0, 1), 7: (3, 4, 5)}
POOL_CHUNKS = (2,)
PE_CHUNKS = (6, 7)
DIAGS = 4


def place_second(nc, m):
    sb = nc.alloc_sbuf_tensor
    m.before = sb("before", [P, P], F32)
    m.ones = sb("ones", [P, P], F32)
    m.iota64 = sb("iota64", [P, T], F32)
    m.rounds_i = sb("rounds_i", [1, 1], mybir.dt.int32)
    m.stat = sb("stat", [P, 64], F32)
    m.cur = sb("cur", [P, 2, TILES, 2], F32)
    q = m.qkT[:].rearrange("p s t -> p (s t)")
    m.mix_mod = q[:, 0:3072].rearrange("p (k d) -> p k d", k=3)
    m.upad = q[:, 3072:3072 + KC * (SEQ + PAD)].rearrange("p (j t) -> p j t", j=KC)
    m.cvT = q[:, 5360:7408].rearrange("p (j t) -> p j t", j=KC)
    m.sg2 = q[:, 7408:8432].rearrange("p (b t) -> p b t", b=4)
    m.pool_tap = q[:, 8432:8432 + 2 * SEQ].rearrange("p (b t) -> p b t", b=2)
    m.xg = q[:, 3072:4096].rearrange("p (j s) -> p j s", j=KC)
    m.G = q[:, 4096:4352].rearrange("p (g s) -> p g s", s=T)
    m.Gw = q[:, 4352:4608].rearrange("p (g s) -> p g s", s=T)
    m.GwT = q[:, 4608:4864].rearrange("p (i t) -> p i t", i=TILES)
    m.ye = q[:, 4864:5888]
    m.hid2 = q[:, 5888:6400]
    m.sgx = q[:, 6400:6912]
    m.hidT = m.hT[:].rearrange("p j t -> p (j t)")[:, 0:512].rearrange("p (c s) -> p c s", c=4)
    m.yacc = q[:, 6912:8960].rearrange("p (i d) -> p i d", i=TILES)
    z = m.z[:].rearrange("p i c -> p (i c)")
    m.diag = m.O[:].rearrange("p i d -> p (i d)").rearrange("p (g c) -> p g c", c=P)
    m.rows = [z[:, k * D:(k + 1) * D] for k in range(3)]
    m.prm = z[0:N_V, 3072:4096]
    m.vec = z[:, 4096:4096 + KC * N_V].rearrange("p (j v) -> p j v", j=KC)
    m.mix_ln = z[:, 0:2 * D].rearrange("p (k d) -> p k d", k=2)
    m.exp_mod = m.late[:, 0:3 * D].rearrange("p (k d) -> p k d", k=3)
    m.final_g = z[:, 4408:4408 + D]
    m.exp_ln = [m.late[:, 3 * D:4 * D], m.final_g]
    m.r_w = [z[:, at:at + KC * 36].rearrange("p (j e) -> p j e", j=KC) for at in (5440, 3072)]
    m.r_b = [z[:, at:at + 36] for at in (5728, 3360)]
    r = m.rows[2]
    def tile(at, n):
        return r[:, at:at + TILES * n].rearrange("p (i e) -> p i e", i=TILES)
    m.lg, m.geq, m.gcs, m.gfirst, m.gex = tile(0, 36), tile(72, 4), tile(80, 4), tile(88, 4), tile(96, 4)
    m.lm, m.eq, m.cs, m.first1, m.first2 = tile(112, 32), tile(176, 32), tile(240, 32), tile(304, 32), tile(368, 32)
    m.zero32 = r[:, 432:464]
    m.A, m.W, m.posm = tile(496, 32), tile(560, 32), tile(624, 32)
    m.w1t = tile(688, 32)


def second_sems(nc, m):
    sem = nc.alloc_semaphore
    m.t = {name: sem(name) for name in SECOND_SEMS}
    m.second_range = range(m.t["std2"].num, m.t["arrive2"].num + 1)
    assert len(m.second_range) == len(SECOND_SEMS)
    m.x_out = sem("x_out")
    m.rounds_set = [sem(f"rounds_set{l}") for l in range(DEPTH)]
    m.rel2, m.rows_in = sem("rel2"), sem("rows_in")
    m.e_full = [[sem(f"e_full{l}_{c}") for c in range(6)] for l in range(DEPTH)]
    m.e_used = [[sem(f"e_used{l}_{c}") for c in range(3)] for l in range(DEPTH)]


def phase_end(eng, m, k):
    eng.drain().then_inc(m.t["arrive2"], 1)
    eng.wait_ge(m.rel2, k)
    eng.sem_inc(m.seen, 1)


def phase_end_leader(dve, m):
    dve.wait_ge(m.t["arrive2"], 3)
    dve.sem_clear(m.second_range)
    dve.sem_inc(m.rel2, 1)


ROW_LOADS = [1, 10, 7, 3, 7]


def rows_count(phase):
    return 16 * sum(ROW_LOADS[:phase + 1])


def rows_loader(pool, m):
    def load(dst, src):
        pool.dma_start(dst, src).then_inc(m.rows_in, 16)
    return load


def second_rows(nc, pool, m, a):
    load = rows_loader(pool, m)
    load(m.final_g, a["norm_final"].partition_broadcast(P))
    load(m.prm[V_DWB:N_V, :], a["b_w_dw_2"][0])
    load(m.prm[V_DW:V_DW + K_A, :], a["a_w_dw_2"][0])
    load(m.prm[V_BDW:V_BDW + 1, :], a["a_b_dw_2"])
    load(m.prm[V_LG:V_LG + 1, :], a["a_ln_g_2"])
    load(m.prm[V_LB:V_LB + 1, :], a["a_ln_b_2"])
    load(m.prm[V_BA:V_BA + 2, :], a["a_b_in_2"][0].rearrange("(h d) -> h d", h=2))
    load(m.rows[2], a["a_b_out_2"][0].partition_broadcast(P))
    load(m.mix_ln[:, 0, :], a["mix_ln_g_2"][0].partition_broadcast(P))
    load(m.mix_ln[:, 1, :], a["mix_ln_b_2"][0].partition_broadcast(P))
    load(m.mix_mod.rearrange("p k d -> p (k d)"), m.mods[0][0:3 * D].partition_broadcast(P))


def second_pool(nc, pool, m, a):
    load = rows_loader(pool, m)

    def expert_rows(l):
        load(m.exp_mod.rearrange("p k d -> p (k d)"), m.mods[l][3 * D:6 * D].partition_broadcast(P))
        load(m.r_w[l][:, :, 0:N_GRP], a["r_w_group_2"][l].rearrange("(p j) e -> p j e", j=KC))
        load(m.r_w[l][:, :, N_GRP:], a["r_w_expert_2"][l].rearrange("(p j) e -> p j e", j=KC))
        load(m.r_b[l][:, 0:N_GRP], a["r_b_group_2"][l].partition_broadcast(P))
        load(m.r_b[l][:, N_GRP:], a["r_b_expert_2"][l].partition_broadcast(P))
        load(m.exp_ln[0], a["ffn_ln_g_2"][l].partition_broadcast(P))
        load(m.exp_ln[1], a["ffn_ln_b_2"][l].partition_broadcast(P))

    phase_end(pool, m, 1)
    for l in range(DEPTH):
        expert_rows(l)
        if l == 0:
            for c in POOL_CHUNKS:
                pool.wait_ge(m.t["glu"], c + 1)
                for k in range(K_A):
                    if k <= 1:
                        pool.drain()
                    w = m.vec[:, c, V_DW + k:V_DW + k + 1]
                    src = m.upad[:, c, k:k + SEQ]
                    if k == 0:
                        nc.gpsimd.tensor_scalar(m.cvT[:, c, :], src, w, m.vec[:, c, V_BDW:V_BDW + 1], ALU.mult, ALU.add)
                    else:
                        nc.gpsimd.tensor_scalar(m.pool_tap[:, k % 2, :], src, w, None, ALU.mult)
                        pool.drain()
                        last = nc.gpsimd.tensor_tensor(m.cvT[:, c, :], m.cvT[:, c, :], m.pool_tap[:, k % 2, :], ALU.add)
                last.then_inc(m.t["v_ready"], 1)
        phase_end(pool, m, 2 + 2 * l)
        nc.gpsimd.memset(m.yacc, 0.0)
        nc.gpsimd.memset(m.ye, 0.0)
        nc.gpsimd.memset(m.GwT, 0.0)
        pool.drain().then_inc(m.t["zeros"], 1)
        if l == 0:
            load(m.mix_mod.rearrange("p k d -> p (k d)"), m.mods[1][0:3 * D].partition_broadcast(P))
            load(m.mix_ln[:, 0, :], a["mix_ln_g_2"][1].partition_broadcast(P))
            load(m.mix_ln[:, 1, :], a["mix_ln_b_2"][1].partition_broadcast(P))
        phase_end(pool, m, 3 + 2 * l)


def expert_load(sp, m, a, l, e, c):
    src = [a["e_w_gate_2"], a["e_w_up_2"], a["e_w_down_2"]][c % 3][l]
    return src[e].rearrange("(p j) n -> p (j n)", p=P)


def second_sync(nc, sp, m, a, out):
    def load(what, k, src, three=True):
        slot, frees, _ = RING[what, k]
        sp.wait_ge(m.ring_free[slot], frees)
        dst = m.slot[slot].rearrange("p (j n) -> p j n", j=KC) if three else m.slot[slot]
        sp.dma_start(dst, src).then_inc(m.ring_full[slot], 16)

    def halves(what, w, order, rows):
        w = w.rearrange(rows, j=KC)
        for k, at in enumerate(order):
            load(what, k, w[:, :, at:at + 512])

    def experts(l):
        full = m.e_full[l]
        for c in ((0, 2, 1), (1, 2, 0))[l]:
            for x in range(2):
                slot, frees, _ = RING[f"moe{l}", 2 * c + x]
                assert slot == 2 * c + x
                sp.wait_ge(m.ring_free[slot], frees)
                sp.dma_start(m.slot[slot], expert_load(sp, m, a, l, x, c)).then_inc(full[slot], 16)

        def pairs(r, first=0):
            with sp.Fori(first, N_PAIRS) as p:
                it = r * N_PAIRS + p
                for c in range(3):
                    sp.wait_ge(m.e_used[l][c], it + 1)
                    for x in range(2):
                        sp.dma_start(m.slot[2 * c + x], expert_load(sp, m, a, l, p * 2 + x, c)).then_inc(full[2 * c + x], 16)
        pairs(0, 1)
        sp.wait_ge(m.rounds_set[l], 1)
        rounds = sp.value_load(m.rounds_i[0:1, 0:1], min_val=1, max_val=4)
        with sp.If(rounds > 1):
            with sp.Fori(1, rounds) as r:
                pairs(r)

    halves("a_in", a["a_w_in_2"][0], (0, D, 512, D + 512), "(p j) n -> p j n")
    halves("a_out", a["a_w_out_2"][0], (0, 512), "(j p) n -> p j n")
    experts(0)
    halves("b_in", a["b_w_in_2"][0], (0, D, 2 * D, 512, D + 512, 2 * D + 512), "(p j) n -> p j n")
    halves("b_out", a["b_w_out_2"][0], (0, 512), "(j p) n -> p j n")
    experts(1)
    for i in range(TILES):
        sp.wait_ge(m.x_out, 1)
        sp.dma_start(out[0, i * P:(i + 1) * P, :], m.x[:, i, :]).then_inc(m.stored, 16)
    sp.wait_ge(m.stored, 16 * TILES)


def second_tensor(nc, pe, m):
    t = m.t
    mm = nc.tensor.matmul

    def full(what, k):
        slot, _, count = RING[what, k]
        pe.wait_ge(m.ring_full[slot], count)
        return slot, m.slot[slot].rearrange("p (j n) -> p j n", j=KC)

    def free(slot):
        pe.drain().then_inc(m.ring_free[slot], 1)

    phase_end(pe, m, 1)

    for l in range(DEPTH):
        if l == 0:
            pe.wait_ge(m.rows_in, rows_count(1))
            for j in range(KC):
                last = nc.tensor.transpose(m.ps[:, 7, j * N_V:(j + 1) * N_V], m.prm[:, j * P:(j + 1) * P], m.ident[0:N_V, 0:N_V])
            last.then_inc(t["vec_ps"], 1)
        transpose_pe(nc, pe, m, t["hn2"], TILES, t["tr2"])
        pe.wait_ge(t["hT2"], KC)
        if l == 0:
            pe.wait_ge(t["vec"], 1)
            w = [full("a_in", k)[1] for k in range(2)]
            for c in range(KC):
                if c == 4:
                    for k in (0, 1):
                        free(RING["a_in", k][0])
                    w = [full("a_in", k)[1] for k in (2, 3)]
                if c >= 4:
                    pe.wait_ge(t["glu"], c - 3)
                at = (c % 4) * P
                for half in range(2):
                    for j in range(KC):
                        last = mm(m.ps[:, c % 4, half * SEQ:(half + 1) * SEQ], w[half][:, j, at:at + P], m.hT[:, j, :], start=(j == 0), stop=(j == KC - 1))
                last.then_inc(t["ag"], 1)
            for k in (2, 3):
                free(RING["a_in", k][0])
            pe.wait_ge(t["glu"], KC)
            for n, c in enumerate(PE_CHUNKS):
                for k in range(K_A):
                    g = n * K_A + k
                    if g % DIAGS == 0:
                        pe.wait_ge(t["diag"], g // DIAGS + 1)
                    last = mm(m.ps[:, 4 + n, 0:SEQ], m.diag[:, g % (4 * DIAGS), :], m.upad[:, c, k:k + SEQ], start=(k == 0), stop=(k == K_A - 1))
                    if g % DIAGS == DIAGS - 1:
                        last.then_inc(t["diag_used"], 1)
                last.then_inc(t["dw_ps"], 1)
            pe.wait_ge(t["v_ready"], KC)
            for i in range(TILES):
                for c in range(KC):
                    dst = m.ps[:, 4 + 2 * i + c // 4, (c % 4) * P:(c % 4 + 1) * P]
                    last = nc.tensor.transpose(dst, m.cvT[:, c, i * P:(i + 1) * P], m.ident[:])
                last.then_inc(t["back_ps"], 1)
            pe.wait_ge(t["ln_x"], 1)
            for c in range(KC):
                for i in range(TILES):
                    last = nc.tensor.transpose(m.ps[:, c // 2, (c % 2) * SEQ + i * P:(c % 2) * SEQ + (i + 1) * P], m.O[:, i, c * P:(c + 1) * P], m.ident[:])
                last.then_inc(t["tr3"], 1)
            pe.wait_ge(t["silu_T"], KC)
            vT, what = m.hT, "a_out"
        else:
            for c in range(KC):
                if c % 4 == 0:
                    w = [full("b_in", 3 * (c // 4) + k)[1] for k in range(3)]
                if c >= 2:
                    pe.wait_ge(t["v_ready"], c - 1)
                at = (c % 4) * P
                for half, bank in ((1, c % 2), (2, c % 2), (0, 2 + c % 2)):
                    dst = m.ps[:, bank, 0:SEQ] if half != 2 else m.ps[:, bank, SEQ:2 * SEQ]
                    for j in range(KC):
                        last = mm(dst, w[half][:, j, at:at + P], m.hT[:, j, :], start=(j == 0), stop=(j == KC - 1))
                last.then_inc(t["ag"], 1)
                if c % 4 == 3:
                    for k in range(3):
                        free(3 * (c // 4) + k)
            pe.wait_ge(t["v_ready"], KC)
            vT, what = m.cvT, "b_out"
        for n in range(2):
            slot, w = full(what, n)
            for i in range(TILES):
                for j in range(KC):
                    last = mm(m.ps[:, 4 + 2 * i + n, :], vT[:, j, i * P:(i + 1) * P], w[:, j, :], start=(j == 0), stop=(j == KC - 1))
            free(slot)
        pe.drain().then_inc(t["y2"], 1)
        phase_end(pe, m, 2 + 2 * l)

        for c in range(3):
            pe.sem_inc(m.e_used[l][c], 1)
        transpose_pe(nc, pe, m, t["hn2"], TILES, t["tr2"])
        pe.wait_ge(m.rows_in, rows_count(2 + 2 * l))
        pe.wait_ge(t["hT2"], KC)
        for i in range(TILES):
            for j in range(KC):
                last = mm(m.ps[:, 6, i * 36:(i + 1) * 36], m.hT[:, j, i * P:(i + 1) * P], m.r_w[l][:, j, :], start=(j == 0), stop=(j == KC - 1))
        last.then_inc(t["router_ps"], 1)
        pe.wait_ge(t["routed"], 1)
        mm(m.ps[:, 7, 0:32], m.before[:], m.A[:, 0, :], start=True, stop=True)
        mm(m.ps[:, 7, 32:64], m.ones[:], m.A[:, 0, :], start=True, stop=False)
        mm(m.ps[:, 7, 32:64], m.before[:], m.A[:, 1, :], start=False, stop=True)
        mm(m.ps[:, 7, 64:96], m.ones[:], m.A[:, 0, :], start=True, stop=False)
        mm(m.ps[:, 7, 64:96], m.ones[:], m.A[:, 1, :], start=False, stop=True).then_inc(t["pos_ps"], 1)
        pe.wait_ge(t["rounds"], 1)
        pe.wait_ge(t["zeros"], 1)
        rounds = pe.value_load(m.rounds_i[0:1, 0:1], min_val=1, max_val=4)
        ef = m.e_full[l]

        def combine(i):
            for n in range(2):
                last = mm(m.ps[:, 6 + n, :], m.GwT[:, i, :], m.ye[:, n * 512:(n + 1) * 512], start=True, stop=True)
            last.then_inc(t["comb"], 1)

        with pe.Fori(0, rounds) as r:
            with pe.Fori(0, N_PAIRS) as p:
                it = r * N_PAIRS + p

                def product(c, out, count, operand):
                    for x in range(2):
                        pe.wait_ge(ef[2 * c + x], it * 16 + 16)
                        if x == 0:
                            pe.sem_inc(m.seen, 1)
                    halves = 2 if c == 2 else 1
                    w = [m.slot[2 * c + x].rearrange("p (j n) -> p j n", j=count) for x in range(2)]
                    for n in range(halves):
                        for j in range(count):
                            for x in range(2):
                                last = mm(m.ps[x * T:(x + 1) * T, out + n, :], operand[:, j, x * T:(x + 1) * T], w[x][:, j, n * 512:(n + 1) * 512],
                                          start=(j == 0), stop=(j == count - 1))
                    last.then_inc(m.e_used[l][c], 1)

                pe.wait_ge(t["gsel"], it + 1)
                for j in range(KC):
                    for i in range(TILES):
                        hN = m.O[:, i, :].rearrange("t (p j) -> t j p", j=KC)[:, j, :]
                        g = m.G[:, 2 * i:2 * i + 2, :].rearrange("p x s -> p (x s)")
                        last = mm(m.ps[:, j // 4, (j % 4) * P:(j % 4 + 1) * P], hN, g, start=(i == 0), stop=(i == 1))
                last.then_inc(t["xg_ps"], 1)
                pe.wait_ge(t["ye"], it + 1)
                pe.sem_inc(m.seen, 1)
                pe.wait_ge(t["acc"], it * 2 + 1)
                combine(0)
                pe.wait_ge(t["xg"], it + 1)
                pe.sem_inc(m.seen, 1)
                product(0, 2, KC, m.xg)
                product(1, 3, KC, m.xg)
                pe.wait_ge(t["acc"], it * 2 + 2)
                combine(1)
                pe.wait_ge(t["ehid"], it + 1)
                for c in range(4):
                    src = m.hid2.rearrange("s (p c) -> s c p", c=4)[:, c, :]
                    last = nc.tensor.transpose(m.ps[:, 1, c * P:(c + 1) * P], src, m.ident[:])
                last.then_inc(t["hidT_ps"], 1)
                pe.wait_ge(t["gw"], it + 1)
                for i in range(TILES):
                    last = nc.tensor.transpose(m.ps[:, 0, i * P:(i + 1) * P], m.Gw[:, 2 * i:2 * i + 2, :].rearrange("p x s -> p (x s)"), m.ident[:])
                last.then_inc(t["gwt_ps"], 1)
                pe.wait_ge(t["hidT"], it + 1)
                pe.sem_inc(m.seen, 1)
                product(2, 4, 4, m.hidT)
        done = rounds * N_PAIRS
        for i in range(TILES):
            if i == 0:
                pe.wait_ge(t["ye"], done + 1)
                pe.sem_inc(m.seen, 1)
            pe.wait_ge(t["acc"], done * 2 + (i + 1))
            combine(i)
        for c in range(N_SLOTS):
            free(c)
        phase_end(pe, m, 3 + 2 * l)


def second_scalar(nc, act, m):
    t = m.t
    a = nc.scalar.activation

    def diagonals(group):
        for g in range(group * DIAGS, min((group + 1) * DIAGS, len(PE_CHUNKS) * K_A)):
            c, k = PE_CHUNKS[g // K_A], g % K_A
            last = a(m.diag[:, g % (4 * DIAGS), :], m.ident[:], ACT.Copy, scale=m.vec[:, c, V_DW + k:V_DW + k + 1])
        last.then_inc(t["diag"], 1)

    norm_act(nc, act, m, t["std2"])
    phase_end(act, m, 1)
    for l in range(DEPTH):
        if l == 0:
            for c in range(KC):
                act.wait_ge(t["ag"], c + 1)
                if c == 0:
                    act.wait_ge(t["vec"], 1)
                if c >= 4:
                    act.wait_ge(t["glu"], c - 3)
                a(m.sg2[:, c % 4, :], m.ps[:, c % 4, SEQ:2 * SEQ], ACT.Sigmoid, bias=m.vec[:, c, V_BG:V_BG + 1]).then_inc(t["sig"], 1)
                if c == 2:
                    act.wait_ge(t["tr2"], KC)
                    for group in range(4):
                        diagonals(group)
            for group in range(4, -(-len(PE_CHUNKS) * K_A // DIAGS)):
                act.wait_ge(t["diag_used"], group - 3)
                diagonals(group)
            for n, c in enumerate(PE_CHUNKS):
                act.wait_ge(t["dw_ps"], n + 1)
                a(m.cvT[:, c, :], m.ps[:, 4 + n, 0:SEQ], ACT.Identity, bias=m.vec[:, c, V_BDW:V_BDW + 1]).then_inc(t["v_ready"], 1)
            act.wait_ge(t["ln_var"], 1)
            a(m.stat[:, 32:34], m.stat[:, 28:32].rearrange("p (i k) -> p i k", k=2)[:, :, 1], ACT.Sqrt, bias=m.eps[:, 2:3]).then_inc(t["ln_std"], 1)
            for c in range(KC):
                act.wait_ge(t["tr3"], 2 * (c // 2) + 2)
                a(m.hT[:, c, :], m.ps[:, c // 2, (c % 2) * SEQ:(c % 2 + 1) * SEQ], ACT.Silu,
                  bias=m.vec[:, c, V_LB:V_LB + 1], scale=m.vec[:, c, V_LG:V_LG + 1]).then_inc(t["silu_T"], 1)
        else:
            for c in range(KC):
                act.wait_ge(t["ag"], c + 1)
                if c >= 2:
                    act.wait_ge(t["glu"], c - 1)
                a(m.sg2[:, c % 2, :], m.ps[:, c % 2, 0:SEQ], ACT.Copy).then_inc(t["sig"], 1)
        act.wait_ge(t["var3"], 1)
        a(m.stat[:, 32:34], m.stat[:, 28:32].rearrange("p (i k) -> p i k", k=2)[:, :, 1], ACT.Sqrt, bias=m.eps[:, 2:3]).then_inc(t["std3"], 1)
        phase_end(act, m, 2 + 2 * l)
        act.wait_ge(t["gmaxed"], 1)
        a(m.gex, m.gex, ACT.Exp).then_inc(t["gexp"], 1)
        act.wait_ge(t["emaxed"], 1)
        a(m.stat[:, 44:46], m.stat[:, 42:44], ACT.Exp).then_inc(t["eexp"], 1)
        act.wait_ge(t["rounds"], 1)
        act.wait_ge(t["zeros"], 1)
        act.sem_inc(t["ye"], 1)
        act.sem_inc(t["gwt"], 1)
        rounds = act.value_load(m.rounds_i[0:1, 0:1], min_val=1, max_val=4)
        with act.Fori(0, rounds) as r:
            with act.Fori(0, N_PAIRS) as p:
                it = r * N_PAIRS + p
                act.wait_ge(t["xg_ps"], it + 1)
                a(m.xg.rearrange("p j s -> p (j s)"), banks(m, 0, 2), ACT.Copy).then_inc(t["xg"], 1)
                act.wait_ge(m.e_used[l][0], it + 2)
                a(m.sgx, m.ps[:, 2, :], ACT.Silu).then_inc(t["esilu"], 1)
                act.wait_ge(t["hidT_ps"], it + 1)
                a(m.hidT.rearrange("p c s -> p (c s)"), m.ps[:, 1, :], ACT.Copy).then_inc(t["hidT"], 1)
                act.wait_ge(t["gwt_ps"], it + 1)
                a(m.GwT.rearrange("p i t -> p (i t)"), m.ps[:, 0, 0:256], ACT.Copy).then_inc(t["gwt"], 1)
                act.wait_ge(m.e_used[l][2], it + 2)
                a(m.ye, banks(m, 4, 2), ACT.Copy).then_inc(t["ye"], 1)
        act.wait_ge(t["var3"], 1)
        a(m.stat[:, 32:34], m.stat[:, 28:32].rearrange("p (i k) -> p i k", k=2)[:, :, 1], ACT.Sqrt, bias=m.eps[:, 2:3]).then_inc(t["std3"], 1)
        phase_end(act, m, 3 + 2 * l)


def conv_tap(v, m, c, k, row, first, bias):
    w = m.vec[:, c, row + k:row + k + 1]
    src = m.upad[:, c, first + k:first + k + SEQ]
    acc = m.cvT[:, c, :]
    if k == 0 and bias:
        return v.tensor_scalar(acc, src, w, m.vec[:, c, V_BDW:V_BDW + 1], ALU.mult, ALU.add)
    if k == 0:
        return v.tensor_scalar(acc, src, w, None, ALU.mult)
    return v.scalar_tensor_tensor(acc, src, w, acc, ALU.mult, ALU.add)


def second_vector(nc, dve, m):
    t = m.t
    v = nc.vector
    tt, ts, stt = v.tensor_tensor, v.tensor_scalar, v.scalar_tensor_tensor
    dve.wait_ge(t["std2"], 1)
    v.reciprocal(m.rstd, m.std)
    dve.drain()
    for i in range(TILES):
        ts(m.x[:, i, :], m.x[:, i, :], m.rstd[:, i:i + 1], None, ALU.mult)
    v.memset(m.eps[:, 2:3], LN_EPS)
    dve.wait_ge(m.rows_in, rows_count(0))
    dve.drain()
    tt(m.x[:], m.x[:], bcast(m.final_g.unsqueeze(1), [P, TILES, D]), ALU.mult)
    dve.drain()
    phase_end_leader(dve, m)

    def modulate(mod):
        dve.drain()
        stt(m.O[:], bcast(mod[:, 1, :].unsqueeze(1), [P, TILES, D]), 1.0, m.x[:], ALU.add, ALU.mult)
        dve.drain()
        for i in range(TILES):
            tt(m.O[:, i, :], m.O[:, i, :], mod[:, 0, :], ALU.add).then_inc(t["hn2"], 1)

    def stats(src, sem):
        for i in range(TILES):
            for n in range(2):
                v.bn_stats(m.stat[:, (2 * i + n) * 6:(2 * i + n + 1) * 6], src(i, n))
        dve.drain()
        for i in range(TILES):
            last = v.bn_aggr(m.stat[:, 28 + 2 * i:30 + 2 * i], m.stat[:, 12 * i:12 * i + 12])
        last.then_inc(sem, 1)

    def layer_norm(gain, bias):
        dve.drain()
        stats(lambda i, n: m.x[:, i, n * 512:(n + 1) * 512], t["var3"])
        dve.wait_ge(t["std3"], 1)
        v.reciprocal(m.stat[:, 34:36], m.stat[:, 32:34])
        dve.drain()
        for i in range(TILES):
            ts(m.x[:, i, :], m.x[:, i, :], m.stat[:, 28 + 2 * i:29 + 2 * i], m.stat[:, 34 + i:35 + i], ALU.subtract, ALU.mult)
        dve.drain()
        tt(m.x[:], m.x[:], bcast(gain.unsqueeze(1), [P, TILES, D]), ALU.mult)
        dve.drain()
        tt(m.x[:], m.x[:], bcast(bias.unsqueeze(1), [P, TILES, D]), ALU.add)
        dve.drain()

    def residual(y, mod):
        dve.drain()
        stt(m.O[:], bcast(mod[:, 2, :].unsqueeze(1), [P, TILES, D]), 1.0, y, ALU.add, ALU.mult)
        dve.drain()
        stt(m.x[:].rearrange("p i d -> p (i d)"), m.x[:].rearrange("p i d -> p (i d)"), ALPHA, m.O[:].rearrange("p i d -> p (i d)"), ALU.mult, ALU.add)

    for l in range(DEPTH):
        if l == 0:
            dve.wait_ge(t["vec_ps"], 1)
            v.tensor_copy(m.vec.rearrange("p j v -> p (j v)"), m.ps[:, 7, 0:KC * N_V]).then_inc(t["vec"], 1)
        dve.wait_ge(m.rows_in, rows_count(1 + 2 * l))
        modulate(m.mix_mod)
        evacuate_dve(nc, dve, m, None, t["tr2"], t["hT2"])
        v.memset(m.upad[:, :, 0:PAD], 0.0)
        for c in range(KC):
            dve.wait_ge(t["sig"], c + 1)
            u = m.upad[:, c, PAD:]
            if l == 0:
                stt(u, m.ps[:, c % 4, 0:SEQ], m.vec[:, c, V_BA:V_BA + 1], m.sg2[:, c % 4, :], ALU.add, ALU.mult).then_inc(t["glu"], 1)
                taps, first, row = K_A, 0, V_DW
            else:
                tt(u, m.ps[:, c % 2, SEQ:2 * SEQ], m.sg2[:, c % 2, :], ALU.mult).then_inc(t["glu"], 1)
                taps, first, row = K_B, PAD - (K_B - 1), V_DWB
            group = CONV_GROUPS.get(c, ()) if l == 0 else (c,)
            if not group:
                continue
            for k in range(taps):
                dve.drain()
                for cc in group:
                    last = conv_tap(v, m, cc, k, row, first, l == 0)
                    if l == 0 and k == taps - 1:
                        last.then_inc(t["v_ready"], 1)
            if l == 1:
                dve.drain()
                tt(m.cvT[:, c, :], m.ps[:, 2 + c % 2, 0:SEQ], m.cvT[:, c, :], ALU.mult).then_inc(t["v_ready"], 1)
        if l == 0:
            dve.wait_ge(t["back_ps"], TILES)
            stats(lambda i, n: m.ps[:, 4 + 2 * i + n, :], t["ln_var"])
            dve.wait_ge(t["ln_std"], 1)
            v.reciprocal(m.stat[:, 34:36], m.stat[:, 32:34])
            dve.drain()
            for i in range(TILES):
                last = ts(m.O[:, i, :], banks(m, 4 + 2 * i, 2), m.stat[:, 28 + 2 * i:29 + 2 * i], m.stat[:, 34 + i:35 + i], ALU.subtract, ALU.mult)
            last.then_inc(t["ln_x"], 1)
        dve.wait_ge(t["y2"], 1)
        for i in range(TILES):
            if l == 0:
                tt(m.O[:, i, :], banks(m, 4 + 2 * i, 2), m.rows[2], ALU.add)
            else:
                v.tensor_copy(m.O[:, i, :], banks(m, 4 + 2 * i, 2))
        residual(m.O[:], m.mix_mod)
        layer_norm(m.mix_ln[:, 0, :], m.mix_ln[:, 1, :])
        phase_end_leader(dve, m)

        dve.wait_ge(m.rows_in, rows_count(2 + 2 * l))
        modulate(m.exp_mod)
        evacuate_dve(nc, dve, m, None, t["tr2"], t["hT2"])
        dve.wait_ge(t["router_ps"], 1)
        tt(m.lg, m.ps[:, 6, 0:72].rearrange("p (i e) -> p i e", i=TILES), bcast(m.r_b[l].unsqueeze(1), [P, TILES, 36]), ALU.add)
        v.memset(m.zero32, 0.0)
        st = m.stat
        dve.drain()
        gl = m.lg[:, :, 0:N_GRP]

        def first_of(eq, cs, out, n):
            for i in range(TILES):
                v.tensor_tensor_scan(out=cs[:, i, :], data0=eq[:, i, :], data1=m.zero32[:, 0:n], initial=0.0, op0=ALU.add, op1=ALU.add)
            dve.drain()
            stt(out, cs, 1.0, eq, ALU.is_equal, ALU.mult)
            dve.drain()
        v.reduce_max(st[:, 36:38], gl, axis=AX)
        dve.drain()
        gm = bcast(st[:, 36:38].unsqueeze(2), [P, TILES, N_GRP])
        tt(m.gex, gl, gm, ALU.subtract).then_inc(t["gmaxed"], 1)
        tt(m.geq, gl, gm, ALU.is_equal)
        dve.drain()
        first_of(m.geq, m.gcs, m.gfirst, N_GRP)
        ts(m.gcs, m.gfirst, 1.0, 1e30, ALU.subtract, ALU.mult)
        for i in range(TILES):
            tt(m.lm[:, i, :].rearrange("p (g e) -> p g e", g=N_GRP), m.lg[:, i, N_GRP:].rearrange("p (g e) -> p g e", g=N_GRP),
               bcast(m.gfirst[:, i, :].unsqueeze(2), [P, N_GRP, PER_GRP]), ALU.mult)
        dve.drain()
        for i in range(TILES):
            lm = m.lm[:, i, :].rearrange("p (g e) -> p g e", g=N_GRP)
            tt(lm, lm, bcast(m.gcs[:, i, :].unsqueeze(2), [P, N_GRP, PER_GRP]), ALU.add)
        dve.drain()
        v.reduce_max(st[:, 38:40], m.lm, axis=AX)
        dve.drain()
        tt(m.eq, m.lm, bcast(st[:, 38:40].unsqueeze(2), [P, TILES, N_EXP]), ALU.is_equal)
        dve.drain()
        first_of(m.eq, m.cs, m.first1, N_EXP)
        stt(m.lm, m.first1, -2e30, m.lm, ALU.mult, ALU.add)
        dve.drain()
        v.reduce_max(st[:, 40:42], m.lm, axis=AX)
        dve.drain()
        tt(st[:, 42:44], st[:, 40:42], st[:, 38:40], ALU.subtract).then_inc(t["emaxed"], 1)
        tt(m.eq, m.lm, bcast(st[:, 40:42].unsqueeze(2), [P, TILES, N_EXP]), ALU.is_equal)
        dve.drain()
        first_of(m.eq, m.cs, m.first2, N_EXP)
        tt(m.A, m.first1, m.first2, ALU.add).then_inc(t["routed"], 1)
        dve.wait_ge(t["gexp"], 1)
        v.reduce_sum(st[:, 46:48], m.gex, axis=AX)
        dve.wait_ge(t["eexp"], 1)
        ts(st[:, 48:50], st[:, 44:46], 1.0, None, ALU.add)
        dve.drain()
        tt(st[:, 50:52], st[:, 48:50], st[:, 46:48], ALU.mult)
        dve.drain()
        v.reciprocal(st[:, 52:54], st[:, 50:52])
        dve.drain()
        tt(st[:, 54:56], st[:, 52:54], st[:, 44:46], ALU.mult)
        tt(m.w1t, m.first1, bcast(st[:, 52:54].unsqueeze(2), [P, TILES, N_EXP]), ALU.mult)
        dve.drain()
        tt(m.W, m.first2, bcast(st[:, 54:56].unsqueeze(2), [P, TILES, N_EXP]), ALU.mult)
        dve.drain()
        tt(m.W, m.W, m.w1t, ALU.add)
        dve.wait_ge(t["pos_ps"], 1)
        stt(m.posm, m.ps[:, 7, 0:64].rearrange("p (i e) -> p i e", i=TILES), 1.0, m.A, ALU.add, ALU.mult)
        v.reduce_max(st[:, 56:57], m.ps[:, 7, 64:96], axis=AX)
        dve.drain()
        ts(m.posm, m.posm, -1.0, None, ALU.add)
        for k in range(1, 4):
            ts(st[:, 56 + k:57 + k], st[:, 56:57], T * k + 0.5, None, ALU.is_gt)
        dve.drain()
        tt(st[:, 60:61], st[:, 57:58], st[:, 58:59], ALU.add)
        dve.drain()
        stt(st[:, 60:61], st[:, 60:61], 1.0, st[:, 59:60], ALU.add, ALU.add)
        dve.drain()
        v.tensor_copy(m.rounds_i[:], st[0:1, 60:61]).then_inc(t["rounds"], 1)
        dve.drain().then_inc(m.rounds_set[l], 1)
        dve.wait_ge(t["zeros"], 1)
        dve.sem_inc(t["acc"], 1)
        rounds = dve.value_load(m.rounds_i[0:1, 0:1], min_val=1, max_val=4)
        pairs = lambda ap: ap.rearrange("p i (q x) -> p i q x", x=2)
        with dve.Fori(0, rounds) as r:
            with dve.Fori(0, N_PAIRS) as p:
                it = r * N_PAIRS + p
                v.tensor_copy(m.cur[:, 0], pairs(m.posm)[:, :, p, :])
                v.tensor_copy(m.cur[:, 1], pairs(m.W)[:, :, p, :])
                dve.drain()
                dve.wait_ge(t["gwt"], it + 1)
                cur = m.cur[:].rearrange("p k i x -> p k (i x)")
                wide = [P, 4, T]
                tt(m.G, bcast(m.iota64[:].unsqueeze(1), wide), bcast(cur[:, 0, :].unsqueeze(2), wide), ALU.is_equal)
                dve.drain().then_inc(t["gsel"], 1)
                tt(m.Gw, m.G, bcast(cur[:, 1, :].unsqueeze(2), wide), ALU.mult).then_inc(t["gw"], 1)
                dve.wait_ge(t["comb"], it * 2 + 1)
                tt(m.yacc[:, 0, :], banks(m, 6, 2), m.yacc[:, 0, :], ALU.add).then_inc(t["acc"], 1)
                dve.wait_ge(t["esilu"], it + 1)
                dve.sem_inc(m.seen, 1)
                dve.wait_ge(m.e_used[l][1], it + 2)
                tt(m.hid2, m.ps[:, 3, :], m.sgx, ALU.mult).then_inc(t["ehid"], 1)
                dve.wait_ge(t["comb"], it * 2 + 2)
                tt(m.yacc[:, 1, :], banks(m, 6, 2), m.yacc[:, 1, :], ALU.add).then_inc(t["acc"], 1)
            ts(m.posm, m.posm, -float(T), None, ALU.add)
            dve.drain()
        done = rounds * N_PAIRS
        for x in range(2):
            dve.wait_ge(t["comb"], done * 2 + (x + 1))
            tt(m.yacc[:, x, :], banks(m, 6, 2), m.yacc[:, x, :], ALU.add).then_inc(t["acc"], 1)
        dve.drain()
        residual(m.yacc, m.exp_mod)
        dve.wait_ge(m.rows_in, rows_count(2 + 2 * l))
        layer_norm(*m.exp_ln)
        if l == DEPTH - 1:
            dve.drain().then_inc(m.x_out, 1)
        phase_end_leader(dve, m)


CONSTS = ["cos64", "sin64", "cos32", "sin32", "causal", "dil_mask", "dil_counts", "cmp_mask", "cmp_seen", "head_rows",
          "before", "ones", "iota64"]


def program(nc, a, out):
    m = Mem()
    place(nc, m)
    place_second(nc, m)
    sem = nc.alloc_semaphore
    m.s = {name: sem(name) for name in FIRST_SEMS}
    m.first_range = range(m.s["std"].num, m.s["arrive"].num + 1)
    assert len(m.first_range) == len(FIRST_SEMS)
    m.ring_full = [sem(f"ring_full{i}") for i in range(N_SLOTS)]
    m.ring_free = [sem(f"ring_free{i}") for i in range(N_SLOTS)]
    m.c_act, m.c_set, m.ada_bias = sem("c_act"), sem("c_set"), sem("ada_bias")
    m.params, m.release = sem("params"), sem("release")
    m.x_in, m.eps_set, m.heads_w, m.consts_in, m.zeroed = sem("x_in"), sem("eps_set"), sem("heads_w"), sem("consts_in"), sem("zeroed")
    m.stored = sem("stored")
    m.seen = sem("seen")
    second_sems(nc, m)
    m.n_consts = len(CONSTS)
    m.mods = nc.dram_tensor("mods", (DEPTH, 6 * D), F32, kind="Internal").ap()
    with nc.Block() as block:
        @block.sync
        def _(sp):
            for i in range(TILES):
                sp.dma_start(m.x[:, i, :], a["x"][0, i * P:(i + 1) * P, :]).then_inc(m.x_in, 16)
            sp.dma_start(m.cc[:], a["c_2"][0].rearrange("(p j) -> p j", j=KC)).then_inc(m.x_in, 16)
            sp.dma_start(m.ident[:], a["ident"]).then_inc(m.x_in, 16)
            for k, name in enumerate(("norm_mix", "norm_ffn")):
                sp.dma_start(m.gains[:, k, :, :], a[name].rearrange("l (p j) -> p l j", j=KC)).then_inc(m.x_in, 16)
            first_sync(nc, sp, m, a)
            second_sync(nc, sp, m, a, out)

        @block.gpsimd
        def _(pool):
            nc.gpsimd.memset(m.wqz, 0.0)
            nc.gpsimd.memset(m.wkz, 0.0)
            nc.gpsimd.memset(m.uT[:, :, 0:3], 0.0)
            pool.drain()
            pool.wait_ge(m.ring_full[1], 16)
            for name in CONSTS:
                dst = {"cos64": m.cos64, "sin64": m.sin64, "cos32": m.cos32, "sin32": m.sin32, "causal": m.causal,
                       "dil_mask": m.dil_mask, "dil_counts": m.dil_counts, "cmp_mask": m.cmp_mask[:], "cmp_seen": m.cmp_seen[:],
                       "head_rows": m.head_rows[:], "before": m.before[:], "ones": m.ones[:], "iota64": m.iota64[:]}[name]
                src = a[name]
                if name not in ("head_rows", "before", "ones", "iota64"):
                    src = src.rearrange("(i p) c -> p i c", p=P)
                pool.dma_start(dst, src).then_inc(m.consts_in, 16)
            first_pool(nc, pool, m, a)
            second_pool(nc, pool, m, a)

        @block.scalar
        def _(act):
            first_scalar(nc, act, m)
            second_scalar(nc, act, m)

        @block.tensor
        def _(pe):
            pe.wait_ge(m.x_in, 16 * 6)
            first_tensor(nc, pe, m)
            second_tensor(nc, pe, m)

        @block.vector
        def _(dve):
            first_vector(nc, dve, m)
            second_vector(nc, dve, m)


INPUTS = ["x", "norm_mix", "w_in", "nsa_cmp_pos", "nsa_cmp_w", "diff_lambda", "diff_norm", "mlstm_conv_w", "mlstm_conv_b",
          "mlstm_wq", "mlstm_wk", "mlstm_gate_b", "mlstm_norm", "w_out", "norm_ffn", "w_gate", "w_up", "w_down", "norm_final",
          "c_2", "ada_w_2", "ada_b_2", "a_w_in_2", "a_b_in_2", "a_w_dw_2", "a_b_dw_2", "a_ln_g_2", "a_ln_b_2", "a_w_out_2",
          "a_b_out_2", "b_w_in_2", "b_w_dw_2", "b_w_out_2", "mix_ln_g_2", "mix_ln_b_2", "ffn_ln_g_2", "ffn_ln_b_2",
          "r_w_group_2", "r_b_group_2", "r_w_expert_2", "r_b_expert_2", "e_w_gate_2", "e_w_up_2", "e_w_down_2"]


def kernel(**inputs):
    import numpy as np
    import concourse.bacc as bacc
    from concourse.bass_utils import run_bass_kernel_spmd

    nc = bacc.Bacc("TRN2", target_bir_lowering=False, num_devices=1)
    arrays = {}
    args = {}
    sources = {name: np.ascontiguousarray(inputs[name]) for name in INPUTS}
    sources.update(host_tables())
    for name, value in sources.items():
        arrays["in_" + name] = value
        args[name] = nc.dram_tensor("in_" + name, value.shape, mybir.dt.from_np(value.dtype), kind="ExternalInput").ap()
    out = nc.dram_tensor("out_0", (1, SEQ, D), F32, kind="ExternalOutput").ap()
    program(nc, args, out)
    r = run_bass_kernel_spmd(nc, [arrays], core_ids=[0])
    return r.results[0]["out_0"]
```
